# Optimizing a Trainium2 kernel written in Bass

```python
import jax, jax.numpy as jnp
from jax import lax
import numpy as np

D_MODEL = 1024
BATCH = 1
SEQ = 1024
DEPTH = 1

N_META = 16
GRID_W = 64
BRANCH_W = D_MODEL // 2
D_MIX = 3 * BRANCH_W
NORM_EPS = 1e-6
NA_HD = 64
NA_HEADS = BRANCH_W // NA_HD
WIN_R = 8
WIN_C = 16
GLA_HEADS = 4
GLA_DV = BRANCH_W // GLA_HEADS
GLA_DK = GLA_DV // 2
GLA_KW = GLA_HEADS * GLA_DK
GLA_LR = 16
GLA_NORMALIZER = 16.0
GLA_CHUNK = 64
GLA_NORM_EPS = 1e-5
RW_N = 64
RW_HEADS = BRANCH_W // RW_N
RW_W_LORA = 64
RW_A_LORA = 64
RW_V_LORA = 32
RW_GN_EPS = 64e-5
CONV_W = 3
NA_COLS = 4 * BRANCH_W
GLA_COLS = 2 * GLA_KW + 2 * BRANCH_W + 2 * GLA_LR
RW_SHIFT_COLS = 3 * BRANCH_W + 2 * RW_W_LORA + 2 * RW_A_LORA
RW_COLS = RW_SHIFT_COLS + BRANCH_W
P_IN = NA_COLS + GLA_COLS + RW_COLS


def rms_norm(x, g, eps=NORM_EPS):
    x32 = x.astype(jnp.float32)
    y = x32 * lax.rsqrt(jnp.mean(x32 * x32, axis=-1, keepdims=True) + eps)
    return (y * g.astype(jnp.float32)).astype(x.dtype)

def _split(z, widths):
    bounds = [int(b) for b in np.cumsum(widths)[:-1]]
    return jnp.split(z, bounds, axis=-1)

def _reorder_bwd(z):
    return jnp.concatenate([z[:, :N_META], jnp.flip(z[:, N_META:], axis=1)], axis=1)

def _to_dirs(z_fwd, z_bwd):
    return jnp.stack([z_fwd, _reorder_bwd(z_bwd)], axis=0)

def _sum_dirs(y):
    return y[0] + _reorder_bwd(y[1])

def centred_dwconv(z, w):
    c = z.shape[-1]
    return lax.conv_general_dilated(
        z, w[:, None, :].astype(z.dtype), window_strides=(1,),
        padding=[(CONV_W // 2, CONV_W // 2)],
        dimension_numbers=('NWC', 'WIO', 'NWC'), feature_group_count=c)

def neighbourhood_attention(q, k, v, rpb):
    B, L, H, hd = q.shape
    T = L - N_META
    rows = T // GRID_W
    wr = min(WIN_R, rows)
    scale = hd ** -0.5
    qm, km, vm = q[:, :N_META], k[:, :N_META], v[:, :N_META]
    to_grid = lambda a: a[:, N_META:].reshape(B, rows, GRID_W, H, hd).transpose(0, 3, 1, 2, 4)
    qg, kg, vg = to_grid(q), to_grid(k), to_grid(v)
    km_h, vm_h = km.transpose(0, 2, 1, 3), vm.transpose(0, 2, 1, 3)
    cols = np.arange(GRID_W)
    cstart = np.clip(cols - WIN_C // 2, 0, GRID_W - WIN_C)
    col_idx = cstart[:, None] + np.arange(WIN_C)[None, :]
    dc = col_idx - cols[:, None] + (WIN_C - 1)

    def row_block(r):
        rs = jnp.clip(r - wr // 2, 0, rows - wr)
        qr = lax.dynamic_index_in_dim(qg, r, axis=2, keepdims=False)
        kb = lax.dynamic_slice_in_dim(kg, rs, wr, axis=2)
        vb = lax.dynamic_slice_in_dim(vg, rs, wr, axis=2)
        kw = kb[:, :, :, col_idx]
        vw = vb[:, :, :, col_idx]
        s_loc = jnp.einsum('bhcd,bhrckd->bhcrk', qr, kw).astype(jnp.float32) * scale
        dr = rs + jnp.arange(wr) - r + (WIN_R - 1)
        bias = rpb[:, dr][:, :, dc]
        s_loc = s_loc + bias.transpose(0, 2, 1, 3)[None].astype(jnp.float32)
        s_meta = jnp.einsum('bhcd,bhmd->bhcm', qr, km_h).astype(jnp.float32) * scale
        s = jnp.concatenate([s_loc.reshape(B, H, GRID_W, wr * WIN_C), s_meta], axis=-1)
        p = jax.nn.softmax(s, axis=-1).astype(v.dtype)
        p_loc = p[..., :wr * WIN_C].reshape(B, H, GRID_W, wr, WIN_C)
        p_meta = p[..., wr * WIN_C:]
        return (jnp.einsum('bhcrk,bhrckd->bhcd', p_loc, vw)
                + jnp.einsum('bhcm,bhmd->bhcd', p_meta, vm_h))

    og = lax.map(row_block, jnp.arange(rows))
    og = og.transpose(1, 0, 3, 2, 4).reshape(B, T, H, hd)
    s_mm = jnp.einsum('bmhd,bnhd->bhmn', qm, km).astype(jnp.float32) * scale
    p_mm = jax.nn.softmax(s_mm, axis=-1).astype(v.dtype)
    om = jnp.einsum('bhmn,bnhd->bmhd', p_mm, vm)
    return jnp.concatenate([om, og], axis=1)

def na_branch(z, rpb):
    B, L, _ = z.shape
    q, k, v, g = _split(z, (BRANCH_W,) * 4)
    heads = lambda a: a.reshape(B, L, NA_HEADS, NA_HD)
    o = neighbourhood_attention(heads(q), heads(k), heads(v), rpb)
    return o.reshape(B, L, BRANCH_W) * jax.nn.silu(g)

def gla_chunked(q, k, v, g):
    Dn, B, L, H, dk = q.shape
    dv = v.shape[-1]
    C = GLA_CHUNK
    pad = (-N_META) % C
    padf = lambda a: jnp.pad(a, ((0, 0), (0, 0), (pad, 0), (0, 0), (0, 0)))
    nc = (L + pad) // C
    ch = lambda a: padf(a).reshape(Dn, B, nc, C, H, a.shape[-1]).transpose(0, 1, 4, 2, 3, 5)
    q, k, v, g = ch(q), ch(k), ch(v), ch(g)
    b = jnp.cumsum(g, axis=-2)
    qe = q * jnp.exp(b)
    ke = k * jnp.exp(-b)
    kd = k * jnp.exp(b[..., -1:, :] - b)
    mask = np.tril(np.ones((C, C), dtype=bool))
    A = jnp.where(mask, jnp.einsum('zbhnid,zbhnjd->zbhnij', qe, ke), 0.0)
    o = jnp.einsum('zbhnij,zbhnjv->zbhniv', A, v)
    dS = jnp.einsum('zbhnjd,zbhnjv->zbhndv', kd, v)
    dec = jnp.exp(b[..., -1, :])

    def step(S, inp):
        dS_n, dec_n = inp
        return dec_n[..., None] * S + dS_n, S

    S0 = jnp.zeros((Dn, B, H, dk, dv), jnp.float32)
    _, S_prev = lax.scan(step, S0, (jnp.moveaxis(dS, 3, 0), jnp.moveaxis(dec, 3, 0)))
    S_prev = jnp.moveaxis(S_prev, 0, 3)
    o = o + jnp.einsum('zbhnid,zbhndv->zbhniv', qe, S_prev)
    o = o.transpose(0, 1, 3, 4, 2, 5).reshape(Dn, B, nc * C, H, dv)
    return o[:, :, pad:]

def gla_branch(z, g_up, g_b, norm_g):
    B, L, _ = z.shape
    f32 = jnp.float32
    q, k, v, g, gd = _split(z.astype(f32), (GLA_KW, GLA_KW, BRANCH_W, BRANCH_W, 2 * GLA_LR))
    logits = jnp.einsum('bldr,drc->dblc', gd.reshape(B, L, 2, GLA_LR), g_up.astype(f32)) + g_b[:, None, None, :]
    gk = jax.nn.log_sigmoid(logits) / GLA_NORMALIZER
    hk = lambda a: a.reshape(a.shape[:-1] + (GLA_HEADS, -1))
    q = q * GLA_DK ** -0.5
    o = gla_chunked(hk(_to_dirs(q, q)), hk(_to_dirs(k, k)), hk(_to_dirs(v, v)),
                    hk(_to_dirs(gk[0], gk[1])))
    o = _sum_dirs(o)
    o = o * lax.rsqrt(jnp.mean(o * o, axis=-1, keepdims=True) + GLA_NORM_EPS) * norm_g
    return (o.reshape(B, L, BRANCH_W) * jax.nn.silu(g)).astype(z.dtype)

def rwkv7_scan(r, w, k, v, a, b):
    def step(S, inp):
        r_t, w_t, k_t, v_t, a_t, b_t = inp
        sa = jnp.einsum('zbhvk,zbhk->zbhv', S, a_t)
        S = (S * w_t[..., None, :] + sa[..., :, None] * b_t[..., None, :]
             + v_t[..., :, None] * k_t[..., None, :])
        return S, jnp.einsum('zbhvk,zbhk->zbhv', S, r_t)

    Dn, B, L, H, N = r.shape
    S0 = jnp.zeros((Dn, B, H, N, N), jnp.float32)
    xs = tuple(jnp.moveaxis(t, 2, 0) for t in (r, w, k, v, a, b))
    _, y = lax.scan(step, S0, xs)
    return jnp.moveaxis(y, 0, 2)

def rwkv7_branch(z, v_first, conv_w, w0, w_up, a0, a_up, k_k, k_a, r_k, ln_g, ln_b, v_mix):
    B, L, _ = z.shape
    f32 = jnp.float32
    zs = centred_dwconv(z[..., :RW_SHIFT_COLS], conv_w).astype(f32)
    gate = z[..., RW_SHIFT_COLS:].astype(f32)
    r, k, v, wd, ad = _split(zs, (BRANCH_W,) * 3 + (2 * RW_W_LORA, 2 * RW_A_LORA))
    w_lora = jnp.einsum('bldr,drc->dblc', jnp.tanh(wd.reshape(B, L, 2, RW_W_LORA)), w_up) + w0[:, None, None, :]
    decay = jnp.exp(-jnp.exp(-jax.nn.softplus(-w_lora) - 0.5))
    alpha = jax.nn.sigmoid(jnp.einsum('bldr,drc->dblc', ad.reshape(B, L, 2, RW_A_LORA), a_up) + a0[:, None, None, :])
    hd = lambda a: a.reshape(a.shape[:-1] + (RW_HEADS, RW_N))
    kk = hd(k * k_k)
    kk = kk / jnp.maximum(jnp.sqrt(jnp.sum(kk * kk, axis=-1, keepdims=True)), 1e-12)
    kk = kk.reshape(B, L, BRANCH_W)
    k_mod = k * (1.0 + (alpha - 1.0) * k_a)
    if v_mix is None:
        v_first = v
    else:
        v0, v_down, v_up = v_mix
        v = v + (v_first - v) * jax.nn.sigmoid(v0 + (v @ v_down) @ v_up)
    y = rwkv7_scan(hd(_to_dirs(r, r)), hd(_to_dirs(decay[0], decay[1])),
                   hd(_to_dirs(k_mod[0], k_mod[1])), hd(_to_dirs(v, v)),
                   hd(_to_dirs(-kk, -kk)), hd(_to_dirs(kk * alpha[0], kk * alpha[1])))
    y = _sum_dirs(y)
    mu = jnp.mean(y, axis=-1, keepdims=True)
    var = jnp.mean(jnp.square(y - mu), axis=-1, keepdims=True)
    y = ((y - mu) * lax.rsqrt(var + RW_GN_EPS)).reshape(B, L, BRANCH_W) * ln_g + ln_b
    k_bonus = 0.5 * (k_mod[0] + k_mod[1])
    bonus = jnp.sum(hd(r * k_bonus * r_k), axis=-1, keepdims=True) * hd(v)
    y = y + bonus.reshape(B, L, BRANCH_W)
    return (y * jax.nn.silu(gate)).astype(z.dtype), v_first

def first_inputs(seed: int = 0) -> dict:
    key = jax.random.key(seed)
    ks = jax.random.split(key, 24)
    nrm = lambda k, shape, s: jax.random.normal(k, shape, jnp.float32) * s
    dm1 = DEPTH - 1
    conv_base = jnp.array([0.25, 0.5, 0.25], jnp.float32)[None, :, None]
    return {
        'x': nrm(ks[0], (BATCH, SEQ, D_MODEL), 1.0),
        'meta': nrm(ks[1], (N_META, D_MODEL), 1.0),
        'norm_g': 1.0 + nrm(ks[2], (DEPTH, D_MODEL), 0.02),
        'w_in': nrm(ks[3], (DEPTH, D_MODEL, P_IN), D_MODEL ** -0.5),
        'w_out': nrm(ks[4], (DEPTH, D_MIX, D_MODEL), D_MIX ** -0.5),
        'na_rpb': nrm(ks[5], (DEPTH, NA_HEADS, 2 * WIN_R - 1, 2 * WIN_C - 1), 0.1),
        'gla_g_up': nrm(ks[6], (DEPTH, 2, GLA_LR, GLA_KW), GLA_LR ** -0.5),
        'gla_g_b': nrm(ks[7], (DEPTH, 2, GLA_KW), 0.1),
        'gla_norm_g': 1.0 + nrm(ks[8], (DEPTH, GLA_DV), 0.02),
        'rw_conv': conv_base + nrm(ks[9], (DEPTH, CONV_W, RW_SHIFT_COLS), 0.05),
        'rw_w0': jax.random.uniform(ks[10], (DEPTH, 2, BRANCH_W), jnp.float32, -4.0, 1.0),
        'rw_w_up': nrm(ks[11], (DEPTH, 2, RW_W_LORA, BRANCH_W), 0.5 * RW_W_LORA ** -0.5),
        'rw_a0': nrm(ks[12], (DEPTH, 2, BRANCH_W), 0.1),
        'rw_a_up': nrm(ks[13], (DEPTH, 2, RW_A_LORA, BRANCH_W), 0.5 * RW_A_LORA ** -0.5),
        'rw_k_k': 0.85 + nrm(ks[14], (DEPTH, BRANCH_W), 0.05),
        'rw_k_a': 1.0 + nrm(ks[15], (DEPTH, BRANCH_W), 0.05),
        'rw_r_k': nrm(ks[16], (DEPTH, BRANCH_W), 0.1),
        'rw_ln_g': 1.0 + nrm(ks[17], (DEPTH, BRANCH_W), 0.02),
        'rw_ln_b': nrm(ks[18], (DEPTH, BRANCH_W), 0.02),
        'rw_v0': 1.0 + nrm(ks[19], (dm1, BRANCH_W), 0.1),
        'rw_v_down': nrm(ks[20], (dm1, BRANCH_W, RW_V_LORA), BRANCH_W ** -0.5),
        'rw_v_up': nrm(ks[21], (dm1, RW_V_LORA, BRANCH_W), 0.5 * RW_V_LORA ** -0.5),
        'final_norm_g': 1.0 + nrm(ks[22], (D_MODEL,), 0.02),
    }

def first_block(x, meta, norm_g, w_in, w_out, na_rpb, gla_g_up, gla_g_b, gla_norm_g,
              rw_conv, rw_w0, rw_w_up, rw_a0, rw_a_up, rw_k_k, rw_k_a, rw_r_k,
              rw_ln_g, rw_ln_b, rw_v0, rw_v_down, rw_v_up, final_norm_g):
    B, _, D = x.shape
    h = jnp.concatenate([jnp.broadcast_to(meta[None].astype(x.dtype), (B, N_META, D)), x], axis=1)
    v_first = None
    for l in range(DEPTH):
        hn = rms_norm(h, norm_g[l])
        w = w_in[l]
        z_na = hn @ w[:, :NA_COLS]
        z_gla = hn @ w[:, NA_COLS:NA_COLS + GLA_COLS]
        z_rw = hn @ w[:, NA_COLS + GLA_COLS:]
        o_na = na_branch(z_na, na_rpb[l])
        o_gla = gla_branch(z_gla, gla_g_up[l], gla_g_b[l], gla_norm_g[l])
        v_mix = None if l == 0 else (rw_v0[l - 1], rw_v_down[l - 1], rw_v_up[l - 1])
        o_rw, v_first = rwkv7_branch(z_rw, v_first, rw_conv[l], rw_w0[l], rw_w_up[l], rw_a0[l],
                                     rw_a_up[l], rw_k_k[l], rw_k_a[l], rw_r_k[l],
                                     rw_ln_g[l], rw_ln_b[l], v_mix)
        h = h + jnp.concatenate([o_na, o_gla, o_rw], axis=-1) @ w_out[l]
    return rms_norm(h, final_norm_g)[:, N_META:]


_first_inputs = first_inputs


def first_inputs(seed=0):
    import zlib

    import numpy as np

    out = dict(_first_inputs(seed))
    spreads = {}
    factors = {'norm_g': 3.024,
     'na_rpb': 8.0,
     'gla_g_b': 4.367,
     'gla_norm_g': 8.0,
     'rw_w_up': 4.293,
     'rw_a0': 4.333,
     'rw_k_k': 5.96,
     'rw_k_a': 2.851,
     'rw_ln_g': 8.0,
     'rw_ln_b': 8.0,
     'final_norm_g': 2.82}
    for name, (base, spread) in spreads.items():
        noise = np.random.default_rng([zlib.crc32(name.encode()), seed]).standard_normal(out[name].shape)
        drawn = base * np.exp(spread * noise) if base else spread * noise
        out[name] = __import__('jax').numpy.asarray(drawn.astype(out[name].dtype))
    for name, factor in factors.items():
        out[name] = (out[name] * factor).astype(out[name].dtype)
    return out


_narrow_inputs = first_inputs


def first_inputs(seed=0):

    out = dict(_narrow_inputs(seed))
    wider = {'gla_norm_g': 4.65, 'rw_k_k': 5.27, 'rw_ln_g': 5.04, 'rw_ln_b': 5.03, 'final_norm_g': 3.18}
    for name, times in wider.items():
        mean = out[name].mean()
        out[name] = (mean + times * (out[name] - mean)).astype(out[name].dtype)
    return out


DEPTH_2 = 2

N_MIXERS = 2
HEAD_DIM = 64
N_Q_HEADS = D_MODEL // HEAD_DIM
N_KV_HEADS = N_Q_HEADS // 4
GQA_GROUP = N_Q_HEADS // N_KV_HEADS
WINDOW = 128
BLOCK = 128
ROT_DIM = HEAD_DIM // 4
ROPE_THETA = 500000.0
LRU_WIDTH = D_MODEL
LRU_BLOCKS = 4
LRU_BLOCK_W = LRU_WIDTH // LRU_BLOCKS
CONV_WIDTH = 4
CONV_LEFT = 2
LRU_C = 8.0
N_EXPERTS = 16
EXPERT_FF = D_MODEL
CAPACITY_FACTOR = 2
LN_EPS = 1e-5
ALPHA = (2 * DEPTH_2) ** 0.25
BETA = (8 * DEPTH_2) ** -0.25
N_ATTN_LAYERS = (DEPTH_2 + 1) // 2
N_LRU_LAYERS = DEPTH_2 // 2


def layer_norm(x, g, b):
    xf = x.astype(jnp.float32)
    mu = jnp.mean(xf, axis=-1, keepdims=True)
    var = jnp.mean(jnp.square(xf - mu), axis=-1, keepdims=True)
    y = (xf - mu) * lax.rsqrt(var + LN_EPS) * g.astype(jnp.float32) + b.astype(jnp.float32)
    return y.astype(x.dtype)

def partial_rotary(t, cos, sin):
    tr, tp = t[..., :ROT_DIM], t[..., ROT_DIM:]
    t1, t2 = tr[..., :ROT_DIM // 2], tr[..., ROT_DIM // 2:]
    rot = jnp.concatenate([-t2, t1], axis=-1)
    return jnp.concatenate([tr * cos + rot * sin, tp], axis=-1)

def windowed_gqa_sink(x, w_qkv, w_o, sink):
    B, S, _ = x.shape
    nb = S // BLOCK
    qkv = x @ w_qkv
    q, k, v = jnp.split(qkv, [N_Q_HEADS * HEAD_DIM, (N_Q_HEADS + N_KV_HEADS) * HEAD_DIM], axis=-1)
    q = q.reshape(B, S, N_KV_HEADS, GQA_GROUP, HEAD_DIM)
    k = k.reshape(B, S, N_KV_HEADS, HEAD_DIM)
    v = v.reshape(B, S, N_KV_HEADS, HEAD_DIM)
    pos = jnp.arange(S, dtype=jnp.float32)
    inv_freq = ROPE_THETA ** (-jnp.arange(0, ROT_DIM, 2, dtype=jnp.float32) / ROT_DIM)
    ang = pos[:, None] * inv_freq[None, :]
    ang = jnp.concatenate([ang, ang], axis=-1)
    cos, sin = jnp.cos(ang).astype(x.dtype), jnp.sin(ang).astype(x.dtype)
    q = partial_rotary(q, cos[None, :, None, None, :], sin[None, :, None, None, :])
    k = partial_rotary(k, cos[None, :, None, :], sin[None, :, None, :])

    pad = ((0, 0), (BLOCK, BLOCK), (0, 0), (0, 0))
    kb = jnp.pad(k, pad).reshape(B, nb + 2, BLOCK, N_KV_HEADS, HEAD_DIM)
    vb = jnp.pad(v, pad).reshape(B, nb + 2, BLOCK, N_KV_HEADS, HEAD_DIM)
    k_band = jnp.concatenate([kb[:, :-2], kb[:, 1:-1], kb[:, 2:]], axis=2)
    v_band = jnp.concatenate([vb[:, :-2], vb[:, 1:-1], vb[:, 2:]], axis=2)
    qb = q.reshape(B, nb, BLOCK, N_KV_HEADS, GQA_GROUP, HEAD_DIM)

    s = jnp.einsum('bnqhgd,bnkhd->bnhgqk', qb, k_band).astype(jnp.float32) * (HEAD_DIM ** -0.5)
    blk = jnp.arange(nb)
    qpos = blk[:, None] * BLOCK + jnp.arange(BLOCK)[None, :]
    kpos = (blk[:, None] - 1) * BLOCK + jnp.arange(3 * BLOCK)[None, :]
    valid = ((jnp.abs(qpos[:, :, None] - kpos[:, None, :]) <= WINDOW)
             & (kpos[:, None, :] >= 0) & (kpos[:, None, :] < S))
    s = jnp.where(valid[None, :, None, None], s, -jnp.inf)
    sink_l = sink.astype(jnp.float32).reshape(N_KV_HEADS, GQA_GROUP)[None, None, :, :, None, None]
    m = jnp.maximum(jnp.max(s, axis=-1, keepdims=True), sink_l)
    p = jnp.exp(s - m)
    denom = jnp.sum(p, axis=-1, keepdims=True) + jnp.exp(sink_l - m)
    probs = (p / denom).astype(x.dtype)
    o = jnp.einsum('bnhgqk,bnkhd->bnqhgd', probs, v_band).reshape(B, S, D_MODEL)
    return o @ w_o

def _linear_combine(left, right):
    a1, b1 = left
    a2, b2 = right
    return a1 * a2, a2 * b1 + b2

def bidir_rglru_block(x, w_in, conv_w, conv_b, w_rgate, b_rgate, w_igate, b_igate, lam, w_out):
    B, S, _ = x.shape
    gate_br, xb = jnp.split(x @ w_in, 2, axis=-1)
    xp = jnp.pad(xb, ((0, 0), (CONV_LEFT, CONV_WIDTH - 1 - CONV_LEFT), (0, 0)))
    xc = conv_b
    for j in range(CONV_WIDTH):
        xc = xc + conv_w[j] * xp[:, j:j + S]
    xr = xc.reshape(B, S, LRU_BLOCKS, LRU_BLOCK_W)
    r = jax.nn.sigmoid(jnp.einsum('bsnc,zncf->zbsnf', xr, w_rgate).reshape(2, B, S, LRU_WIDTH).astype(jnp.float32)
                       + b_rgate.astype(jnp.float32)[:, None, None, :])
    i = jax.nn.sigmoid(jnp.einsum('bsnc,zncf->zbsnf', xr, w_igate).reshape(2, B, S, LRU_WIDTH).astype(jnp.float32)
                       + b_igate.astype(jnp.float32)[:, None, None, :])
    log_a = -LRU_C * r * jax.nn.softplus(-lam.astype(jnp.float32))[:, None, None, :]
    a = jnp.exp(log_a)
    mult = jnp.sqrt(-jnp.expm1(2.0 * log_a))
    t = jnp.arange(S)
    is_start = jnp.stack([t == 0, t == S - 1])
    mult = jnp.where(is_start[:, None, :, None], 1.0, mult)
    u = mult * i * xc.astype(jnp.float32)[None]
    _, h_f = lax.associative_scan(_linear_combine, (a[0], u[0]), axis=1)
    _, h_b = lax.associative_scan(_linear_combine, (a[1], u[1]), reverse=True, axis=1)
    h = (h_f + h_b).astype(x.dtype)
    return (h * jax.nn.gelu(gate_br)) @ w_out

def expert_choice_moe(x, w_router, w_gate_up, w_down):
    B, S, _ = x.shape
    cap = CAPACITY_FACTOR * S // N_EXPERTS
    aff = jax.nn.softmax((x @ w_router).astype(jnp.float32), axis=-1)
    gates, idx = lax.top_k(jnp.swapaxes(aff, 1, 2), cap)
    bi = jnp.arange(B)[:, None, None]
    xs = x[bi, idx]
    g, u = jnp.split(jnp.einsum('becd,edf->becf', xs, w_gate_up), 2, axis=-1)
    out = jnp.einsum('becf,efd->becd', jax.nn.silu(g) * u, w_down) * gates[..., None].astype(x.dtype)
    return jnp.zeros_like(x).at[bi, idx].add(out)

def second_inputs(seed: int = 0) -> dict:
    key = jax.random.key(seed)
    ks = jax.random.split(key, 24)
    f32 = jnp.float32
    nrm = lambda k, shape, scale: jax.random.normal(k, shape, f32) * scale
    qkv_out = (N_Q_HEADS + 2 * N_KV_HEADS) * HEAD_DIM
    a8 = jax.random.uniform(ks[11], (N_LRU_LAYERS, 2, LRU_WIDTH), f32, 0.9, 0.999)
    a_base = a8 ** (1.0 / LRU_C)
    lam = jnp.log(a_base) - jnp.log1p(-a_base)
    return {
        'x': jax.random.normal(ks[0], (BATCH, SEQ, D_MODEL), f32),
        'attn_w_qkv': nrm(ks[1], (N_ATTN_LAYERS, D_MODEL, qkv_out), D_MODEL ** -0.5),
        'attn_w_o': nrm(ks[2], (N_ATTN_LAYERS, D_MODEL, D_MODEL), BETA * D_MODEL ** -0.5),
        'attn_sink': nrm(ks[3], (N_ATTN_LAYERS, N_Q_HEADS), 0.5),
        'lru_w_in': nrm(ks[4], (N_LRU_LAYERS, D_MODEL, 2 * LRU_WIDTH), D_MODEL ** -0.5),
        'lru_conv_w': nrm(ks[5], (N_LRU_LAYERS, CONV_WIDTH, LRU_WIDTH), CONV_WIDTH ** -0.5),
        'lru_conv_b': nrm(ks[6], (N_LRU_LAYERS, LRU_WIDTH), 0.02),
        'lru_w_rgate': nrm(ks[7], (N_LRU_LAYERS, 2, LRU_BLOCKS, LRU_BLOCK_W, LRU_BLOCK_W), LRU_BLOCK_W ** -0.5),
        'lru_b_rgate': nrm(ks[8], (N_LRU_LAYERS, 2, LRU_WIDTH), 0.02),
        'lru_w_igate': nrm(ks[9], (N_LRU_LAYERS, 2, LRU_BLOCKS, LRU_BLOCK_W, LRU_BLOCK_W), LRU_BLOCK_W ** -0.5),
        'lru_b_igate': nrm(ks[10], (N_LRU_LAYERS, 2, LRU_WIDTH), 0.02),
        'lru_lambda': lam,
        'lru_w_out': nrm(ks[12], (N_LRU_LAYERS, LRU_WIDTH, D_MODEL), BETA * LRU_WIDTH ** -0.5),
        'moe_w_router': nrm(ks[13], (DEPTH_2, D_MODEL, N_EXPERTS), D_MODEL ** -0.5),
        'moe_w_gate_up': nrm(ks[14], (DEPTH_2, N_EXPERTS, D_MODEL, 2 * EXPERT_FF), D_MODEL ** -0.5),
        'moe_w_down': nrm(ks[15], (DEPTH_2, N_EXPERTS, EXPERT_FF, D_MODEL), BETA * EXPERT_FF ** -0.5),
        'ln_mix_g': 1.0 + nrm(ks[16], (DEPTH_2, D_MODEL), 0.02),
        'ln_mix_b': nrm(ks[17], (DEPTH_2, D_MODEL), 0.02),
        'ln_ffn_g': 1.0 + nrm(ks[18], (DEPTH_2, D_MODEL), 0.02),
        'ln_ffn_b': nrm(ks[19], (DEPTH_2, D_MODEL), 0.02),
    }

def second_block(x, attn_w_qkv, attn_w_o, attn_sink, lru_w_in, lru_conv_w, lru_conv_b,
              lru_w_rgate, lru_b_rgate, lru_w_igate, lru_b_igate, lru_lambda, lru_w_out,
              moe_w_router, moe_w_gate_up, moe_w_down, ln_mix_g, ln_mix_b, ln_ffn_g, ln_ffn_b):
    for layer in range(DEPTH_2):
        j = layer // N_MIXERS
        if layer % N_MIXERS == 0:
            mix = windowed_gqa_sink(x, attn_w_qkv[j], attn_w_o[j], attn_sink[j])
        else:
            mix = bidir_rglru_block(x, lru_w_in[j], lru_conv_w[j], lru_conv_b[j],
                                    lru_w_rgate[j], lru_b_rgate[j], lru_w_igate[j], lru_b_igate[j],
                                    lru_lambda[j], lru_w_out[j])
        x = layer_norm(ALPHA * x + mix, ln_mix_g[layer], ln_mix_b[layer])
        ffn = expert_choice_moe(x, moe_w_router[layer], moe_w_gate_up[layer], moe_w_down[layer])
        x = layer_norm(ALPHA * x + ffn, ln_ffn_g[layer], ln_ffn_b[layer])
    return x


def setup_inputs(seed=0):
    out = dict(first_inputs(seed))
    for name, value in second_inputs(seed + 1).items():
        if name != "x":
            out[name + "_2"] = value
    return out


def reference(
    x, meta, norm_g, w_in, w_out, na_rpb, gla_g_up, gla_g_b, gla_norm_g, rw_conv, rw_w0,
    rw_w_up, rw_a0, rw_a_up, rw_k_k, rw_k_a, rw_r_k, rw_ln_g, rw_ln_b, rw_v0, rw_v_down,
    rw_v_up, final_norm_g, attn_w_qkv_2, attn_w_o_2, attn_sink_2, lru_w_in_2, lru_conv_w_2,
    lru_conv_b_2, lru_w_rgate_2, lru_b_rgate_2, lru_w_igate_2, lru_b_igate_2, lru_lambda_2,
    lru_w_out_2, moe_w_router_2, moe_w_gate_up_2, moe_w_down_2, ln_mix_g_2, ln_mix_b_2,
    ln_ffn_g_2, ln_ffn_b_2,
):
    x = first_block(
        x, meta, norm_g, w_in, w_out, na_rpb, gla_g_up, gla_g_b, gla_norm_g, rw_conv, rw_w0,
        rw_w_up, rw_a0, rw_a_up, rw_k_k, rw_k_a, rw_r_k, rw_ln_g, rw_ln_b, rw_v0, rw_v_down,
        rw_v_up, final_norm_g,
    )
    return second_block(
        x, attn_w_qkv_2, attn_w_o_2, attn_sink_2, lru_w_in_2, lru_conv_w_2, lru_conv_b_2,
        lru_w_rgate_2, lru_b_rgate_2, lru_w_igate_2, lru_b_igate_2, lru_lambda_2, lru_w_out_2,
        moe_w_router_2, moe_w_gate_up_2, moe_w_down_2, ln_mix_g_2, ln_mix_b_2, ln_ffn_g_2,
        ln_ffn_b_2,
    )


_drawn_inputs = setup_inputs


def setup_inputs(seed=0):
    import zlib

    import numpy as np

    out = dict(_drawn_inputs(seed))
    spreads = {}
    factors = {'attn_sink_2': 64.0, 'lru_b_rgate_2': 55.421, 'lru_b_igate_2': 33.595}
    for name, (base, spread) in spreads.items():
        noise = np.random.default_rng([zlib.crc32(name.encode()), seed]).standard_normal(out[name].shape)
        drawn = base * np.exp(spread * noise) if base else spread * noise
        out[name] = __import__('jax').numpy.asarray(drawn.astype(out[name].dtype))
    for name, factor in factors.items():
        out[name] = (out[name] * factor).astype(out[name].dtype)
    return out
```

```python
from contextlib import ExitStack, contextmanager

import numpy as np

import concourse.bass as bass
from concourse import mybir

F32 = mybir.dt.float32
I32 = mybir.dt.int32
ALU = mybir.AluOpType
ACT = mybir.ActivationFunctionType
AX = mybir.AxisListType
P = 128


class Count:

    def __init__(self, core, name):
        self.sem = core.ctx.enter_context(core.nc.semaphore(name))
        self.n, self.core = 0, core
        core.counts.append(self)

    def mark(self):
        return self, self.n, self.core.epoch


class Line(Count):

    def __init__(self, core, name, eng, chained):
        super().__init__(core, name)
        self.eng, self.chained, self.seen = eng, chained, {}

    def after(self, *marks):
        for m in marks:
            if m is None:
                continue
            c, n, epoch = m.mark() if isinstance(m, Count) else m
            if epoch == self.core.epoch and n > self.seen.get(c, 0):
                self.eng.wait_ge(c.sem, n)
                self.seen[c] = n

    def start(self, marks):
        self.after(*marks)
        if self.chained:
            self.after(self)

    def done(self, ins):
        ins.then_inc(self.sem, 1)
        self.n += 1
        return self.mark()


class Elementwise(Line):

    def tt(self, out, a, b, op, after=()):
        self.start(after)
        return self.done(self.eng.tensor_tensor(out, a, b, op))

    def ts(self, out, a, s1, op0, s2=None, op1=None, after=()):
        self.start(after)
        if op1 is None:
            return self.done(self.eng.tensor_scalar(out, a, s1, None, op0))
        return self.done(self.eng.tensor_scalar(out, a, s1, s2, op0, op1))

    def stt(self, out, a, s, b, op0, op1, after=()):
        self.start(after)
        return self.done(self.eng.scalar_tensor_tensor(out, a, s, b, op0, op1))

    def copy(self, out, a, after=()):
        self.start(after)
        return self.done(self.eng.tensor_copy(out, a))

    def fill(self, out, value, after=()):
        self.start(after)
        return self.done(self.eng.memset(out, value))

    def recip(self, out, a, after=()):
        self.start(after)
        return self.done(self.eng.reciprocal(out, a))

    def reduce(self, out, a, op, after=()):
        self.start(after)
        return self.done(self.eng.tensor_reduce(out, a, AX.X, op))

    def scan(self, out, keep, add, after=()):
        self.start(after)
        return self.done(self.eng.tensor_tensor_scan(out, keep, add, 0.0, ALU.mult, ALU.add))


class Activations(Line):
    def act(self, out, a, func, bias=0.0, scale=1.0, accum=None, after=()):
        self.start(after)
        return self.done(self.eng.activation(out, a, func, bias=bias, scale=scale, accum_out=accum))

    def copy(self, out, a, after=()):
        return self.act(out, a, ACT.Copy, after=after)


class Products(Line):
    def mm(self, out, lhsT, rhs, start=True, stop=True, after=()):
        self.start(after)
        return self.done(self.eng.matmul(out, lhsT, rhs, start=start, stop=stop))

    def turn(self, out, a, ident, after=()):
        self.start(after)
        return self.done(self.eng.transpose(out, a, ident))


class Core:

    def __init__(self, nc, ctx):
        self.nc, self.ctx, self.counts, self.epoch = nc, ctx, [], 0
        self.V = Elementwise(self, "vector_done", nc.vector, True)
        self.G = Elementwise(self, "gpsimd_done", nc.gpsimd, True)
        self.A = Activations(self, "scalar_done", nc.scalar, True)
        self.T = Products(self, "tensor_done", nc.tensor, False)
        self.S = Line(self, "sync_done", nc.sync, False)
        self.lines = [self.V, self.G, self.A, self.T, self.S]
        self.loads, self.phases = {}, 0

    def dma(self, name, out, in_, after=(), line=None):
        line = line or self.S
        if name not in self.loads:
            self.loads[name] = Count(self, name)
        c = self.loads[name]
        line.after(*after)
        line.eng.dma_start(out, in_).then_inc(c.sem, 16)
        c.n += 16
        return c.mark()

    def barrier(self):
        self.S.after(*self.loads.values())
        self.nc.all_engine_barrier()
        used = [c for c in self.counts if c.n]
        for c in used:
            self.nc.sync.sem_clear(c.sem)
        self.nc.all_engine_barrier()
        self.epoch += 1
        for c in self.counts:
            c.n = 0
        for line in self.lines:
            line.seen = {}

    @contextmanager
    def loop(self, n):
        self.barrier()
        with self.nc.Fori(0, n) as i:
            yield i
            self.barrier()


def one(ap, i, dim=0):
    return ap[i] if dim == 0 else ap[:, i]


D = 1024
KD = D // P
SEQ = 1024
META = 16
CH = 64
X0 = CH
M0 = X0 - META
COLS = X0 + SEQ
NC = SEQ // CH
SPANS = [(M0, META), (X0, 512), (X0 + 512, 512)]
BW = 512
NA_COLS, GLA_COLS = 4 * BW, 3 * BW + 32
RW0 = NA_COLS + GLA_COLS
HALF = (slice(0, 64), slice(64, 128))
WIN_R, WIN_C = 8, 16
RPB_R, RPB_C = 2 * WIN_R - 1, 2 * WIN_C - 1
RPB_PAD = CH
NEG = -1e30
RB = 4


def sigmoid_of(k, out, x, bias=0.0, after=()):
    e = k.A.act(out, x, ACT.Exp, bias=bias, scale=-1.0, after=after)
    k.V.ts(out, out, 1.0, ALU.add, after=[e])
    return k.V.recip(out, out)


def constants(k, sb):
    G = k.G
    c = {}

    def mask(name, cols, conds):
        m = c[name] = sb(name, [P, cols], F32)
        G.fill(m[:, :], 1.0)
        for base, col, part in conds:
            G.start(())
            G.done(G.eng.affine_select(out=m[:, :], in_=m[:, :], compare_op=ALU.is_ge, fill=0.0, base=base,
                                       pattern=[[col, cols]], channel_multiplier=part))

    mask("ident", P, [(0, 1, -1), (0, -1, 1)])
    mask("ones", P, [])
    mask("before", P, [(-1, 1, -1)])
    mask("after", P, [(-1, -1, 1)])
    mask("upto", P, [(0, 1, -1)])
    mask("from", P, [(0, -1, 1)])
    for name, sign in (("upto64", 1), ("from64", -1)):
        m = c[name] = sb(name, [P, CH], F32)
        G.fill(m[:, :], 1.0)
        for h in HALF:
            G.start(())
            G.done(G.eng.affine_select(out=m[h, :], in_=m[h, :], compare_op=ALU.is_ge, fill=0.0, base=0,
                                       pattern=[[sign, CH]], channel_multiplier=-sign))
    m = c["halves"] = sb("halves", [P, P], F32)
    G.fill(m[:, :], 0.0)
    for h in HALF:
        G.fill(m[h, h], 1.0)
    return c


def rms_scale(k, st, x, rows, eps, dump, after=()):
    a = k.A.act(dump, x, ACT.Square, accum=st[0:rows, 0:1], after=after)
    k.V.ts(st[0:rows, 0:1], st[0:rows, 0:1], 1.0 / D, ALU.mult, eps, ALU.add, after=[a])
    a = k.A.act(st[0:rows, 0:1], st[0:rows, 0:1], ACT.Sqrt, after=[k.V])
    return k.V.recip(st[0:rows, 1:2], st[0:rows, 0:1], after=[a])


def block_one_norm(k, c, ps, io, hnT, sb):
    xt = sb("x_tile", [P, D], F32)
    dump = sb("squares", [P, D], F32)
    st = sb("norm_stats", [P, 2], F32)
    gcol = sb("norm_g_cols", [P, KD], F32)
    m = k.dma("norm_g_in", gcol[:, :], io["norm_g_cols"])
    k.G.fill(hnT[:, :, 0:M0], 0.0)

    def tile(src, rows, col):
        load = k.dma("x_in", xt[0:rows, :], src)
        r = rms_scale(k, st, xt[0:rows, :], rows, 1e-6, dump[0:rows, :], after=[load])
        k.V.ts(xt[0:rows, :], xt[0:rows, :], st[0:rows, 1:2], ALU.mult)
        k.T.after(k.V, k.G)
        for b in range(KD):
            t = k.T.turn(ps[b // 4][:, (b % 4) * P:(b % 4) * P + rows], xt[0:rows, b * P:(b + 1) * P],
                         c["ident"][0:rows, 0:rows])
        for half in range(2):
            src_ps = ps[half][:, 0:512].rearrange("p (b t) -> p b t", b=4)[:, :, 0:rows]
            g = gcol[:, 4 * half:4 * half + 4].unsqueeze(2).broadcast_to([P, 4, rows])
            k.V.tt(hnT[:, 4 * half:4 * half + 4, col], src_ps, g, ALU.mult, after=[t, m])

    tile(io["meta"], META, slice(M0, X0))
    with k.loop(SEQ // P) as i:
        tile(io["x"][0, bass.ds(i * P, P), :], P, bass.ds(i * P + X0, P))


class Projector:

    def __init__(self, k, ps, w_in, hnT, sb, ring):
        self.k, self.ps, self.hnT, self.ring, self.n = k, ps, hnT, ring, 0
        self.w = w_in[0].rearrange("(k p) c -> p k c", p=P)
        self.bufs = [sb(f"w_block{i}", [P, KD, P], F32) for i in range(ring)]
        self.used = [None] * ring
        self.evac = [None, None]
        self.side = 1
        self.loads = []

    def reset(self):
        self.used, self.evac, self.n, self.loads = [None] * self.ring, [None, None], 0, []

    def load(self, cols, width=P):
        b = self.n % self.ring
        self.n += 1
        mark = self.k.dma(f"w_in{b}", self.bufs[b][:, :, 0:width], self.w[:, :, cols], after=[self.used[b]])
        self.loads.append((b, mark, width))

    def part(self, half, cols):
        b = self.n % self.ring
        self.mark = self.k.dma(f"w_in{b}", self.bufs[b][:, :, half], self.w[:, :, cols], after=[self.used[b]])

    def whole(self):
        self.loads.append((self.n % self.ring, self.mark, P))
        self.n += 1

    def block(self, take, spans=SPANS):
        k = self.k
        b, mark, width = self.loads.pop(0)
        s = self.side = 1 - self.side
        k.T.after(mark, *(self.evac[s] or ()))
        marks = []
        for j, (col, n) in enumerate(spans):
            out = self.ps[3 * s + j][0:width, 0:n]
            for d in range(KD):
                m = k.T.mm(out, self.bufs[b][:, d, 0:width], self.hnT[:, d, col:col + n], start=d == 0, stop=d == KD - 1)
            marks.append(m)
        self.used[b] = m
        got = []
        for j, (col, n) in enumerate(spans):
            got += take(j, col, n, self.ps[3 * s + j][0:width, 0:n], marks[j])
        self.evac[s] = got


def silu_block(k, pr, out, tmp, off=X0):
    def take(j, col, n, z, m):
        s = slice(col - off, col - off + n)
        sigmoid_of(k, tmp[:, s], z, after=[m, k.V])
        return [k.V.tt(out[:, s], z, tmp[:, s], ALU.mult)]
    pr.block(take, SPANS[1:])


def copy_block(k, pr, out):
    def take(j, col, n, z, m):
        return [k.A.copy(out[0:z.shape[0], col:col + n], z, after=[m])]
    pr.block(take)


def attention_branch(k, c, ps, io, hnT, mix, sb):
    V, A, T, G = k.V, k.A, k.T, k.G
    NP = BW // P
    pr = Projector(k, ps, io["w_in"], hnT, sb, 4)
    qT = sb("na_q", [P, COLS], F32)
    kT = sb("na_k", [P, COLS], F32)
    vT = sb("na_v", [P, COLS], F32)
    gate = sb("na_gate", [P, SEQ], F32)
    vt = sb("na_v_tiles", [P, NC, P], F32)
    vm = sb("na_v_meta", [META, P], F32)
    bias = sb("na_bias", [P, BW // P * RPB_R, CH], F32)
    away = sb("na_outside", [P, CH], F32)
    qbd = sb("na_q_pair", [P, P], F32)
    s_sb = sb("na_scores", [P, 512 + META], F32)
    pT = sb("na_probs_T", [P, 5, P], F32)
    o_sb = sb("na_o", [P, P], F32)
    oT = sb("na_oT", [P, SEQ], F32)
    st = sb("na_stats", [P, 4], F32)
    G.fill(qbd[:, :], 0.0)
    for h in HALF:
        G.fill(away[h, :], 0.0)
        for base, col, q in ((WIN_C // 2, 1, -1), (WIN_C // 2 - 1, -1, 1)):
            G.start(())
            G.done(G.eng.affine_select(out=away[h, :], in_=away[h, :], compare_op=ALU.is_ge, fill=NEG,
                                       base=base + (CH - 1) * q, pattern=[[col, CH]], channel_multiplier=-q))
    edge = sb("na_edge", [P, 2, CH], F32)
    for h in HALF:
        for e, (base, q) in enumerate(((WIN_C // 2 - 1, -1), (-(CH - WIN_C // 2), 1))):
            G.fill(edge[h, e, :], 1.0)
            G.start(())
            G.done(G.eng.affine_select(out=edge[h, e, :], in_=edge[h, e, :], compare_op=ALU.is_ge, fill=0.0,
                                       base=base + (CH - 1) * q, pattern=[[0, CH]], channel_multiplier=-q))
            G.start(())
            G.done(G.eng.affine_select(out=edge[h, e, :], in_=edge[h, e, :], compare_op=ALU.is_ge, fill=0.0,
                                       base=(WIN_C - 1) if e == 0 else -(CH - WIN_C),
                                       pattern=[[-1 if e == 0 else 1, CH]], channel_multiplier=0))
    G.tt(edge[:, 0, :], edge[:, 0, :], edge[:, 1, :], ALU.add)
    G.ts(edge[:, 0, :], edge[:, 0, :], -1.0, ALU.mult, 1.0, ALU.add)
    G.tt(away[:, :], away[:, :], edge[:, 0, :], ALU.mult)

    rpb = bass.AP(io["rpb_padded"].tensor, RPB_PAD + WIN_C - 1 - (CH - 1),
                  [[RPB_R * RPB_C, BW // 64], [1, CH], [RPB_C, RPB_R], [1, CH]])
    for h in range(2):
        for p in range(NP):
            m = k.dma("na_bias_in", bias[HALF[h], p * RPB_R:(p + 1) * RPB_R, :], rpb[2 * p + h])
    G.tt(bias[:, :, :], bias[:, :, :], away[:, :].unsqueeze(1).broadcast_to([P, NP * RPB_R, CH]), ALU.add, after=[m])
    with k.loop(NP) as p:
        pr.reset()
        for j in range(4):
            pr.load(bass.ds(p * P + j * BW, P))
        copy_block(k, pr, qT)
        copy_block(k, pr, kT)
        copy_block(k, pr, vT)
        silu_block(k, pr, gate, oT)
        T.after(A)
        for g in range(0, NC, 4):
            bank = ps[6 + (g // 4) % 2]
            T.after(A)
            for j in range(g, min(g + 4, NC - 1)):
                t = T.turn(bank[:, (j - g) * P:(j - g + 1) * P], vT[:, X0 + CH * j:X0 + CH * j + P], c["ident"][:, :])
            n = min(4, NC - 1 - g)
            A.copy(vt[:, g:g + n, :], bank[:, 0:n * P].rearrange("p (j f) -> p j f", f=P), after=[t])
        t = T.turn(ps[6][0:META, 0:P], vT[:, M0:X0], c["ident"][:, :], after=[A])
        A.copy(vm[:, :], ps[6][0:META, 0:P], after=[t])

        def grid_row(r, first, dr0):
            qs = bass.ds(r * CH + X0, CH)
            for h in HALF:
                A.copy(qbd[h, h][:, ::-1], qT[h, qs])
            T.mm(ps[0][:, :], qbd[:, :], kT[:, bass.ds(first * CH + X0, 512)], after=[A])
            t = T.mm(ps[1][:, 0:META], qbd[:, :], kT[:, M0:X0])
            scale = CH ** -0.5
            V.stt(s_sb[:, 0:512].rearrange("p (r c) -> p r c", c=CH), ps[0][:, :].rearrange("p (r c) -> p r c", c=CH),
                  scale, bias[:, bass.ds(p * RPB_R + dr0, WIN_R), :], ALU.mult, ALU.add, after=[t, G])
            V.ts(s_sb[:, 512:], ps[1][:, 0:META], scale, ALU.mult)
            V.reduce(st[:, 0:1], s_sb[:, :], ALU.max)
            V.ts(st[:, 1:2], st[:, 0:1], -1.0, ALU.mult)
            a = A.act(s_sb[:, :], s_sb[:, :], ACT.Exp, bias=st[:, 1:2], accum=st[:, 2:3], after=[V])
            V.recip(st[:, 3:4], st[:, 2:3], after=[a])
            for j in range(4):
                t = T.turn(ps[2][:, j * P:(j + 1) * P], s_sb[:, j * P:(j + 1) * P], c["ident"][:, :], after=[a])
            tm = T.turn(ps[3][0:META, 0:P], s_sb[:, 512:512 + META], c["ident"][:, :])
            m1 = A.copy(pT[:, 0:4, :], ps[2][:, :].rearrange("p (j q) -> p j q", q=P), after=[t])
            m2 = V.copy(pT[0:META, 4, :], ps[3][0:META, 0:P], after=[tm])
            T.after(m1, m2)
            for j in range(4):
                T.mm(ps[4][:, 0:P], pT[:, j, :], one(vt, first + 2 * j, 1), start=j == 0, stop=False)
            t = T.mm(ps[4][:, 0:P], pT[0:META, 4, :], vm[:, :], start=False)
            V.ts(o_sb[:, :], ps[4][:, 0:P], st[:, 3:4], ALU.mult, after=[t])
            t = T.turn(ps[5][:, 0:P], o_sb[:, :], c["ident"][:, :], after=[V])
            os = bass.ds(r * CH, CH)
            for h in HALF:
                V.tt(oT[h, os], ps[5][h, h][:, ::-1], gate[h, os], ALU.mult, after=[t])

        with k.loop(4) as r:
            grid_row(r, 0, 7 - r)
        with k.loop(NC - 8) as r:
            grid_row(r + 4, r, 3)
        with k.loop(4) as r:
            grid_row(r + NC - 4, NC - 8, 3 - r)
        k.dma("mix_out", one(mix, p), oT[:, :])


def keep_masks(k, sb):
    keep = sb("keep", [P, 2, COLS], F32)
    k.G.fill(keep[:, :, :], 1.0)
    for d, at in ((0, 0), (1, CH - 1)):
        m = k.G.fill(keep[:, d, :].rearrange("p (c t) -> p c t", t=CH)[:, :, at:at + 1], 0.0)
    return keep, m


def chunk_sums(k, out, x, keep, d, after=()):
    V = k.V
    if d == 0:
        return V.scan(out[:, :], keep[:, 0, :], x[:, :], after=after)
    V.scan(out[:, 0:X0], keep[:, 0, 0:X0], x[:, 0:X0], after=after)
    back = slice(COLS - 1, X0 - 1, -1)
    return V.scan(out[:, back], keep[:, 1, back], x[:, back])


def chunk_ends(k, out, e, d):
    v = e[:, :].rearrange("p (c t) -> p c t", t=CH)
    if d == 0:
        return k.V.copy(out[:, :], v[:, :, CH - 1])
    k.V.copy(out[:, 0:1], v[:, 0:1, CH - 1])
    return k.V.copy(out[:, 1:], v[:, 1:, 0])


def both(*steps):
    steps = list(steps)
    while steps:
        for s in list(steps):
            if next(s, StopIteration) is StopIteration:
                steps.remove(s)


def spread(line, pair, src, n, after=()):
    for h in HALF:
        m = line.copy(pair[h, 0:n, h], src[h, :].rearrange("p (c t) -> p c t", t=CH), after=after)
    return m


def gla_branch(k, c, ps, io, hnT, mix, sb):
    V, A, T, G = k.V, k.A, k.T, k.G
    pr = Projector(k, ps, io["w_in"], hnT, sb, 4)
    keep, _ = keep_masks(k, sb)
    q = sb("gla_q", [P, COLS], F32)
    kk = sb("gla_k", [P, COLS], F32)
    vT = sb("gla_v", [P, NC + 1, 2, CH], F32)
    gd = [sb(f"gla_gd{d}", [META, COLS], F32) for d in range(2)]
    up = sb("gla_up", [16, 2, 2 * P], F32)
    upb = sb("gla_up_bias", [P, 2, 2], F32)
    upp = sb("gla_up_pair", [16, 2, P], F32)
    ng = sb("gla_norm", [P, 1], F32)
    gate = sb("gla_gate", [P, 2, SEQ], F32)
    o = sb("gla_out", [P, 2, SEQ], F32)
    lw = sb("gla_log_decay", [P, COLS], F32)
    cum = sb("gla_sums", [P, COLS], F32)
    tmp = sb("gla_tmp", [P, COLS], F32)
    qe = [sb(f"gla_qe{d}", [P, COLS], F32) for d in range(2)]
    ke = [sb(f"gla_ke{d}", [P, COLS], F32) for d in range(2)]
    dec = [sb(f"gla_dec{d}", [P, NC + 1], F32) for d in range(2)]
    small = [{n: sb(f"gla_{n}{d}", [P, RB, P], F32) for n in ("q2", "k2", "vc", "kt", "vt", "at", "ds")}
             for d in range(2)]
    state = [sb(f"gla_state{d}", [P, RB + 1, P], F32) for d in range(2)]
    for d in range(2):
        for n in ("q2", "k2"):
            G.fill(small[d][n][:, :, :], 0.0)
    for t in (q, kk, lw):
        G.fill(t[:, 0:M0], 0.0)
    G.fill(vT[:, 0, :, 0:M0], 0.0)
    k.dma("gla_small_in", up[:, :, :], io["gla_g_up"][0].rearrange("d r c -> r d c"))
    k.dma("gla_small_in", upb[:, :, :], io["gla_g_b_cols"].rearrange("p (d b) -> p d b", d=2))
    k.dma("gla_small_in", ng[:, :], io["gla_norm_g_cols"])
    base = NA_COLS
    for d in range(2):
        pr.load(slice(base + 3 * BW + 16 * d, base + 3 * BW + 16 * d + 16), 16)
    for d in range(2):
        copy_block(k, pr, gd[d])

    def chunks(d, n, first, seq, order):
        w, S = small[d], state[d]
        K = ps[4 * d:4 * d + 4]
        cols = bass.ds(first * CH, n * CH)
        a = A.copy(w["vc"][:, 0:n, :].rearrange("p c (h t) -> p c h t", t=CH), vT[:, bass.ds(first, n), :, :])
        g1 = spread(G, w["q2"], qe[d][:, cols], n)
        g2 = spread(G, w["k2"], ke[d][:, cols], n)
        yield
        T.after(a, g1, g2)
        for j in range(n):
            js = slice(j * P, j * P + P)
            T.mm(K[0][:, js], w["k2"][:, j, :], w["q2"][:, j, :])
            T.turn(K[1][:, js], w["k2"][:, j, :], c["ident"][:, :])
            t = T.turn(K[2][:, js], w["vc"][:, j, :], c["ident"][:, :])
        v3 = lambda b: K[b][:, 0:n * P].rearrange("p (c t) -> p c t", t=P)
        forwards = d == 0 or not seq
        mask = c["upto" if forwards else "from"][:, :].unsqueeze(1).broadcast_to([P, n, P])
        v1 = V.tt(w["at"][:, 0:n, :], v3(0), mask, ALU.mult, after=[t])
        a1 = A.copy(w["kt"][:, 0:n, :], v3(1), after=[t])
        a2 = A.copy(w["vt"][:, 0:n, :], v3(2))
        yield
        T.after(v1, a1, a2)
        for j in range(n):
            t = T.mm(K[1][:, j * P:j * P + P], w["kt"][:, j, :], w["vt"][:, j, :])
        V.tt(w["ds"][:, 0:n, :], v3(1), dec[d][:, bass.ds(first, n)].unsqueeze(2).broadcast_to([P, n, P]), ALU.mult,
             after=[t])
        for i, j in enumerate(order):
            m = V.stt(S[:, i + 1, :], S[:, i, :], dec[d][:, bass.ds(first + j, 1)], w["ds"][:, j, :], ALU.mult, ALU.add)
        yield
        if seq:
            T.after(m)
            for i, j in enumerate(order):
                js = slice(j * P, j * P + P)
                T.mm(K[0][:, js], w["vt"][:, j, :], w["at"][:, j, :], stop=False)
                t = T.mm(K[0][:, js], S[:, i, :], w["q2"][:, j, :], start=False)
            ov = o[:, :, bass.ds(first * CH - X0, n * CH)].rearrange("p h (c t) -> p c h t", t=CH)
            V.tt(ov, K[0][:, 0:n * P].rearrange("p (c h t) -> p c h t", h=2, t=CH), ov, ALU.add, after=[t])
        V.copy(S[:, 0, :], S[:, n, :])
        yield

    with k.loop(2) as p:
        pr.reset()
        for cols in (bass.ds(p * P + base, P), bass.ds(p * P + base + 256, P),
                     bass.ds(p * 256 + base + BW, P), bass.ds(p * 256 + base + BW + P, P),
                     bass.ds(p * 256 + base + 2 * BW, P), bass.ds(p * 256 + base + 2 * BW + P, P)):
            pr.load(cols)
            if pr.n == 4:
                copy_block(k, pr, q)
                copy_block(k, pr, kk)
        for h in range(2):
            def take(j, col, n, z, m, h=h):
                dst = vT[:, :, :, :].rearrange("p c h t -> p h c t")[:, h]
                if n < CH:
                    return [A.copy(dst[:, 0, M0:X0], z, after=[m])]
                return [A.copy(dst[:, col // CH:(col + n) // CH, :], z.rearrange("p (c t) -> p c t", t=CH), after=[m])]
            pr.block(take)
        for h in range(2):
            silu_block(k, pr, gate[:, h, :], tmp)
        A.copy(upp[:, :, :], up[:, :, bass.ds(p * P, P)])
        for d in range(2):
            for j, (col, n) in enumerate(SPANS):
                s = slice(col, col + n)
                t = T.mm(ps[6][:, 0:n], upp[:, d, :], gd[d][:, s],
                         after=[A, V, G])
                V.ts(lw[:, s], ps[6][:, 0:n], upb[:, d, bass.ds(p, 1)], ALU.add, after=[t])
            s = slice(M0, COLS)
            V.stt(tmp[:, s], lw[:, s], -1.0, lw[:, s], ALU.mult, ALU.min)
            A.act(tmp[:, s], tmp[:, s], ACT.Exp, after=[V])
            a = A.act(tmp[:, s], tmp[:, s], ACT.Ln, bias=1.0)
            V.stt(lw[:, s], lw[:, s], 0.0, tmp[:, s], ALU.min, ALU.subtract, after=[a])
            V.ts(lw[:, s], lw[:, s], 1.0 / 16.0, ALU.mult)
            v = chunk_sums(k, cum, lw, keep, d)
            a = A.act(tmp[:, :], cum[:, :], ACT.Exp, after=[v])
            V.stt(qe[d][:, :], q[:, :], CH ** -0.5, tmp[:, :], ALU.mult, ALU.mult, after=[a])
            v = chunk_ends(k, dec[d], tmp, d)
            a = A.act(tmp[:, :], cum[:, :], ACT.Exp, scale=-1.0, after=[v])
            V.tt(ke[d][:, :], kk[:, :], tmp[:, :], ALU.mult, after=[a])
            G.fill(state[d][:, 0, :], 0.0)
        G.fill(o[:, :, :], 0.0)
        A.after(V)
        G.after(V)
        V.after(G)
        both(*[chunks(d, 1, 0, False, [0]) for d in range(2)])
        with k.loop(NC // RB) as i:
            both(chunks(0, RB, i * RB + 1, True, range(RB)),
                 chunks(1, RB, (NC - RB + 1) - i * RB, True, range(RB)[::-1]))
        for h in range(2):
            for s in (slice(0, 512), slice(512, 1024)):
                a = A.act(tmp[:, s], o[:, h, s], ACT.Square, after=[V])
                t = T.mm(ps[0][:, :], c["ones"][:, :], tmp[:, s], after=[a])
                V.ts(tmp[:, s], ps[0][:, :], 1.0 / P, ALU.mult, 1e-5, ALU.add, after=[t])
                a = A.act(tmp[:, s], tmp[:, s], ACT.Sqrt, after=[V])
                V.recip(tmp[:, s], tmp[:, s], after=[a])
                V.tt(tmp[:, s], tmp[:, s], gate[:, h, s], ALU.mult)
                V.stt(o[:, h, s], o[:, h, s], ng[:, 0:1], tmp[:, s], ALU.mult, ALU.mult)
            k.dma("mix_out", one(mix, 2 * p + 4 + h), o[:, h, :], after=[V])


DECAY = float(np.exp(-0.5))


def rwkv_branch(k, c, ps, io, hnT, mix, sb):
    V, A, T, G = k.V, k.A, k.T, k.G
    pr = Projector(k, ps, io["w_in"], hnT, sb, 3)
    keep, _ = keep_masks(k, sb)
    full = lambda name, n=COLS: sb("rw_" + name, [P, n], F32)
    raw = full("raw", COLS + 2)
    r, kx, v, kk = full("r"), full("k"), full("v"), full("kk")
    twd, ad = full("decay_in"), full("alpha_in")
    kt, bt, at, rt = ([full(f"{n}{d}") for d in range(2)] for n in ("kt", "bt", "at", "rt"))
    tA = full("tmp_a")
    tB = raw[:, 1:1 + COLS]
    gate = full("gate", SEQ)
    bonus = full("bonus", SEQ)
    y = kx
    conv = sb("rw_conv_cols", [P, 3, 14], F32)
    wup = sb("rw_w_up", [P, BW], F32)
    aup = sb("rw_a_up", [P, BW], F32)
    up2 = sb("rw_up_pair", [P, 2, P], F32)
    w0 = sb("rw_w0c", [P, 2, 4], F32)
    a0 = sb("rw_a0c", [P, 2, 4], F32)
    vec = {n: sb(f"rw_{n}c", [P, 4], F32) for n in ("k_k", "k_a", "one_k_a", "r_k", "ln_g", "ln_b")}
    dec = [sb(f"rw_dec{d}", [P, NC + 1], F32) for d in range(2)]
    names = ("a2", "b2", "k2", "v2", "P0", "PT0", "P1", "PT1", "TT", "AK", "RQ", "aT", "bT", "kT", "vT", "QY")
    small = [{n: sb(f"rw_{n}_{d}", [P, RB, P], F32) for n in names} for d in range(2)]
    state = [sb(f"rw_state{d}", [P, P], F32) for d in range(2)]

    for d in range(2):
        for n in ("a2", "b2", "k2", "v2"):
            G.fill(small[d][n][:, :, :], 0.0)
    for t in (r, kk, v, tA, *kt, *bt, *at, *rt):
        G.fill(t[:, 0:M0], 0.0)
    G.fill(raw[:, :], 0.0)
    for name, t in (("rw_conv", conv), ("rw_w0", w0), ("rw_a0", a0)):
        k.dma("rw_small_in", t[:, :, :].rearrange("p a b -> p (a b)"), io[name + "_cols"])
    for n, t in vec.items():
        if n != "one_k_a":
            k.dma("rw_small_in", t[:, :], io[f"rw_{n}_cols"])
    k.dma("rw_small_in", wup[:, :], io["rw_w_up"][0].rearrange("d r c -> (d r) c"))
    small_in = k.dma("rw_small_in", aup[:, :], io["rw_a_up"][0].rearrange("d r c -> (d r) c"))
    V.ts(vec["one_k_a"][:, :], vec["k_a"][:, :], -1.0, ALU.mult, 1.0, ALU.add, after=[small_in, G])
    V.ts(w0[:, :, :], w0[:, :, :], -1.0, ALU.mult)
    V.ts(a0[:, :, :], a0[:, :, :], -1.0, ALU.mult)
    V.ts(vec["r_k"][:, :], vec["r_k"][:, :], 0.5, ALU.mult)
    A.after(V, G)
    T.after(V)

    def conv_block(out, blk):
        def take(j, col, n, z, m):
            return [A.copy(raw[:, 1 + col:1 + col + n], z, after=[m, V])]
        pr.block(take)
        s = slice(M0, COLS)
        tap = lambda i: conv[:, i, blk]
        V.ts(out[:, s], raw[:, 1 + M0:1 + COLS], tap(1), ALU.mult, after=[A, G])
        V.stt(out[:, s], raw[:, M0:COLS], tap(0), out[:, s], ALU.mult, ALU.add)
        V.stt(out[:, s], raw[:, 2 + M0:2 + COLS], tap(2), out[:, s], ALU.mult, ALU.add)

    for j in range(2):
        pr.load(slice(RW0 + 3 * BW + P * j, RW0 + 3 * BW + P * j + P))
    conv_block(twd, slice(12, 13))
    conv_block(ad, slice(13, 14))
    s0 = slice(M0, COLS)
    e = A.act(twd[:, s0], twd[:, s0], ACT.Tanh, after=[V])

    def chunks(d, n, first, seq, order):
        w, S = small[d], state[d]
        K = ps[4 * d:4 * d + 4]
        cols = bass.ds(first * CH, n * CH)
        v3 = lambda b: K[b][:, 0:n * P].rearrange("p (c t) -> p c t", t=P)
        v4 = lambda b: K[b][:, 0:n * P].rearrange("p (c x t) -> p c x t", x=2, t=CH)
        g = spread(G, w["k2"], kt[d][:, cols], n)
        g = spread(G, w["v2"], v[:, cols], n)
        a = spread(A, w["b2"], bt[d][:, cols], n)
        m = spread(V, w["a2"], at[d][:, cols], n)
        rs = A.copy(w["QY"][:, 0:n, 0:CH], rt[d][:, cols].rearrange("p (c t) -> p c t", t=CH))
        yield
        T.after(g, rs, m)
        for j in range(n):
            js = slice(j * P, j * P + P)
            T.mm(K[0][:, js], w["b2"][:, j, :], w["a2"][:, j, :])
            T.mm(K[1][:, js], w["a2"][:, j, :], w["b2"][:, j, :])
            T.mm(K[2][:, js], w["k2"][:, j, :], w["a2"][:, j, :])
            T.mm(K[3][:, j * P:j * P + CH], w["b2"][:, j, :], w["QY"][:, j, 0:CH])
            t = T.mm(K[3][:, j * P + CH:j * P + P], w["k2"][:, j, :], w["QY"][:, j, 0:CH])
        forwards = d == 0 or not seq
        less, more, upto = ("before", "after", "upto64") if forwards else ("after", "before", "from64")
        wide = lambda name: c[name][:, :].unsqueeze(1).broadcast_to([P, n, P])
        f1 = V.tt(w["PT0"][:, 0:n, :], v3(0), wide(less), ALU.mult, after=[t])
        f2 = V.tt(w["P0"][:, 0:n, :], v3(1), wide(more), ALU.mult)
        gt = G.tt(w["TT"][:, 0:n, :], w["PT0"][:, 0:n, :], wide("ident"), ALU.add, after=[f1])
        V.tt(w["AK"][:, 0:n, :], v3(2), wide(less), ALU.mult)
        for x in range(2):
            f3 = V.tt(w["RQ"][:, 0:n, x * CH:x * CH + CH], v4(3)[:, :, x, :],
                      c[upto][:, :].unsqueeze(1).broadcast_to([P, n, CH]), ALU.mult)
        yield
        T.after(f3)
        for b, (src, dst) in enumerate((("a2", "aT"), ("b2", "bT"), ("k2", "kT"), ("v2", "vT"))):
            for j in range(n):
                t = T.turn(K[b][:, j * P:j * P + P], w[src][:, j, :], c["ident"][:, :])
        for b, dst in enumerate(("aT", "bT", "kT", "vT")):
            a = A.copy(w[dst][:, 0:n, :], v3(b), after=[t])
        yield
        T.after(a, gt)
        x, xt = "P0", "PT0"
        for i in range(5):
            nx, nxt = ("P1", "PT1") if i % 2 == 0 else ("P0", "PT0")
            for j in range(n):
                js = slice(j * P, j * P + P)
                t = T.mm(K[0][:, js], w[xt][:, j, :], w[x][:, j, :])
            f = V.copy(w[nx][:, 0:n, :], v3(0), after=[t])
            if i < 4:
                for j in range(n):
                    t = T.mm(K[1][:, j * P:j * P + P], w[x][:, j, :], w[xt][:, j, :])
                a = A.copy(w[nxt][:, 0:n, :], v3(1), after=[t])
            yield
            T.after(f)
            for j in range(n):
                t = T.mm(K[2][:, j * P:j * P + P], w[nx][:, j, :], w["TT"][:, j, :])
            f = V.tt(w["TT"][:, 0:n, :], v3(2), w["TT"][:, 0:n, :], ALU.add, after=[t])
            T.after(a)
            x, xt = nx, nxt
            yield
        for j in range(n):
            t = T.mm(K[3][:, j * P:j * P + P], w["AK"][:, j, :], w["vT"][:, j, :])
        a = A.copy(w["P0"][:, 0:n, :], v3(3), after=[t])
        yield
        T.after(f, a)
        for j in range(n):
            js = slice(j * P, j * P + P)
            T.mm(K[0][:, js], w["TT"][:, j, :], w["aT"][:, j, :])
            t = T.mm(K[1][:, js], w["TT"][:, j, :], w["P0"][:, j, :])
        a = A.copy(w["PT0"][:, 0:n, :], v3(0), after=[t])
        f = V.copy(w["PT1"][:, 0:n, :], v3(1), after=[t])
        yield
        T.after(a, f)
        for j in range(n):
            js = slice(j * P, j * P + P)
            T.mm(K[0][:, js], w["PT0"][:, j, :], w["bT"][:, j, :])
            T.mm(K[1][:, js], w["kT"][:, j, :], w["vT"][:, j, :], stop=False)
            T.mm(K[1][:, js], w["bT"][:, j, :], w["PT1"][:, j, :], start=False)
            q, yy = slice(j * P, j * P + CH), slice(j * P + CH, j * P + P)
            T.mm(K[2][:, q], w["PT0"][:, j, :], w["RQ"][:, j, 0:CH])
            T.mm(K[2][:, yy], w["vT"][:, j, :], w["RQ"][:, j, CH:], stop=False)
            t = T.mm(K[2][:, yy], w["PT1"][:, j, :], w["RQ"][:, j, 0:CH], start=False)
        V.tt(w["P1"][:, 0:n, :], v3(0), wide("ident"), ALU.add, after=[t])
        V.tt(w["a2"][:, 0:n, :], v3(1), dec[d][:, bass.ds(first, n)].unsqueeze(2).broadcast_to([P, n, P]), ALU.mult)
        f = V.tt(w["QY"][:, 0:n, 0:CH], v4(2)[:, :, 0, :], w["QY"][:, 0:n, 0:CH], ALU.add)
        yv = None
        if seq:
            yv = y[:, bass.ds(first * CH - X0, n * CH)].rearrange("p (c t) -> p c t", t=CH)
            f = V.tt(w["QY"][:, 0:n, CH:], v4(2)[:, :, 1, :], yv, ALU.add)
        yield
        for j in order:
            T.after(f)
            if seq:
                T.mm(K[3][:, 0:CH], S[:, :], w["QY"][:, j, 0:CH])
            t = T.mm(K[3][:, P:2 * P], w["P1"][:, j, :], S[:, :])
            f = V.stt(S[:, :], K[3][:, P:2 * P], dec[d][:, bass.ds(first + j, 1)], w["a2"][:, j, :], ALU.mult, ALU.add,
                      after=[t])
            if seq:
                f = V.tt(y[:, bass.ds((first + j) * CH - X0, CH)], K[3][:, 0:CH], w["QY"][:, j, CH:], ALU.add)
            yield

    blocks = SEQ // 512
    with k.loop(4) as p:
        pr.reset()
        for j in range(3):
            pr.load(bass.ds(p * P + RW0 + j * BW, P))
        for j, out in enumerate((r, kx, v)):
            conv_block(out, bass.ds(p + 4 * j, 1))
            if j == 0:
                pr.load(bass.ds(p * P + RW0 + 3 * BW + 2 * P, P))
        silu_block(k, pr, gate, tA)
        A.copy(up2[:, 0, :], wup[:, bass.ds(p * P, P)])
        A.copy(up2[:, 1, :], aup[:, bass.ds(p * P, P)])
        one_col = lambda t: t[:, bass.ds(p, 1)]

        def group_sum(x, s, after):
            return T.mm(ps[7][:, 0:s.stop - s.start], c["halves"][:, :], x[:, s], after=after)

        V.ts(kk[:, s0], kx[:, s0], one_col(vec["k_k"]), ALU.mult)
        a = A.act(tB[:, s0], kk[:, s0], ACT.Square, after=[V])
        for col, n in SPANS:
            s = slice(col, col + n)
            t = group_sum(tB, s, [a, V])
            a2 = A.act(tA[:, s], ps[7][:, 0:n], ACT.Sqrt, after=[t])
            V.ts(tA[:, s], tA[:, s], 1e-12, ALU.max, after=[a2])
            V.recip(tA[:, s], tA[:, s])
            V.tt(kk[:, s], kk[:, s], tA[:, s], ALU.mult)
        for d in range(2):
            def lora(x, which, bias, out):
                for col, n in SPANS:
                    s = slice(col, col + n)
                    t = T.mm(ps[6][:, 0:n], up2[HALF[d], which, :], x[HALF[d], s], after=[A])
                    sigmoid_of(k, out[:, s], ps[6][:, 0:n], bias=bias[:, d, bass.ds(p, 1)], after=[t, V])
            lora(ad, 1, a0, tA)
            V.tt(bt[d][:, s0], kk[:, s0], tA[:, s0], ALU.mult)
            V.ts(tA[:, s0], tA[:, s0], one_col(vec["k_a"]), ALU.mult, one_col(vec["one_k_a"]), ALU.add)
            V.tt(kt[d][:, s0], kx[:, s0], tA[:, s0], ALU.mult)
            lora(twd, 0, w0, tA)
            V.ts(tA[:, s0], tA[:, s0], -DECAY, ALU.mult)
            G.fill(tA[:, 0:M0], 0.0, after=[V])
            f = chunk_sums(k, tB, tA, keep, d, after=[G])
            if d == 0:
                V.copy(bonus[:, :], kt[0][:, X0:])
            else:
                V.tt(bonus[:, :], bonus[:, :], kt[1][:, X0:], ALU.add)
            V.tt(tA[:, :], tB[:, :], tA[:, :], ALU.subtract)
            a = A.act(tA[:, :], tA[:, :], ACT.Exp, after=[V])
            V.stt(at[d][:, s0], kk[:, s0], -1.0, tA[:, s0], ALU.mult, ALU.mult, after=[a])
            a = A.act(tA[:, :], tB[:, :], ACT.Exp, after=[V])
            V.tt(rt[d][:, s0], r[:, s0], tA[:, s0], ALU.mult, after=[a])
            chunk_ends(k, dec[d], tA, d)
            a = A.act(tA[:, :], tB[:, :], ACT.Exp, scale=-1.0, after=[V])
            V.tt(kt[d][:, s0], kt[d][:, s0], tA[:, s0], ALU.mult, after=[a])
            V.tt(bt[d][:, s0], bt[d][:, s0], tA[:, s0], ALU.mult)
            G.fill(state[d][:, :], 0.0)
        V.tt(bonus[:, :], bonus[:, :], r[:, X0:], ALU.mult)
        V.ts(bonus[:, :], bonus[:, :], one_col(vec["r_k"]), ALU.mult)
        for i in range(blocks):
            s = slice(512 * i, 512 * i + 512)
            t = group_sum(bonus, s, [V])
            V.tt(bonus[:, s], ps[7][:, :], v[:, X0 + 512 * i:X0 + 512 * i + 512], ALU.mult, after=[t])
        G.fill(y[:, 0:SEQ], 0.0, after=[V])
        A.after(V)
        V.after(G)
        both(*[chunks(d, 1, 0, False, [0]) for d in range(2)])
        with k.loop(NC // RB) as i:
            both(chunks(0, RB, i * RB + 1, True, range(RB)),
                 chunks(1, RB, (NC - RB + 1) - i * RB, True, range(RB)[::-1]))
        for i in range(blocks):
            s = slice(512 * i, 512 * i + 512)
            t = group_sum(y, s, [V])
            V.stt(y[:, s], ps[7][:, :], -1.0 / CH, y[:, s], ALU.mult, ALU.add, after=[t])
            a = A.act(tA[:, s], y[:, s], ACT.Square, after=[V])
            t = group_sum(tA, s, [a])
            V.ts(tA[:, s], ps[7][:, :], 1.0 / CH, ALU.mult, 64e-5, ALU.add, after=[t])
            a = A.act(tA[:, s], tA[:, s], ACT.Sqrt, after=[V])
            V.recip(tA[:, s], tA[:, s], after=[a])
            V.stt(y[:, s], y[:, s], one_col(vec["ln_g"]), tA[:, s], ALU.mult, ALU.mult)
            V.stt(y[:, s], y[:, s], one_col(vec["ln_b"]), bonus[:, s], ALU.add, ALU.add)
            V.tt(y[:, s], y[:, s], gate[:, s], ALU.mult)
        k.dma("mix_out", one(mix, p + 8), y[:, 0:SEQ], after=[V])


NT = SEQ // P
ALPHA = 4 ** 0.25
LN_EPS = 1e-5


def row_in(k, name, t, src):
    return k.dma(name, t[:, :], src.partition_broadcast(P))


def layer_norm_tile(k, st, y, total, g, b, out, dump):
    V, A, G = k.V, k.A, k.G
    V.ts(st[:, 0:1], total, -1.0 / D, ALU.mult)
    a = A.act(dump, y, ACT.Square, bias=st[:, 0:1], accum=st[:, 1:2], after=[V])
    V.ts(st[:, 1:2], st[:, 1:2], 1.0 / D, ALU.mult, LN_EPS, ALU.add, after=[a])
    a = A.act(st[:, 1:2], st[:, 1:2], ACT.Sqrt, after=[V])
    V.recip(st[:, 2:3], st[:, 1:2], after=[a])
    V.ts(y, y, st[:, 0:1], ALU.add, st[:, 2:3], ALU.mult)
    v = V.tt(y, y, g, ALU.mult)
    return G.tt(out, y, b, ALU.add, after=[v])


def out_project(k, ps, sb, src, blocks, w, finish):
    A, T = k.A, k.T
    wt = sb("out_w", [P, blocks, D], F32)
    xt = [sb(f"out_in{i}", [P, blocks, P], F32) for i in range(2)]
    wv = w.rearrange("(b p) n -> p b n", p=P)
    for b in range(0, blocks, 4):
        k.dma("out_w_in", wt[:, b:b + 4, :], wv[:, b:b + 4, :])
    with k.loop(NT // 2) as i:
        marks = [k.dma(f"out_in{u}", xt[u][:, :, :],
                       src[0:blocks, :, bass.ds((2 * i + u) * P, P)].rearrange("b p t -> p b t")) for u in range(2)]
        for u in range(2):
            T.after(marks[u])
            for h in range(2):
                for b in range(blocks):
                    t = T.mm(ps[2 * u + h][:, :], xt[u][:, b, :], wt[:, b, 512 * h:512 * h + 512],
                             start=b == 0, stop=b == blocks - 1)
            finish(2 * i + u, ps[2 * u:2 * u + 2], t)


def tile_of(X, t):
    return one(X, t, 1)


def block_one_out(k, ps, io, mix, X, sb):
    V, A = k.V, k.A
    y = sb("h_tile", [P, D], F32)
    xin = sb("h_in", [P, D], F32)
    dump = sb("squares", [P, D], F32)
    g = sb("final_g", [P, D], F32)
    st = sb("out_stats", [P, 2], F32)
    row_in(k, "final_g_in", g, io["final_norm_g"])

    def finish(t, banks, m):
        x = k.dma("h_in", xin[:, :], io["x"][0, bass.ds(t * P, P), :], after=[V])
        for h in range(2):
            s = slice(512 * h, 512 * h + 512)
            V.tt(y[:, s], banks[h][:, :], xin[:, s], ALU.add, after=[m, x, A])
        rms_scale(k, st, y[:, :], P, 1e-6, dump[:, :], after=[V])
        V.stt(tile_of(X, t), y[:, :], st[:, 1:2], g[:, :], ALU.mult, ALU.mult)

    out_project(k, ps, sb, mix, 12, io["w_out"][0], finish)


def mixer_out(k, ps, io, mix, blocks, w, layer, X, sb):
    V, A, G = k.V, k.A, k.G
    y = sb("y_tile", [P, D], F32)
    dump = sb("squares", [P, D], F32)
    g, b = sb("ln_g", [P, D], F32), sb("ln_b", [P, D], F32)
    st = sb("ln_stats", [P, 6], F32)
    row_in(k, "ln_in", g, io["ln_mix_g_2"][layer])
    row_in(k, "ln_in", b, io["ln_mix_b_2"][layer])

    def finish(t, banks, m):
        for h in range(2):
            s = slice(512 * h, 512 * h + 512)
            V.start([m, A, G])
            V.done(V.eng.scalar_tensor_tensor(y[:, s], tile_of(X, t)[:, s], ALPHA, banks[h][:, :], ALU.mult, ALU.add,
                                              accum_out=st[:, 3 + h:4 + h]))
        V.tt(st[:, 5:6], st[:, 3:4], st[:, 4:5], ALU.add)
        layer_norm_tile(k, st, y[:, :], st[:, 5:6], g[:, :], b[:, :], tile_of(X, t), dump[:, :])

    out_project(k, ps, sb, mix, blocks, w, finish)


def turned(k, c, ps, X, tile, take):
    with k.loop(NT) as t:
        m = k.A.copy(tile[:, :], tile_of(X, t))
        k.T.after(m)
        for b in range(KD):
            m = k.T.turn(ps[b // 4][:, (b % 4) * P:(b % 4) * P + P], tile[:, b * P:(b + 1) * P], c["ident"][:, :])
        take(t, m)


def transpose_x(k, c, ps, X, xT, sb):
    tile = sb("x_tile", [P, D], F32)

    def take(t, m):
        for h in range(2):
            (k.V if h else k.A).copy(xT[:, 4 * h:4 * h + 4, bass.ds(t * P, P)],
                                     ps[h][:, :].rearrange("p (b t) -> p b t", b=4), after=[m])
    turned(k, c, ps, X, tile, take)


def windowed_attention(k, c, ps, io, X, mix, sb):
    V, A, T, G = k.V, k.A, k.T, k.G
    HQ, HK, HD = 16, 4, 64
    BAND = 3 * P
    spans = [(0, 512), (512, 512)]
    xT = sb("xT", [P, KD, SEQ], F32)
    transpose_x(k, c, ps, X, xT, sb)
    pr = Projector(k, ps, io["attn_w_qkv_2"], xT, sb, 3)
    cos, sin = sb("cos", [P, SEQ], F32), sb("sin", [P, SEQ], F32)
    rot = sb("rotate", [P, P], F32)
    wv = sb("wv", [P, KD, HK * HD], F32)
    qT = sb("aq", [P, 2, SEQ], F32)
    kT = sb("ak", [P, SEQ + 2 * P], F32)
    vt = sb("av", [P, NT + 2, HK * HD], F32)
    raw, tmp = sb("a_raw", [P, SEQ], F32), sb("a_tmp", [P, SEQ], F32)
    oT = sb("ao", [P, 2, SEQ], F32)
    mask = sb("a_mask", [P, 3, BAND], F32)
    sink = sb("a_sink", [P, HQ], F32)
    qw = sb("a_qw", [P, 2, P], F32)
    kw = sb("a_kw", [P, BAND], F32)
    vw = sb("a_vw", [P, 3, HD], F32)
    s_sb = sb("a_s", [P, 4, BAND], F32)
    pT = sb("a_pT", [P, 4, BAND], F32)
    st = sb("a_st", [P, 5, 4], F32)
    for e in range(3):
        G.fill(mask[:, e, :], 0.0)
        rules = [(0, 1, -1), (2 * P, -1, 1)]
        if e != 1:
            rules.append((-P, 1, 0) if e == 0 else (2 * P - 1, -1, 0))
        for base, col, part in rules:
            G.start(())
            G.done(G.eng.affine_select(out=mask[:, e, :], in_=mask[:, e, :], compare_op=ALU.is_ge, fill=NEG, base=base,
                                       pattern=[[col, BAND]], channel_multiplier=part))
    for e in (0, SEQ + P):
        G.fill(kT[:, e:e + P], 0.0)
    for e in (0, NT + 1):
        G.fill(vt[:, e, :], 0.0)
    k.dma("a_small_in", cos[:, :], io["rope_cos"])
    k.dma("a_small_in", sin[:, :], io["rope_sin"])
    k.dma("a_small_in", rot[:, :], io["rope_turn"])
    row_in(k, "a_small_in", sink, io["attn_sink_2"][0])
    w3 = io["attn_w_qkv_2"][0].rearrange("(k p) c -> p k c", p=P)
    m = k.dma("a_wv_in", wv[:, :, :], w3[:, :, (HQ + HK) * HD:])
    T.after(m)
    for t in range(NT):
        bank = ps[6 + t % 2]
        T.after(A)
        for d in range(KD):
            m = T.mm(bank[:, 0:HK * HD], xT[:, d, t * P:(t + 1) * P], wv[:, d, :], start=d == 0, stop=d == KD - 1)
        A.copy(vt[:, t + 1, :], bank[:, 0:HK * HD], after=[m])

    def rotary(out):
        def take(j, col, n, z, m):
            s = slice(col, col + n)
            a = A.copy(raw[:, s], z, after=[m, V, T])
            t = T.mm(ps[6 + j][:, 0:n], rot[:, :], raw[:, s], after=[a, V])
            V.tt(tmp[:, s], ps[6 + j][:, 0:n], sin[:, s], ALU.mult, after=[t])
            g = G.tt(out[:, s], raw[:, s], cos[:, s], ALU.mult, after=[a, V])
            return [V.tt(out[:, s], out[:, s], tmp[:, s], ALU.add, after=[g])]
        pr.block(take, spans)

    def block(qb, g, e):
        scale = HD ** -0.5
        m1 = A.copy(qw[:, :, :], qT[:, :, bass.ds(qb * P, P)])
        m2 = G.copy(kw[:, :], kT[:, bass.ds(qb * P, BAND)])
        m3 = G.copy(vw[:, :, :], vt[:, bass.ds(qb, 3), bass.ds(g * HD, HD)])
        T.after(m1, m2, m3)
        for h in range(4):
            half = HALF[h % 2]
            m = T.mm(ps[h][:, 0:BAND], qw[half, h // 2, :], kw[half, :])
            V.stt(s_sb[:, h, :], ps[h][:, 0:BAND], scale, mask[:, e, :], ALU.mult, ALU.add, after=[m])
        V.reduce(st[:, 0, :], s_sb[:, :, :], ALU.max)
        sk = sink[:, bass.ds(g * 4, 4)]
        V.tt(st[:, 0, :], st[:, 0, :], sk, ALU.max)
        V.ts(st[:, 1, :], st[:, 0, :], -1.0, ALU.mult)
        v = V.tt(st[:, 2, :], sk, st[:, 0, :], ALU.subtract)
        for h in range(4):
            A.act(s_sb[:, h, :], s_sb[:, h, :], ACT.Exp, bias=st[:, 1, h:h + 1], accum=st[:, 3, h:h + 1], after=[v])
        a = A.act(st[:, 2, :], st[:, 2, :], ACT.Exp)
        V.tt(st[:, 3, :], st[:, 3, :], st[:, 2, :], ALU.add, after=[a])
        V.recip(st[:, 4, :], st[:, 3, :])
        for h in range(4):
            v = V.ts(s_sb[:, h, :], s_sb[:, h, :], st[:, 4, h:h + 1], ALU.mult)
            T.after(v)
            for j in range(3):
                m = T.turn(ps[h][:, j * P:(j + 1) * P], s_sb[:, h, j * P:(j + 1) * P], c["ident"][:, :])
            a = A.copy(pT[:, h, :], ps[h][:, 0:BAND], after=[m])
        T.after(a)
        for h in range(4):
            half = HALF[h % 2]
            for j in range(3):
                m = T.mm(ps[4][half, (h // 2) * P:(h // 2) * P + P], vw[:, j, :], pT[:, h, j * P:(j + 1) * P],
                         start=j == 0, stop=j == 2)
        A.copy(oT[:, :, bass.ds(qb * P, P)], ps[4][:, 0:2 * P].rearrange("p (x q) -> p x q", x=2), after=[m])

    with k.loop(HK) as g:
        pr.reset()
        for half in HALF:
            pr.part(half, bass.ds(g * HD + HQ * HD, HD))
        pr.whole()
        pr.load(bass.ds(g * 2 * P, P))
        pr.load(bass.ds(g * 2 * P + P, P))
        rotary(kT[:, P:P + SEQ])
        for x in range(2):
            rotary(qT[:, x, :])
        for line in (A, G, T):
            line.after(V)
        block(0, g, 0)
        with k.loop(NT - 2) as b:
            block(b + 1, g, 1)
        block(NT - 1, g, 2)
        k.dma("mix_out", mix[bass.ds(2 * g, 2), :, :].rearrange("x p t -> p x t"), oT[:, :, :], after=[A])


def lru(k, c, ps, io, X, mix, sb):
    V, A, T, G = k.V, k.A, k.T, k.G
    BLK = 256
    spans = [(0, 512), (512, 512)]
    xT = sb("xT", [P, KD, SEQ], F32)
    transpose_x(k, c, ps, X, xT, sb)
    pr = Projector(k, ps, io["lru_w_in_2"], xT, sb, 4)
    gate = sb("l_gate", [P, 2, SEQ], F32)
    raw = sb("l_raw", [P, SEQ + 3], F32)
    xc = sb("l_xc", [P, 2, SEQ], F32)
    rr, ii, a_, t1 = (sb(f"l_{n}", [P, SEQ], F32) for n in ("r", "i", "a", "t"))
    hf, hb = sb("l_hf", [P, SEQ], F32), sb("l_hb", [P, SEQ], F32)
    wg = sb("l_wg", [P, 2, 2, 2, BLK], F32)
    cw, cb = sb("l_cw", [P, 4, 8], F32), sb("l_cb", [P, 8], F32)
    bg = sb("l_bg", [P, 2, 2, 8], F32)
    lam = sb("l_lam", [P, 2, 8], F32)
    sm = [sb(f"l_sm{i}", [P, 2, 8], F32) for i in range(4)]
    for t, n in ((cw[:, :, :].rearrange("p a b -> p (a b)"), "lru_conv_w_2"), (cb[:, :], "lru_conv_b_2"),
                 (bg[:, 0].rearrange("p a b -> p (a b)"), "lru_b_rgate_2"),
                 (bg[:, 1].rearrange("p a b -> p (a b)"), "lru_b_igate_2"),
                 (lam[:, :, :].rearrange("p a b -> p (a b)"), "lru_lambda_2")):
        m = k.dma("l_small_in", t, io[n + "_cols"])
    G.fill(raw[:, :], 0.0)
    e, s, s2, acc = (x[:, :, :] for x in sm)
    V.ts(bg[:, :, :, :].rearrange("p a b c -> p (a b c)"), bg[:, :, :, :].rearrange("p a b c -> p (a b c)"), -1.0,
         ALU.mult, after=[m])
    L = lam[:, :, :]
    V.stt(e, L, -1.0, L, ALU.mult, ALU.min)
    a = A.act(e, e, ACT.Exp, after=[V])
    V.ts(s, e, 2.0, ALU.add, after=[a])
    V.recip(s, s)
    V.tt(s, s, e, ALU.mult)
    V.tt(s2, s, s, ALU.mult)
    V.ts(acc, s2, 1.0 / 19, ALU.mult)
    for n in (17, 15, 13, 11, 9, 7, 5, 3):
        V.stt(acc, acc, 1.0 / n, s2, ALU.add, ALU.mult)
    V.stt(acc, acc, 1.0, s, ALU.add, ALU.mult)
    V.ts(L, L, -1.0, ALU.mult, 0.0, ALU.max)
    V.stt(L, acc, 2.0, L, ALU.mult, ALU.add)
    V.ts(L, L, -8.0, ALU.mult)
    A.after(V)

    with k.loop(4) as n:
        pr.reset()
        for x in range(2):
            pr.load(bass.ds(n * BLK + D + x * P, P))
        for x in range(2):
            pr.load(bass.ds(n * BLK + x * P, P))
        for q, name in enumerate(("lru_w_rgate_2", "lru_w_igate_2")):
            for z in range(2):
                wm = k.dma("l_wg_in", wg[:, q, z], one(io[name][0, z], n).rearrange("(c p) f -> p c f", p=P))
        for x in range(2):
            def take(j, col, m_, z, m):
                return [A.copy(raw[:, 2 + col:2 + col + m_], z, after=[m, V, G])]
            pr.block(take, spans)
            col = lambda t: t[:, bass.ds(2 * n + x, 1)]
            V.ts(xc[:, x, :], raw[:, 0:SEQ], cw[:, 0, bass.ds(2 * n + x, 1)], ALU.mult, col(cb), ALU.add, after=[A, G])
            for j in range(1, 4):
                V.stt(xc[:, x, :], raw[:, j:j + SEQ], cw[:, j, bass.ds(2 * n + x, 1)], xc[:, x, :], ALU.mult, ALU.add)
        for x in range(2):
            def take(j, col, m_, z, m):
                s = slice(col, col + m_)
                a = A.act(t1[:, s], z, ACT.Square, after=[m, V])
                V.ts(t1[:, s], t1[:, s], 0.044715, ALU.mult, 1.0, ALU.add, after=[a])
                V.tt(t1[:, s], t1[:, s], z, ALU.mult)
                a = A.act(t1[:, s], t1[:, s], ACT.Exp, scale=-2 * (2 / np.pi) ** 0.5, after=[V])
                V.ts(t1[:, s], t1[:, s], 1.0, ALU.add, after=[a])
                V.recip(t1[:, s], t1[:, s])
                return [V.tt(gate[:, x, s], z, t1[:, s], ALU.mult)]
            pr.block(take, spans)
        for x in range(2):
            for z in range(2):
                for q, out in enumerate((rr, ii)):
                    for j, (col, m_) in enumerate(spans):
                        s = slice(col, col + m_)
                        bank = ps[2 * q + j]
                        T.after(wm, V)
                        for h in range(2):
                            m = T.mm(bank[:, :], wg[:, q, z, h, x * P:(x + 1) * P], xc[:, h, s], start=h == 0, stop=h == 1)
                        sigmoid_of(k, out[:, s], bank[:, :], bias=bg[:, q, z, bass.ds(2 * n + x, 1)], after=[m, V])
                V.ts(rr[:, :], rr[:, :], lam[:, z, bass.ds(2 * n + x, 1)], ALU.mult)
                A.act(a_[:, :], rr[:, :], ACT.Exp, after=[V])
                a = A.act(rr[:, :], rr[:, :], ACT.Tanh)
                V.ts(t1[:, :], rr[:, :], -1.0, ALU.mult, 1.0, ALU.add, after=[a])
                V.recip(t1[:, :], t1[:, :])
                V.stt(t1[:, :], t1[:, :], -2.0, rr[:, :], ALU.mult, ALU.mult)
                a = A.act(t1[:, :], t1[:, :], ACT.Sqrt, after=[V])
                start = 0 if z == 0 else SEQ - 1
                V.fill(t1[:, start:start + 1], 1.0, after=[a])
                V.tt(t1[:, :], t1[:, :], ii[:, :], ALU.mult)
                V.tt(t1[:, :], t1[:, :], xc[:, x, :], ALU.mult)
                o, back = (hf, slice(0, SEQ)) if z == 0 else (hb, slice(SEQ - 1, None, -1))
                V.scan(o[:, back], a_[:, back], t1[:, back])
            V.tt(hf[:, :], hf[:, :], hb[:, :], ALU.add)
            V.tt(gate[:, x, :], gate[:, x, :], hf[:, :], ALU.mult)
        k.dma("mix_out", mix[bass.ds(2 * n, 2), :, :].rearrange("x p t -> p x t"), gate[:, :, :], after=[V])


NE, FF, CAP = 16, 1024, 128


def moe(k, c, ps, io, layer, X, out, sb):
    nc, V, A, T, G = k.nc, k.V, k.A, k.T, k.G
    CHUNKS = 12
    ring = sb("ring", [P, CHUNKS, 2 * FF], F32)
    Y = sb("Y", [P, NT, D], F32)
    tile = sb("m_tile", [P, D], F32)
    xs = sb("m_xs", [P, D], F32)
    Pm, Pg, PgT = (sb(f"m_{n}", [P, NT, CAP], F32) for n in ("pick", "pick_gated", "place"))
    hid, ys = sb("m_hid", [P, FF], F32), sb("m_ys", [P, D], F32)
    wr = sb("m_router", [P, KD, NE], F32)
    aff = sb("m_aff", [P, NT, NE], F32)
    slot = sb("m_slot", [P, NT, NE], F32)
    st = sb("m_st", [P, 6], F32)
    iota = sb("m_iota", [P, CAP], F32)
    landed = [k.ctx.enter_context(nc.semaphore(f"slab_landed{layer}_{i}")) for i in range(CHUNKS)]
    gu, dn = io["moe_w_gate_up_2"][layer], io["moe_w_down_2"][layer]

    def load(e, i, after=()):
        k.S.after(*after)
        if i < 8:
            src, dst = one(gu, e)[i * P:(i + 1) * P, :], ring[:, i, :]
        else:
            src = one(dn, e)[(i - 8) * 2 * P:(i - 7) * 2 * P, :].rearrange("(a p) d -> p a d", p=P)
            dst = ring[:, i, :].rearrange("p (a d) -> p a d", a=2)
        nc.sync.dma_start(dst, src).then_inc(landed[i], 16)

    def arrived(i):
        nc.tensor.wait_ge(landed[i], 16)
        nc.tensor.sem_clear(landed[i])

    m = k.dma("router_in", wr[:, :, :], io["moe_w_router_2"][layer].rearrange("(k p) e -> p k e", p=P))
    for i in range(CHUNKS):
        load(0, i)
    G.start(())
    G.done(G.eng.iota(iota[:, :], pattern=[[1, CAP]], base=0, channel_multiplier=0,
                      allow_small_or_imprecise_dtypes=True))

    affT, work, sel = (b[0:NE, :] for b in (xs, hid, ys))
    top = Pm[0:NE, 0, 0:8]

    def route(t, m):
        for h in range(2):
            V.copy(Pg[:, 4 * h:4 * h + 4, :], ps[h][:, :].rearrange("p (b t) -> p b t", b=4), after=[m])
        T.after(V)
        for d in range(KD):
            m = T.mm(ps[2][:, 0:NE], Pg[:, d, :], wr[:, d, :], start=d == 0, stop=d == KD - 1)
        V.reduce(st[:, 0:1], ps[2][:, 0:NE], ALU.max, after=[m])
        V.ts(st[:, 1:2], st[:, 0:1], -1.0, ALU.mult)
        a = A.act(PgT[:, 0, 0:NE], ps[2][:, 0:NE], ACT.Exp, bias=st[:, 1:2], accum=st[:, 2:3], after=[V])
        V.recip(st[:, 3:4], st[:, 2:3], after=[a])
        V.ts(PgT[:, 1, 0:NE], PgT[:, 0, 0:NE], st[:, 3:4], ALU.mult)
        a = A.copy(tile_of(aff, t), PgT[:, 1, 0:NE], after=[V])
        m = T.turn(ps[3][0:NE, 0:P], PgT[:, 1, 0:NE], c["ident"][:, :], after=[V])
        V.copy(affT[:, bass.ds(t * P, P)], ps[3][0:NE, 0:P], after=[m])
        V.ts(tile_of(Y, t), tile[:, :], ALPHA, ALU.mult)

    turned(k, c, ps, X, tile, route)

    V.copy(work, affT)
    for i in range(CAP // 8):
        V.start(())
        V.done(V.eng.max(top, work))
        V.start(())
        V.done(V.eng.match_replace(work, top, work, -1.0))
    V.ts(sel, work, 0.0, ALU.is_lt)
    V.fill(affT, 1.0)
    V.scan(work, affT, sel)
    V.tt(work, work, sel, ALU.mult)
    v = V.ts(work, work, -1.0, ALU.add)
    T.after(v)
    for t in range(NT):
        m = T.turn(ps[4][:, t * NE:(t + 1) * NE], work[:, t * P:(t + 1) * P], c["ident"][0:NE, 0:NE])
    V.copy(slot[:, :, :], ps[4][:, 0:NT * NE].rearrange("p (t e) -> p t e", e=NE), after=[m])

    def expert(e, last):
        at = lambda x: x[:, :, bass.ds(e, 1)].broadcast_to([P, NT, CAP])
        v = V.tt(Pm[:, :, :], iota[:, :].unsqueeze(1).broadcast_to([P, NT, CAP]), at(slot), ALU.is_equal)
        g = G.tt(Pg[:, :, :], Pm[:, :, :], at(aff), ALU.mult, after=[v])
        T.after(v)
        for d in range(KD):
            for t in range(NT):
                m = T.mm(ps[4 + d // 4][:, (d % 4) * P:(d % 4) * P + P], X[:, t, d * P:(d + 1) * P], Pm[:, t, :],
                         start=t == 0, stop=t == NT - 1)
            if d % 4 == 3:
                h = d // 4
                a = (V if h else A).copy(xs[:, 512 * h:512 * h + 512], ps[4 + h][:, :], after=[m])
                T.after(a)
        T.after(g)
        for t in range(NT):
            m = T.turn(ps[6 + t // 4][:, (t % 4) * P:(t % 4) * P + P], Pg[:, t, :], c["ident"][:, :])
        for h in range(2):
            pm = A.copy(PgT[:, 4 * h:4 * h + 4, :], ps[6 + h][:, :].rearrange("p (b t) -> p b t", b=4), after=[m])
        for d in range(KD):
            arrived(d)
            for j in range(4):
                m = T.mm(ps[j][:, :], xs[:, d * P:(d + 1) * P], ring[:, d, 512 * j:512 * j + 512], start=d == 0,
                         stop=d == KD - 1)
            if not last:
                load(e + 1, d, after=[m])
        for h in range(2):
            s = slice(512 * h, 512 * h + 512)
            a = A.act(hid[:, s], ps[h][:, :], ACT.Exp, scale=-1.0, after=[m])
            V.ts(hid[:, s], hid[:, s], 1.0, ALU.add, after=[a])
            V.recip(hid[:, s], hid[:, s])
            V.tt(hid[:, s], hid[:, s], ps[h][:, :], ALU.mult)
            v = V.tt(hid[:, s], hid[:, s], ps[2 + h][:, :], ALU.mult)
            T.after(v)
            for b in range(4 * h, 4 * h + 4):
                t_ = T.turn(ps[4 + h][:, (b % 4) * P:(b % 4) * P + P], hid[:, b * P:(b + 1) * P], c["ident"][:, :])
            a = A.copy(xs[:, s], ps[4 + h][:, :], after=[t_])
        T.after(a, pm)
        for d in range(KD):
            if d % 2 == 0:
                arrived(8 + d // 2)
            for j in range(2):
                m = T.mm(ps[6 + j][:, :], xs[:, d * P:(d + 1) * P],
                         ring[:, 8 + d // 2, (d % 2) * D + 512 * j:(d % 2) * D + 512 * j + 512], start=d == 0,
                         stop=d == KD - 1)
            if d % 2 and not last:
                load(e + 1, 8 + d // 2, after=[m])
        for h in range(2):
            a = A.copy(ys[:, 512 * h:512 * h + 512], ps[6 + h][:, :], after=[m])
        T.after(a)
        read = [None, None]
        for t in range(NT):
            T.after(read[t % 2])
            for h in range(2):
                m = T.mm(ps[2 * (t % 2) + h][:, :], PgT[:, t, :], ys[:, 512 * h:512 * h + 512])
            for h in range(2):
                s = slice(512 * h, 512 * h + 512)
                read[t % 2] = V.tt(Y[:, t, s], Y[:, t, s], ps[2 * (t % 2) + h][:, :], ALU.add, after=[m])

    with k.loop(NE - 1) as e:
        expert(e, False)
    expert(NE - 1, True)
    k.barrier()

    g, b = Pm[:, :, :].rearrange("p a b -> p (a b)"), Pg[:, :, :].rearrange("p a b -> p (a b)")
    k.dma("ffn_ln_in", g, io["ln_ffn_g_2"][layer].partition_broadcast(P))
    k.dma("ffn_ln_in", b, io["ln_ffn_b_2"][layer].partition_broadcast(P))
    with k.loop(NT) as t:
        a = A.act(tile[:, :], tile_of(Y, t), ACT.Copy, accum=st[:, 3:4])
        V.after(a)
        layer_norm_tile(k, st, tile[:, :], st[:, 3:4], g, b, tile_of(X, t), hid[:, :])
        if out is not None:
            k.dma("final_out", out[0, bass.ds(t * P, P), :], tile_of(X, t), after=[G])


_INS = ["x", "meta", "norm_g", "w_in", "w_out", "gla_g_up", "gla_g_b", "gla_norm_g", "rw_conv", "rw_w0", "rw_w_up",
        "rw_a0", "rw_a_up", "rw_k_k", "rw_k_a", "rw_r_k", "rw_ln_g", "rw_ln_b", "final_norm_g", "attn_w_qkv_2",
        "attn_w_o_2", "attn_sink_2", "lru_w_in_2", "lru_conv_w_2", "lru_conv_b_2", "lru_w_rgate_2", "lru_b_rgate_2",
        "lru_w_igate_2", "lru_b_igate_2", "lru_lambda_2", "lru_w_out_2", "moe_w_router_2", "moe_w_gate_up_2",
        "moe_w_down_2", "ln_mix_g_2", "ln_mix_b_2", "ln_ffn_g_2", "ln_ffn_b_2"]
_COLS = ["norm_g", "gla_g_b", "gla_norm_g", "rw_conv", "rw_w0", "rw_a0", "rw_k_k", "rw_k_a", "rw_r_k", "rw_ln_g",
         "rw_ln_b", "lru_conv_w_2", "lru_conv_b_2", "lru_b_rgate_2", "lru_b_igate_2", "lru_lambda_2"]


def phase(nc, k):
    @contextmanager
    def held():
        with ExitStack() as ctx:
            k.phases += 1
            yield lambda name, shape, dt, n=k.phases: ctx.enter_context(nc.sbuf_tensor(f"{name}_{n}", shape, dt))
            k.barrier()
    return held()


def program(nc, io, out, mix):
    with ExitStack() as ctx:
        k = Core(nc, ctx)
        ps = [ctx.enter_context(nc.psum_tensor(f"bank{i}", [P, 512], F32)) for i in range(8)]
        c = constants(k, lambda name, shape, dt: ctx.enter_context(nc.sbuf_tensor(name, shape, dt)))
        with phase(nc, k) as own:
            hnT = own("hnT", [P, KD, COLS], F32)
            for stage in (
                lambda sb: block_one_norm(k, c, ps, io, hnT, sb),
                lambda sb: attention_branch(k, c, ps, io, hnT, mix, sb),
                lambda sb: gla_branch(k, c, ps, io, hnT, mix, sb),
                lambda sb: rwkv_branch(k, c, ps, io, hnT, mix, sb),
            ):
                with phase(nc, k) as sb:
                    stage(sb)
        with phase(nc, k) as own:
            X = own("X", [P, NT, D], F32)
            for stage in (
                lambda sb: block_one_out(k, ps, io, mix, X, sb),
                lambda sb: windowed_attention(k, c, ps, io, X, mix, sb),
                lambda sb: mixer_out(k, ps, io, mix, 8, io["attn_w_o_2"][0], 0, X, sb),
                lambda sb: moe(k, c, ps, io, 0, X, None, sb),
                lambda sb: lru(k, c, ps, io, X, mix, sb),
                lambda sb: mixer_out(k, ps, io, mix, 8, io["lru_w_out_2"][0], 1, X, sb),
                lambda sb: moe(k, c, ps, io, 1, X, out, sb),
            ):
                with phase(nc, k) as sb:
                    stage(sb)


def rope_tables():
    rot = 16
    angle = np.arange(SEQ, dtype=np.float32) * (
        np.float32(500000.0) ** (-np.arange(0, rot, 2, dtype=np.float32) / rot))[:, None]
    cos, sin, turn = np.ones((P, SEQ), np.float32), np.zeros((P, SEQ), np.float32), np.zeros((P, P), np.float32)
    for h in (0, 64):
        for i in range(rot // 2):
            for at in (h + i, h + i + rot // 2):
                cos[at], sin[at] = np.cos(angle[i]), np.sin(angle[i])
            turn[h + i + rot // 2, h + i] = -1.0
            turn[h + i, h + i + rot // 2] = 1.0
    return {"rope_cos": cos, "rope_sin": sin, "rope_turn": turn}


def layouts(inputs):
    arrays = {name: np.ascontiguousarray(inputs[name]) for name in _INS}
    arrays.update(rope_tables())
    for name in _COLS:
        a = np.asarray(inputs[name])
        a = a.reshape(-1, a.shape[-1] // P, P)
        arrays[name + "_cols"] = np.ascontiguousarray(a.transpose(2, 0, 1).reshape(P, -1))
    arrays["rpb_padded"] = np.pad(np.ascontiguousarray(inputs["na_rpb"]).reshape(-1), RPB_PAD)
    return arrays


def kernel(**inputs):
    import concourse.bacc as _bacc
    from concourse.bass_utils import run_bass_kernel_spmd as _run

    nc = _bacc.Bacc("TRN2", target_bir_lowering=False, num_devices=1)
    arrays = layouts(inputs)
    io = {name: nc.dram_tensor(f"in_{name}", a.shape, mybir.dt.from_np(a.dtype), kind="ExternalInput").ap()
          for name, a in arrays.items()}
    out = nc.dram_tensor("out", (1, SEQ, D), F32, kind="ExternalOutput").ap()
    mix = nc.dram_tensor("mix", (12, P, SEQ), F32, kind="Internal").ap()
    program(nc, io, out, mix)
    return _run(nc, [{f"in_{name}": a for name, a in arrays.items()}], core_ids=[0]).results[0]["out"]
```

```python
from contextlib import ExitStack, contextmanager

import numpy as np

import concourse.bass as bass
from concourse import mybir

F32 = mybir.dt.float32
I32 = mybir.dt.int32
U32 = mybir.dt.uint32
ALU = mybir.AluOpType
ACT = mybir.ActivationFunctionType
AX = mybir.AxisListType
P = 128


class Count:

    def __init__(self, core, name, steady=False):
        self.sem = core.ctx.enter_context(core.nc.semaphore(name))
        self.n, self.core, self.steady = 0, core, steady
        if not steady:
            core.counts.append(self)

    def mark(self):
        return self, self.n, self.core.epoch


class Line(Count):

    def __init__(self, core, name, eng, chained):
        super().__init__(core, name)
        self.eng, self.chained, self.seen = eng, chained, {}

    def after(self, *marks):
        for m in marks:
            if m is None:
                continue
            c, n, epoch = m.mark() if isinstance(m, Count) else m
            if c.steady:
                self.eng.wait_ge(c.sem, n)
            elif epoch == self.core.epoch and n > self.seen.get(c, 0):
                self.eng.wait_ge(c.sem, n)
                self.seen[c] = n

    def start(self, marks):
        self.after(*marks)
        if self.chained:
            self.after(self)

    def done(self, ins):
        ins.then_inc(self.sem, 1)
        self.n += 1
        return self.mark()


class Elementwise(Line):

    def tt(self, out, a, b, op, after=()):
        self.start(after)
        return self.done(self.eng.tensor_tensor(out, a, b, op))

    def ts(self, out, a, s1, op0, s2=None, op1=None, after=()):
        self.start(after)
        if op1 is None:
            return self.done(self.eng.tensor_scalar(out, a, s1, None, op0))
        return self.done(self.eng.tensor_scalar(out, a, s1, s2, op0, op1))

    def stt(self, out, a, s, b, op0, op1, after=()):
        self.start(after)
        return self.done(self.eng.scalar_tensor_tensor(out, a, s, b, op0, op1))

    def copy(self, out, a, after=()):
        self.start(after)
        return self.done(self.eng.tensor_copy(out, a))

    def fill(self, out, value, after=()):
        self.start(after)
        return self.done(self.eng.memset(out, value))

    def recip(self, out, a, after=()):
        self.start(after)
        return self.done(self.eng.reciprocal(out, a))

    def reduce(self, out, a, op, after=()):
        self.start(after)
        return self.done(self.eng.tensor_reduce(out, a, AX.X, op))

    def scan(self, out, keep, add, after=()):
        self.start(after)
        return self.done(self.eng.tensor_tensor_scan(out, keep, add, 0.0, ALU.mult, ALU.add))


class Activations(Line):
    def act(self, out, a, func, bias=0.0, scale=1.0, accum=None, after=()):
        self.start(after)
        return self.done(self.eng.activation(out, a, func, bias=bias, scale=scale, accum_out=accum))

    def copy(self, out, a, after=()):
        return self.act(out, a, ACT.Copy, after=after)


class Products(Line):
    def mm(self, out, lhsT, rhs, start=True, stop=True, after=()):
        self.start(after)
        return self.done(self.eng.matmul(out, lhsT, rhs, start=start, stop=stop))

    def turn(self, out, a, ident, after=()):
        self.start(after)
        return self.done(self.eng.transpose(out, a, ident))


class Core:

    def __init__(self, nc, ctx):
        self.nc, self.ctx, self.counts, self.epoch = nc, ctx, [], 0
        self.V = Elementwise(self, "vector_done", nc.vector, True)
        self.G = Elementwise(self, "gpsimd_done", nc.gpsimd, True)
        self.A = Activations(self, "scalar_done", nc.scalar, True)
        self.T = Products(self, "tensor_done", nc.tensor, False)
        self.S = Line(self, "sync_done", nc.sync, False)
        self.lines = [self.V, self.G, self.A, self.T, self.S]
        self.loads, self.phases = {}, 0
        self.landed = [ctx.enter_context(nc.semaphore(f"slab_landed{i}")) for i in range(SLABS)]

    def dma(self, name, out, in_, after=(), line=None):
        line = line or self.S
        if name not in self.loads:
            self.loads[name] = Count(self, name)
        c = self.loads[name]
        line.after(*after)
        line.eng.dma_start(out, in_).then_inc(c.sem, 16)
        c.n += 16
        return c.mark()

    def barrier(self):
        self.S.after(*self.loads.values())
        self.nc.all_engine_barrier()
        used = [c for c in self.counts if c.n]
        for c in used:
            self.nc.sync.sem_clear(c.sem)
        self.nc.all_engine_barrier()
        self.epoch += 1
        for c in self.counts:
            c.n = 0
        for line in self.lines:
            line.seen = {}

    @contextmanager
    def loop(self, n):
        self.barrier()
        with self.nc.Fori(0, n) as i:
            yield i
            self.barrier()


def one(ap, i, dim=0):
    return ap[i] if dim == 0 else ap[:, i]


D = 1024
KD = D // P
SEQ = 1024
META = 16
CH = 64
X0 = CH
M0 = X0 - META
COLS = X0 + SEQ
NC = SEQ // CH
SPANS = [(M0, META), (X0, 512), (X0 + 512, 512)]
BW = 512
NA_COLS, GLA_COLS = 4 * BW, 3 * BW + 32
RW0 = NA_COLS + GLA_COLS
HALF = (slice(0, 64), slice(64, 128))
WIN_R, WIN_C = 8, 16
RPB_R, RPB_C = 2 * WIN_R - 1, 2 * WIN_C - 1
RPB_PAD = CH
NEG = -1e30
RB = 4


def constants(k, sb):
    G = k.G
    c = {}

    def mask(name, cols, conds):
        m = c[name] = sb(name, [P, cols], F32)
        G.fill(m[:, :], 1.0)
        for base, col, part in conds:
            G.start(())
            G.done(G.eng.affine_select(out=m[:, :], in_=m[:, :], compare_op=ALU.is_ge, fill=0.0, base=base,
                                       pattern=[[col, cols]], channel_multiplier=part))

    mask("ident", P, [(0, 1, -1), (0, -1, 1)])
    mask("ones", P, [])
    mask("before", P, [(-1, 1, -1)])
    mask("after", P, [(-1, -1, 1)])
    mask("upto", P, [(0, 1, -1)])
    mask("from", P, [(0, -1, 1)])
    for name, sign in (("upto64", 1), ("from64", -1)):
        m = c[name] = sb(name, [P, CH], F32)
        G.fill(m[:, :], 1.0)
        for h in HALF:
            G.start(())
            G.done(G.eng.affine_select(out=m[h, :], in_=m[h, :], compare_op=ALU.is_ge, fill=0.0, base=0,
                                       pattern=[[sign, CH]], channel_multiplier=-sign))
    m = c["halves"] = sb("halves", [P, P], F32)
    G.fill(m[:, :], 0.0)
    for h in HALF:
        G.fill(m[h, h], 1.0)
    return c


def rms_scale(k, st, x, rows, eps, dump, after=()):
    a = k.A.act(dump, x, ACT.Square, accum=st[0:rows, 0:1], after=after)
    k.V.ts(st[0:rows, 0:1], st[0:rows, 0:1], 1.0 / D, ALU.mult, eps, ALU.add, after=[a])
    a = k.A.act(st[0:rows, 0:1], st[0:rows, 0:1], ACT.Sqrt, after=[k.V])
    return k.V.recip(st[0:rows, 1:2], st[0:rows, 0:1], after=[a])


def block_one_norm(k, c, ps, io, hnT, sb):
    xt = sb("x_tile", [P, D], F32)
    dump = sb("squares", [P, D], F32)
    st = sb("norm_stats", [P, 2], F32)
    gcol = sb("norm_g_cols", [P, KD], F32)
    m = k.dma("norm_g_in", gcol[:, :], io["norm_g_cols"])
    k.G.fill(hnT[:, :, 0:M0], 0.0)

    def tile(src, rows, col):
        load = k.dma("x_in", xt[0:rows, :], src)
        r = rms_scale(k, st, xt[0:rows, :], rows, 1e-6, dump[0:rows, :], after=[load])
        k.V.ts(xt[0:rows, :], xt[0:rows, :], st[0:rows, 1:2], ALU.mult)
        k.T.after(k.V, k.G)
        for b in range(KD):
            t = k.T.turn(ps[b // 4][:, (b % 4) * P:(b % 4) * P + rows], xt[0:rows, b * P:(b + 1) * P],
                         c["ident"][0:rows, 0:rows])
        for half in range(2):
            src_ps = ps[half][:, 0:512].rearrange("p (b t) -> p b t", b=4)[:, :, 0:rows]
            g = gcol[:, 4 * half:4 * half + 4].unsqueeze(2).broadcast_to([P, 4, rows])
            k.V.tt(hnT[:, 4 * half:4 * half + 4, col], src_ps, g, ALU.mult, after=[t, m])

    tile(io["meta"], META, slice(M0, X0))
    with k.loop(SEQ // P) as i:
        tile(io["x"][0, bass.ds(i * P, P), :], P, bass.ds(i * P + X0, P))


class Projector:

    def __init__(self, k, ps, w_in, hnT, sb, ring):
        self.k, self.ps, self.hnT, self.ring, self.n = k, ps, hnT, ring, 0
        self.w = w_in[0].rearrange("(k p) c -> p k c", p=P)
        self.bufs = [sb(f"w_block{i}", [P, KD, P], F32) for i in range(ring)]
        self.used = [None] * ring
        self.evac = [None, None]
        self.side = 1
        self.loads = []

    def reset(self):
        self.used, self.evac, self.n, self.loads = [None] * self.ring, [None, None], 0, []

    def load(self, cols, width=P):
        b = self.n % self.ring
        self.n += 1
        mark = self.k.dma(f"w_in{b}", self.bufs[b][:, :, 0:width], self.w[:, :, cols], after=[self.used[b]])
        self.loads.append((b, mark, width))

    def part(self, half, cols):
        b = self.n % self.ring
        self.mark = self.k.dma(f"w_in{b}", self.bufs[b][:, :, half], self.w[:, :, cols], after=[self.used[b]])

    def whole(self):
        self.loads.append((self.n % self.ring, self.mark, P))
        self.n += 1

    def block(self, take, spans=SPANS):
        k = self.k
        b, mark, width = self.loads.pop(0)
        s = self.side = 1 - self.side
        k.T.after(mark, *(self.evac[s] or ()))
        marks = []
        for j, (col, n) in enumerate(spans):
            out = self.ps[3 * s + j][0:width, 0:n]
            for d in range(KD):
                m = k.T.mm(out, self.bufs[b][:, d, 0:width], self.hnT[:, d, col:col + n], start=d == 0, stop=d == KD - 1)
            marks.append(m)
        self.used[b] = m
        got = []
        for j, (col, n) in enumerate(spans):
            got += take(j, col, n, self.ps[3 * s + j][0:width, 0:n], marks[j])
        self.evac[s] = got


def silu_block(k, pr, out, tmp, off=X0):
    def take(j, col, n, z, m):
        s = slice(col - off, col - off + n)
        a = k.A.act(tmp[:, s], z, ACT.Sigmoid, after=[m, k.V])
        return [k.V.tt(out[:, s], z, tmp[:, s], ALU.mult, after=[a])]
    pr.block(take, SPANS[1:])


def copy_block(k, pr, out):
    def take(j, col, n, z, m):
        return [k.A.copy(out[0:z.shape[0], col:col + n], z, after=[m])]
    pr.block(take)


def attention_branch(k, c, ps, io, hnT, mix, sb):
    V, A, T, G = k.V, k.A, k.T, k.G
    NP = BW // P
    pr = Projector(k, ps, io["w_in"], hnT, sb, 4)
    qT = sb("na_q", [P, COLS], F32)
    kT = sb("na_k", [P, COLS], F32)
    vT = sb("na_v", [P, COLS], F32)
    gate = sb("na_gate", [P, SEQ], F32)
    vt = sb("na_v_tiles", [P, NC, P], F32)
    vm = sb("na_v_meta", [META, P], F32)
    bias = sb("na_bias", [P, BW // P * RPB_R, CH], F32)
    away = sb("na_outside", [P, CH], F32)
    lanes = [[sb(f"na_{n}{u}", shape, F32) for n, shape in (
        ("q_pair", [P, P]), ("scores", [P, 512 + META]), ("probs_T", [P, 5, P]), ("o", [P, P]), ("stats", [P, 4]))]
        for u in range(4)]
    oT = sb("na_oT", [P, SEQ], F32)
    for qbd, *_ in lanes:
        G.fill(qbd[:, :], 0.0)
    for h in HALF:
        G.fill(away[h, :], 0.0)
        for base, col, q in ((WIN_C // 2, 1, -1), (WIN_C // 2 - 1, -1, 1)):
            G.start(())
            G.done(G.eng.affine_select(out=away[h, :], in_=away[h, :], compare_op=ALU.is_ge, fill=NEG,
                                       base=base + (CH - 1) * q, pattern=[[col, CH]], channel_multiplier=-q))
    edge = sb("na_edge", [P, 2, CH], F32)
    for h in HALF:
        for e, (base, q) in enumerate(((WIN_C // 2 - 1, -1), (-(CH - WIN_C // 2), 1))):
            G.fill(edge[h, e, :], 1.0)
            G.start(())
            G.done(G.eng.affine_select(out=edge[h, e, :], in_=edge[h, e, :], compare_op=ALU.is_ge, fill=0.0,
                                       base=base + (CH - 1) * q, pattern=[[0, CH]], channel_multiplier=-q))
            G.start(())
            G.done(G.eng.affine_select(out=edge[h, e, :], in_=edge[h, e, :], compare_op=ALU.is_ge, fill=0.0,
                                       base=(WIN_C - 1) if e == 0 else -(CH - WIN_C),
                                       pattern=[[-1 if e == 0 else 1, CH]], channel_multiplier=0))
    G.tt(edge[:, 0, :], edge[:, 0, :], edge[:, 1, :], ALU.add)
    G.ts(edge[:, 0, :], edge[:, 0, :], -1.0, ALU.mult, 1.0, ALU.add)
    G.tt(away[:, :], away[:, :], edge[:, 0, :], ALU.mult)

    rpb = bass.AP(io["rpb_padded"].tensor, RPB_PAD + WIN_C - 1 - (CH - 1),
                  [[RPB_R * RPB_C, BW // 64], [1, CH], [RPB_C, RPB_R], [1, CH]])
    for h in range(2):
        for p in range(NP):
            m = k.dma("na_bias_in", bias[HALF[h], p * RPB_R:(p + 1) * RPB_R, :], rpb[2 * p + h])
    G.tt(bias[:, :, :], bias[:, :, :], away[:, :].unsqueeze(1).broadcast_to([P, NP * RPB_R, CH]), ALU.add, after=[m])
    with k.loop(NP) as p:
        pr.reset()
        for j in range(4):
            pr.load(bass.ds(p * P + j * BW, P))
        copy_block(k, pr, qT)
        copy_block(k, pr, kT)
        copy_block(k, pr, vT)
        silu_block(k, pr, gate, oT)
        T.after(A)
        for g in range(0, NC, 4):
            bank = ps[6 + (g // 4) % 2]
            T.after(A)
            for j in range(g, min(g + 4, NC - 1)):
                t = T.turn(bank[:, (j - g) * P:(j - g + 1) * P], vT[:, X0 + CH * j:X0 + CH * j + P], c["ident"][:, :])
            n = min(4, NC - 1 - g)
            A.copy(vt[:, g:g + n, :], bank[:, 0:n * P].rearrange("p (j f) -> p j f", f=P), after=[t])
        t = T.turn(ps[6][0:META, 0:P], vT[:, M0:X0], c["ident"][:, :], after=[A])
        A.copy(vm[:, :], ps[6][0:META, 0:P], after=[t])

        def grid_row(u, r, first, dr0):
            qbd, s_sb, pT, o_sb, st = lanes[u]
            K, R = ps[2 * u], ps[2 * u + 1]
            qs = bass.ds(r * CH + X0, CH)
            for h in HALF:
                m = A.copy(qbd[h, h][:, ::-1], qT[h, qs])
            T.mm(K[:, :], qbd[:, :], kT[:, bass.ds(first * CH + X0, 512)], after=[m])
            t = T.mm(R[:, 0:META], qbd[:, :], kT[:, M0:X0])
            yield
            scale = CH ** -0.5
            V.stt(s_sb[:, 0:512].rearrange("p (r c) -> p r c", c=CH), K[:, :].rearrange("p (r c) -> p r c", c=CH),
                  scale, bias[:, bass.ds(p * RPB_R + dr0, WIN_R), :], ALU.mult, ALU.add, after=[t, G])
            V.ts(s_sb[:, 512:], R[:, 0:META], scale, ALU.mult)
            V.reduce(st[:, 0:1], s_sb[:, :], ALU.max)
            v = V.ts(st[:, 1:2], st[:, 0:1], -1.0, ALU.mult)
            a = A.act(s_sb[:, :], s_sb[:, :], ACT.Exp, bias=st[:, 1:2], accum=st[:, 2:3], after=[v])
            yield
            for j in range(4):
                t = T.turn(K[:, j * P:(j + 1) * P], s_sb[:, j * P:(j + 1) * P], c["ident"][:, :], after=[a])
            tm = T.turn(R[0:META, 0:P], s_sb[:, 512:512 + META], c["ident"][:, :])
            m1 = A.copy(pT[:, 0:4, :], K[:, :].rearrange("p (j q) -> p j q", q=P), after=[t])
            m2 = V.copy(pT[0:META, 4, :], R[0:META, 0:P], after=[tm])
            V.recip(st[:, 3:4], st[:, 2:3])
            yield
            T.after(m1, m2)
            for j in range(4):
                T.mm(R[:, P:2 * P], pT[:, j, :], one(vt, first + 2 * j, 1), start=j == 0, stop=False)
            t = T.mm(R[:, P:2 * P], pT[0:META, 4, :], vm[:, :], start=False)
            v = V.ts(o_sb[:, :], R[:, P:2 * P], st[:, 3:4], ALU.mult, after=[t])
            yield
            t = T.turn(R[:, 2 * P:3 * P], o_sb[:, :], c["ident"][:, :], after=[v])
            os = bass.ds(r * CH, CH)
            for h in HALF:
                v = V.tt(oT[h, os], R[h, 2 * P + h.start:2 * P + h.stop][:, ::-1], gate[h, os], ALU.mult, after=[t])
            T.after(v)
            yield

        for line in (A, V, T):
            line.after(A, V)
        both(*[grid_row(u, u, 0, 7 - u) for u in range(4)])
        both(*[grid_row(u, u + NC - 4, NC - 8, 3 - u) for u in range(4)])
        with k.loop((NC - 8) // 4) as i:
            both(*[grid_row(u, i * 4 + (u + 4), i * 4 + u, 3) for u in range(4)])
        k.dma("mix_out", one(mix, p), oT[:, :])


def keep_masks(k, sb):
    keep = sb("keep", [P, 2, COLS], F32)
    k.G.fill(keep[:, :, :], 1.0)
    for d, at in ((0, 0), (1, CH - 1)):
        m = k.G.fill(keep[:, d, :].rearrange("p (c t) -> p c t", t=CH)[:, :, at:at + 1], 0.0)
    return keep, m


def chunk_sums(k, out, x, keep, d, after=()):
    V = k.V
    if d == 0:
        return V.scan(out[:, :], keep[:, 0, :], x[:, :], after=after)
    V.scan(out[:, 0:X0], keep[:, 0, 0:X0], x[:, 0:X0], after=after)
    back = slice(COLS - 1, X0 - 1, -1)
    return V.scan(out[:, back], keep[:, 1, back], x[:, back])


def chunk_ends(k, out, e, d):
    v = e[:, :].rearrange("p (c t) -> p c t", t=CH)
    if d == 0:
        return k.V.copy(out[:, :], v[:, :, CH - 1])
    k.V.copy(out[:, 0:1], v[:, 0:1, CH - 1])
    return k.V.copy(out[:, 1:], v[:, 1:, 0])


def both(*steps):
    steps = list(steps)
    while steps:
        for s in list(steps):
            if next(s, StopIteration) is StopIteration:
                steps.remove(s)


def spread(line, pair, src, n, after=()):
    for h in HALF:
        m = line.copy(pair[h, 0:n, h], src[h, :].rearrange("p (c t) -> p c t", t=CH), after=after)
    return m


def gla_branch(k, c, ps, io, hnT, mix, sb):
    V, A, T, G = k.V, k.A, k.T, k.G
    pr = Projector(k, ps, io["w_in"], hnT, sb, 4)
    keep, _ = keep_masks(k, sb)
    q = sb("gla_q", [P, COLS], F32)
    kk = sb("gla_k", [P, COLS], F32)
    vT = sb("gla_v", [P, NC + 1, 2, CH], F32)
    gd = [sb(f"gla_gd{d}", [META, COLS], F32) for d in range(2)]
    up = sb("gla_up", [16, 2, 2 * P], F32)
    upb = sb("gla_up_bias", [P, 2, 2], F32)
    upp = sb("gla_up_pair", [16, 2, P], F32)
    ng = sb("gla_norm", [P, 1], F32)
    gate = sb("gla_gate", [P, 2, SEQ], F32)
    o = sb("gla_out", [P, 2, SEQ], F32)
    lw = sb("gla_log_decay", [P, COLS], F32)
    cum = sb("gla_sums", [P, COLS], F32)
    tmp = sb("gla_tmp", [P, COLS], F32)
    qe = [sb(f"gla_qe{d}", [P, COLS], F32) for d in range(2)]
    ke = [sb(f"gla_ke{d}", [P, COLS], F32) for d in range(2)]
    dec = [sb(f"gla_dec{d}", [P, NC + 1], F32) for d in range(2)]
    small = [{n: sb(f"gla_{n}{d}", [P, RB, P], F32) for n in ("q2", "k2", "vc", "kt", "vt", "at", "ds")}
             for d in range(2)]
    state = [sb(f"gla_state{d}", [P, RB + 1, P], F32) for d in range(2)]
    for d in range(2):
        for n in ("q2", "k2"):
            G.fill(small[d][n][:, :, :], 0.0)
    for t in (q, kk, lw):
        G.fill(t[:, 0:M0], 0.0)
    G.fill(vT[:, 0, :, 0:M0], 0.0)
    k.dma("gla_small_in", up[:, :, :], io["gla_g_up"][0].rearrange("d r c -> r d c"))
    k.dma("gla_small_in", upb[:, :, :], io["gla_g_b_cols"].rearrange("p (d b) -> p d b", d=2))
    k.dma("gla_small_in", ng[:, :], io["gla_norm_g_cols"])
    base = NA_COLS
    for d in range(2):
        pr.load(slice(base + 3 * BW + 16 * d, base + 3 * BW + 16 * d + 16), 16)
    for d in range(2):
        copy_block(k, pr, gd[d])

    def chunks(d, n, first, seq, order):
        w, S = small[d], state[d]
        K = ps[4 * d:4 * d + 4]
        cols = bass.ds(first * CH, n * CH)
        a = A.copy(w["vc"][:, 0:n, :].rearrange("p c (h t) -> p c h t", t=CH), vT[:, bass.ds(first, n), :, :])
        g1 = spread(G, w["q2"], qe[d][:, cols], n)
        g2 = spread(G, w["k2"], ke[d][:, cols], n)
        yield
        T.after(a, g1, g2)
        for j in range(n):
            js = slice(j * P, j * P + P)
            T.mm(K[0][:, js], w["k2"][:, j, :], w["q2"][:, j, :])
            T.turn(K[1][:, js], w["k2"][:, j, :], c["ident"][:, :])
            t = T.turn(K[2][:, js], w["vc"][:, j, :], c["ident"][:, :])
        v3 = lambda b: K[b][:, 0:n * P].rearrange("p (c t) -> p c t", t=P)
        forwards = d == 0 or not seq
        mask = c["upto" if forwards else "from"][:, :].unsqueeze(1).broadcast_to([P, n, P])
        v1 = V.tt(w["at"][:, 0:n, :], v3(0), mask, ALU.mult, after=[t])
        a1 = A.copy(w["kt"][:, 0:n, :], v3(1), after=[t])
        a2 = A.copy(w["vt"][:, 0:n, :], v3(2))
        yield
        T.after(v1, a1, a2)
        for j in range(n):
            t = T.mm(K[1][:, j * P:j * P + P], w["kt"][:, j, :], w["vt"][:, j, :])
        V.tt(w["ds"][:, 0:n, :], v3(1), dec[d][:, bass.ds(first, n)].unsqueeze(2).broadcast_to([P, n, P]), ALU.mult,
             after=[t])
        for i, j in enumerate(order):
            m = V.stt(S[:, i + 1, :], S[:, i, :], dec[d][:, bass.ds(first + j, 1)], w["ds"][:, j, :], ALU.mult, ALU.add)
        yield
        if seq:
            T.after(m)
            for i, j in enumerate(order):
                js = slice(j * P, j * P + P)
                T.mm(K[0][:, js], w["vt"][:, j, :], w["at"][:, j, :], stop=False)
                t = T.mm(K[0][:, js], S[:, i, :], w["q2"][:, j, :], start=False)
            ov = o[:, :, bass.ds(first * CH - X0, n * CH)].rearrange("p h (c t) -> p c h t", t=CH)
            V.tt(ov, K[0][:, 0:n * P].rearrange("p (c h t) -> p c h t", h=2, t=CH), ov, ALU.add, after=[t])
        V.copy(S[:, 0, :], S[:, n, :])
        yield

    with k.loop(2) as p:
        pr.reset()
        for cols in (bass.ds(p * P + base, P), bass.ds(p * P + base + 256, P),
                     bass.ds(p * 256 + base + BW, P), bass.ds(p * 256 + base + BW + P, P),
                     bass.ds(p * 256 + base + 2 * BW, P), bass.ds(p * 256 + base + 2 * BW + P, P)):
            pr.load(cols)
            if pr.n == 4:
                copy_block(k, pr, q)
                copy_block(k, pr, kk)
        for h in range(2):
            def take(j, col, n, z, m, h=h):
                dst = vT[:, :, :, :].rearrange("p c h t -> p h c t")[:, h]
                if n < CH:
                    return [A.copy(dst[:, 0, M0:X0], z, after=[m])]
                return [A.copy(dst[:, col // CH:(col + n) // CH, :], z.rearrange("p (c t) -> p c t", t=CH), after=[m])]
            pr.block(take)
        for h in range(2):
            silu_block(k, pr, gate[:, h, :], tmp)
        A.copy(upp[:, :, :], up[:, :, bass.ds(p * P, P)])
        for d in range(2):
            for j, (col, n) in enumerate(SPANS):
                s = slice(col, col + n)
                t = T.mm(ps[6][:, 0:n], upp[:, d, :], gd[d][:, s],
                         after=[A, V, G])
                V.ts(lw[:, s], ps[6][:, 0:n], upb[:, d, bass.ds(p, 1)], ALU.add, after=[t])
            s = slice(M0, COLS)
            V.stt(tmp[:, s], lw[:, s], -1.0, lw[:, s], ALU.mult, ALU.min)
            A.act(tmp[:, s], tmp[:, s], ACT.Exp, after=[V])
            a = A.act(tmp[:, s], tmp[:, s], ACT.Ln, bias=1.0)
            V.stt(lw[:, s], lw[:, s], 0.0, tmp[:, s], ALU.min, ALU.subtract, after=[a])
            V.ts(lw[:, s], lw[:, s], 1.0 / 16.0, ALU.mult)
            v = chunk_sums(k, cum, lw, keep, d)
            a = A.act(tmp[:, :], cum[:, :], ACT.Exp, after=[v])
            V.stt(qe[d][:, :], q[:, :], CH ** -0.5, tmp[:, :], ALU.mult, ALU.mult, after=[a])
            v = chunk_ends(k, dec[d], tmp, d)
            a = A.act(tmp[:, :], cum[:, :], ACT.Exp, scale=-1.0, after=[v])
            V.tt(ke[d][:, :], kk[:, :], tmp[:, :], ALU.mult, after=[a])
            G.fill(state[d][:, 0, :], 0.0)
        G.fill(o[:, :, :], 0.0)
        A.after(V)
        G.after(V)
        V.after(G)
        both(*[chunks(d, 1, 0, False, [0]) for d in range(2)])
        with k.loop(NC // RB) as i:
            both(chunks(0, RB, i * RB + 1, True, range(RB)),
                 chunks(1, RB, (NC - RB + 1) - i * RB, True, range(RB)[::-1]))
        for h in range(2):
            for s in (slice(0, 512), slice(512, 1024)):
                a = A.act(tmp[:, s], o[:, h, s], ACT.Square, after=[V])
                t = T.mm(ps[0][:, :], c["ones"][:, :], tmp[:, s], after=[a])
                V.ts(tmp[:, s], ps[0][:, :], 1.0 / P, ALU.mult, 1e-5, ALU.add, after=[t])
                a = A.act(tmp[:, s], tmp[:, s], ACT.Sqrt, after=[V])
                V.recip(tmp[:, s], tmp[:, s], after=[a])
                V.tt(tmp[:, s], tmp[:, s], gate[:, h, s], ALU.mult)
                V.stt(o[:, h, s], o[:, h, s], ng[:, 0:1], tmp[:, s], ALU.mult, ALU.mult)
            k.dma("mix_out", one(mix, 2 * p + 4 + h), o[:, h, :], after=[V])


DECAY = float(np.exp(-0.5))


def rwkv_branch(k, c, ps, io, hnT, mix, sb):
    V, A, T, G = k.V, k.A, k.T, k.G
    pr = Projector(k, ps, io["w_in"], hnT, sb, 3)
    keep, _ = keep_masks(k, sb)
    full = lambda name, n=COLS: sb("rw_" + name, [P, n], F32)
    raw = full("raw", COLS + 2)
    r, kx, v, kk = full("r"), full("k"), full("v"), full("kk")
    twd, ad = full("decay_in"), full("alpha_in")
    kt, bt, at, rt = ([full(f"{n}{d}") for d in range(2)] for n in ("kt", "bt", "at", "rt"))
    tA = full("tmp_a")
    tB = raw[:, 1:1 + COLS]
    gate = full("gate", SEQ)
    bonus = full("bonus", SEQ)
    y = kx
    conv = sb("rw_conv_cols", [P, 3, 14], F32)
    wup = sb("rw_w_up", [P, BW], F32)
    aup = sb("rw_a_up", [P, BW], F32)
    up2 = sb("rw_up_pair", [P, 2, P], F32)
    w0 = sb("rw_w0c", [P, 2, 4], F32)
    a0 = sb("rw_a0c", [P, 2, 4], F32)
    vec = {n: sb(f"rw_{n}c", [P, 4], F32) for n in ("k_k", "k_a", "one_k_a", "r_k", "ln_g", "ln_b")}
    dec = [sb(f"rw_dec{d}", [P, NC + 1], F32) for d in range(2)]
    names = ("a2", "b2", "k2", "v2", "P0", "PT0", "P1", "PT1", "TT", "AK", "RQ", "aT", "bT", "kT", "vT", "QY")
    small = [{n: sb(f"rw_{n}_{d}", [P, RB, P], F32) for n in names} for d in range(2)]
    state = [sb(f"rw_state{d}", [P, P], F32) for d in range(2)]

    for d in range(2):
        for n in ("a2", "b2", "k2", "v2"):
            G.fill(small[d][n][:, :, :], 0.0)
    for t in (r, kk, v, tA, *kt, *bt, *at, *rt):
        G.fill(t[:, 0:M0], 0.0)
    G.fill(raw[:, :], 0.0)
    for name, t in (("rw_conv", conv), ("rw_w0", w0), ("rw_a0", a0)):
        k.dma("rw_small_in", t[:, :, :].rearrange("p a b -> p (a b)"), io[name + "_cols"])
    for n, t in vec.items():
        if n != "one_k_a":
            k.dma("rw_small_in", t[:, :], io[f"rw_{n}_cols"])
    k.dma("rw_small_in", wup[:, :], io["rw_w_up"][0].rearrange("d r c -> (d r) c"))
    small_in = k.dma("rw_small_in", aup[:, :], io["rw_a_up"][0].rearrange("d r c -> (d r) c"))
    V.ts(vec["one_k_a"][:, :], vec["k_a"][:, :], -1.0, ALU.mult, 1.0, ALU.add, after=[small_in, G])
    V.ts(vec["r_k"][:, :], vec["r_k"][:, :], 0.5, ALU.mult)
    A.after(V, G)
    T.after(V)

    def conv_block(out, blk):
        def take(j, col, n, z, m):
            return [A.copy(raw[:, 1 + col:1 + col + n], z, after=[m, V])]
        pr.block(take)
        s = slice(M0, COLS)
        tap = lambda i: conv[:, i, blk]
        V.ts(out[:, s], raw[:, 1 + M0:1 + COLS], tap(1), ALU.mult, after=[A, G])
        V.stt(out[:, s], raw[:, M0:COLS], tap(0), out[:, s], ALU.mult, ALU.add)
        V.stt(out[:, s], raw[:, 2 + M0:2 + COLS], tap(2), out[:, s], ALU.mult, ALU.add)

    for j in range(2):
        pr.load(slice(RW0 + 3 * BW + P * j, RW0 + 3 * BW + P * j + P))
    conv_block(twd, slice(12, 13))
    conv_block(ad, slice(13, 14))
    s0 = slice(M0, COLS)
    e = A.act(twd[:, s0], twd[:, s0], ACT.Tanh, after=[V])

    def chunks(d, n, first, seq, order):
        w, S = small[d], state[d]
        K = ps[4 * d:4 * d + 4]
        cols = bass.ds(first * CH, n * CH)
        v3 = lambda b: K[b][:, 0:n * P].rearrange("p (c t) -> p c t", t=P)
        v4 = lambda b: K[b][:, 0:n * P].rearrange("p (c x t) -> p c x t", x=2, t=CH)
        g = spread(G, w["k2"], kt[d][:, cols], n)
        g = spread(G, w["v2"], v[:, cols], n)
        a = spread(A, w["b2"], bt[d][:, cols], n)
        m = spread(V, w["a2"], at[d][:, cols], n)
        rs = A.copy(w["QY"][:, 0:n, 0:CH], rt[d][:, cols].rearrange("p (c t) -> p c t", t=CH))
        yield
        T.after(g, rs, m)
        for j in range(n):
            js = slice(j * P, j * P + P)
            T.mm(K[0][:, js], w["b2"][:, j, :], w["a2"][:, j, :])
            T.mm(K[1][:, js], w["a2"][:, j, :], w["b2"][:, j, :])
            T.mm(K[2][:, js], w["k2"][:, j, :], w["a2"][:, j, :])
            T.mm(K[3][:, j * P:j * P + CH], w["b2"][:, j, :], w["QY"][:, j, 0:CH])
            t = T.mm(K[3][:, j * P + CH:j * P + P], w["k2"][:, j, :], w["QY"][:, j, 0:CH])
        forwards = d == 0 or not seq
        less, more, upto = ("before", "after", "upto64") if forwards else ("after", "before", "from64")
        wide = lambda name: c[name][:, :].unsqueeze(1).broadcast_to([P, n, P])
        f1 = V.tt(w["PT0"][:, 0:n, :], v3(0), wide(less), ALU.mult, after=[t])
        f2 = V.tt(w["P0"][:, 0:n, :], v3(1), wide(more), ALU.mult)
        gt = G.tt(w["TT"][:, 0:n, :], w["PT0"][:, 0:n, :], wide("ident"), ALU.add, after=[f1])
        V.tt(w["AK"][:, 0:n, :], v3(2), wide(less), ALU.mult)
        for x in range(2):
            f3 = V.tt(w["RQ"][:, 0:n, x * CH:x * CH + CH], v4(3)[:, :, x, :],
                      c[upto][:, :].unsqueeze(1).broadcast_to([P, n, CH]), ALU.mult)
        yield
        T.after(f3)
        for b, (src, dst) in enumerate((("a2", "aT"), ("b2", "bT"), ("k2", "kT"), ("v2", "vT"))):
            for j in range(n):
                t = T.turn(K[b][:, j * P:j * P + P], w[src][:, j, :], c["ident"][:, :])
        for b, dst in enumerate(("aT", "bT", "kT", "vT")):
            a = A.copy(w[dst][:, 0:n, :], v3(b), after=[t])
        yield
        T.after(a, gt)
        x, xt = "P0", "PT0"
        for i in range(5):
            nx, nxt = ("P1", "PT1") if i % 2 == 0 else ("P0", "PT0")
            for j in range(n):
                js = slice(j * P, j * P + P)
                t = T.mm(K[0][:, js], w[xt][:, j, :], w[x][:, j, :])
            f = V.copy(w[nx][:, 0:n, :], v3(0), after=[t])
            if i < 4:
                for j in range(n):
                    t = T.mm(K[1][:, j * P:j * P + P], w[x][:, j, :], w[xt][:, j, :])
                a = A.copy(w[nxt][:, 0:n, :], v3(1), after=[t])
            yield
            T.after(f)
            for j in range(n):
                t = T.mm(K[2][:, j * P:j * P + P], w[nx][:, j, :], w["TT"][:, j, :])
            f = V.tt(w["TT"][:, 0:n, :], v3(2), w["TT"][:, 0:n, :], ALU.add, after=[t])
            T.after(a)
            x, xt = nx, nxt
            yield
        for j in range(n):
            t = T.mm(K[3][:, j * P:j * P + P], w["AK"][:, j, :], w["vT"][:, j, :])
        a = A.copy(w["P0"][:, 0:n, :], v3(3), after=[t])
        yield
        T.after(f, a)
        for j in range(n):
            js = slice(j * P, j * P + P)
            T.mm(K[0][:, js], w["TT"][:, j, :], w["aT"][:, j, :])
            t = T.mm(K[1][:, js], w["TT"][:, j, :], w["P0"][:, j, :])
        a = A.copy(w["PT0"][:, 0:n, :], v3(0), after=[t])
        f = V.copy(w["PT1"][:, 0:n, :], v3(1), after=[t])
        yield
        T.after(a, f)
        for j in range(n):
            js = slice(j * P, j * P + P)
            T.mm(K[0][:, js], w["PT0"][:, j, :], w["bT"][:, j, :])
            T.mm(K[1][:, js], w["kT"][:, j, :], w["vT"][:, j, :], stop=False)
            T.mm(K[1][:, js], w["bT"][:, j, :], w["PT1"][:, j, :], start=False)
            q, yy = slice(j * P, j * P + CH), slice(j * P + CH, j * P + P)
            T.mm(K[2][:, q], w["PT0"][:, j, :], w["RQ"][:, j, 0:CH])
            T.mm(K[2][:, yy], w["vT"][:, j, :], w["RQ"][:, j, CH:], stop=False)
            t = T.mm(K[2][:, yy], w["PT1"][:, j, :], w["RQ"][:, j, 0:CH], start=False)
        V.tt(w["P1"][:, 0:n, :], v3(0), wide("ident"), ALU.add, after=[t])
        V.tt(w["a2"][:, 0:n, :], v3(1), dec[d][:, bass.ds(first, n)].unsqueeze(2).broadcast_to([P, n, P]), ALU.mult)
        f = V.tt(w["QY"][:, 0:n, 0:CH], v4(2)[:, :, 0, :], w["QY"][:, 0:n, 0:CH], ALU.add)
        yv = None
        if seq:
            yv = y[:, bass.ds(first * CH - X0, n * CH)].rearrange("p (c t) -> p c t", t=CH)
            f = V.tt(w["QY"][:, 0:n, CH:], v4(2)[:, :, 1, :], yv, ALU.add)
        yield
        for j in order:
            T.after(f)
            if seq:
                T.mm(K[3][:, 0:CH], S[:, :], w["QY"][:, j, 0:CH])
            t = T.mm(K[3][:, P:2 * P], w["P1"][:, j, :], S[:, :])
            f = V.stt(S[:, :], K[3][:, P:2 * P], dec[d][:, bass.ds(first + j, 1)], w["a2"][:, j, :], ALU.mult, ALU.add,
                      after=[t])
            if seq:
                f = V.tt(y[:, bass.ds((first + j) * CH - X0, CH)], K[3][:, 0:CH], w["QY"][:, j, CH:], ALU.add)
            yield

    blocks = SEQ // 512
    with k.loop(4) as p:
        pr.reset()
        for j in range(3):
            pr.load(bass.ds(p * P + RW0 + j * BW, P))
        for j, out in enumerate((r, kx, v)):
            conv_block(out, bass.ds(p + 4 * j, 1))
            if j == 0:
                pr.load(bass.ds(p * P + RW0 + 3 * BW + 2 * P, P))
        silu_block(k, pr, gate, tA)
        A.copy(up2[:, 0, :], wup[:, bass.ds(p * P, P)])
        A.copy(up2[:, 1, :], aup[:, bass.ds(p * P, P)])
        one_col = lambda t: t[:, bass.ds(p, 1)]

        def group_sum(x, s, after):
            return T.mm(ps[7][:, 0:s.stop - s.start], c["halves"][:, :], x[:, s], after=after)

        V.ts(kk[:, s0], kx[:, s0], one_col(vec["k_k"]), ALU.mult)
        a = A.act(tB[:, s0], kk[:, s0], ACT.Square, after=[V])
        for col, n in SPANS:
            s = slice(col, col + n)
            t = group_sum(tB, s, [a, V])
            a2 = A.act(tA[:, s], ps[7][:, 0:n], ACT.Sqrt, after=[t])
            V.ts(tA[:, s], tA[:, s], 1e-12, ALU.max, after=[a2])
            V.recip(tA[:, s], tA[:, s])
            V.tt(kk[:, s], kk[:, s], tA[:, s], ALU.mult)
        for d in range(2):
            def lora(x, which, bias, out):
                for col, n in SPANS:
                    s = slice(col, col + n)
                    t = T.mm(ps[6][:, 0:n], up2[HALF[d], which, :], x[HALF[d], s], after=[A])
                    a = A.act(out[:, s], ps[6][:, 0:n], ACT.Sigmoid, bias=bias[:, d, bass.ds(p, 1)], after=[t, V])
                V.after(a)
            lora(ad, 1, a0, tA)
            V.tt(bt[d][:, s0], kk[:, s0], tA[:, s0], ALU.mult)
            V.ts(tA[:, s0], tA[:, s0], one_col(vec["k_a"]), ALU.mult, one_col(vec["one_k_a"]), ALU.add)
            V.tt(kt[d][:, s0], kx[:, s0], tA[:, s0], ALU.mult)
            lora(twd, 0, w0, tA)
            V.ts(tA[:, s0], tA[:, s0], -DECAY, ALU.mult)
            G.fill(tA[:, 0:M0], 0.0, after=[V])
            f = chunk_sums(k, tB, tA, keep, d, after=[G])
            if d == 0:
                V.copy(bonus[:, :], kt[0][:, X0:])
            else:
                V.tt(bonus[:, :], bonus[:, :], kt[1][:, X0:], ALU.add)
            V.tt(tA[:, :], tB[:, :], tA[:, :], ALU.subtract)
            a = A.act(tA[:, :], tA[:, :], ACT.Exp, after=[V])
            V.stt(at[d][:, s0], kk[:, s0], -1.0, tA[:, s0], ALU.mult, ALU.mult, after=[a])
            a = A.act(tA[:, :], tB[:, :], ACT.Exp, after=[V])
            V.tt(rt[d][:, s0], r[:, s0], tA[:, s0], ALU.mult, after=[a])
            chunk_ends(k, dec[d], tA, d)
            a = A.act(tA[:, :], tB[:, :], ACT.Exp, scale=-1.0, after=[V])
            V.tt(kt[d][:, s0], kt[d][:, s0], tA[:, s0], ALU.mult, after=[a])
            V.tt(bt[d][:, s0], bt[d][:, s0], tA[:, s0], ALU.mult)
            G.fill(state[d][:, :], 0.0)
        V.tt(bonus[:, :], bonus[:, :], r[:, X0:], ALU.mult)
        V.ts(bonus[:, :], bonus[:, :], one_col(vec["r_k"]), ALU.mult)
        for i in range(blocks):
            s = slice(512 * i, 512 * i + 512)
            t = group_sum(bonus, s, [V])
            V.tt(bonus[:, s], ps[7][:, :], v[:, X0 + 512 * i:X0 + 512 * i + 512], ALU.mult, after=[t])
        G.fill(y[:, 0:SEQ], 0.0, after=[V])
        A.after(V)
        V.after(G)
        both(*[chunks(d, 1, 0, False, [0]) for d in range(2)])
        with k.loop(NC // RB) as i:
            both(chunks(0, RB, i * RB + 1, True, range(RB)),
                 chunks(1, RB, (NC - RB + 1) - i * RB, True, range(RB)[::-1]))
        for i in range(blocks):
            s = slice(512 * i, 512 * i + 512)
            t = group_sum(y, s, [V])
            V.stt(y[:, s], ps[7][:, :], -1.0 / CH, y[:, s], ALU.mult, ALU.add, after=[t])
            a = A.act(tA[:, s], y[:, s], ACT.Square, after=[V])
            t = group_sum(tA, s, [a])
            V.ts(tA[:, s], ps[7][:, :], 1.0 / CH, ALU.mult, 64e-5, ALU.add, after=[t])
            a = A.act(tA[:, s], tA[:, s], ACT.Sqrt, after=[V])
            V.recip(tA[:, s], tA[:, s], after=[a])
            V.stt(y[:, s], y[:, s], one_col(vec["ln_g"]), tA[:, s], ALU.mult, ALU.mult)
            V.stt(y[:, s], y[:, s], one_col(vec["ln_b"]), bonus[:, s], ALU.add, ALU.add)
            V.tt(y[:, s], y[:, s], gate[:, s], ALU.mult)
        k.dma("mix_out", one(mix, p + 8), y[:, 0:SEQ], after=[V])


NT = SEQ // P
ALPHA = 4 ** 0.25
LN_EPS = 1e-5


def row_in(k, name, t, src):
    return k.dma(name, t[:, :], src.partition_broadcast(P))


def layer_norm_tile(k, st, y, total, g, b, out, dump):
    V, A, G = k.V, k.A, k.G
    v = V.ts(st[:, 0:1], total, -1.0 / D, ALU.mult)
    a = A.act(dump, y, ACT.Square, bias=st[:, 0:1], accum=st[:, 1:2], after=[v])
    yield
    V.ts(st[:, 1:2], st[:, 1:2], 1.0 / D, ALU.mult, LN_EPS, ALU.add, after=[a])
    a = A.act(st[:, 1:2], st[:, 1:2], ACT.Sqrt, after=[V])
    yield
    V.recip(st[:, 2:3], st[:, 1:2], after=[a])
    V.ts(y, y, st[:, 0:1], ALU.add, st[:, 2:3], ALU.mult)
    v = V.tt(y, y, g, ALU.mult)
    G.tt(out, y, b, ALU.add, after=[v])


def out_project(k, ps, sb, src, blocks, w, finish):
    A, T = k.A, k.T
    wt = sb("out_w", [P, blocks, D], F32)
    xt = [sb(f"out_in{i}", [P, blocks, P], F32) for i in range(2)]
    wv = w.rearrange("(b p) n -> p b n", p=P)
    for b in range(0, blocks, 4):
        k.dma("out_w_in", wt[:, b:b + 4, :], wv[:, b:b + 4, :])
    with k.loop(NT // 2) as i:
        marks = [k.dma(f"out_in{u}", xt[u][:, :, :],
                       src[0:blocks, :, bass.ds((2 * i + u) * P, P)].rearrange("b p t -> p b t")) for u in range(2)]
        for u in range(2):
            T.after(marks[u])
            for h in range(2):
                for b in range(blocks):
                    t = T.mm(ps[2 * u + h][:, :], xt[u][:, b, :], wt[:, b, 512 * h:512 * h + 512],
                             start=b == 0, stop=b == blocks - 1)
            finish(2 * i + u, ps[2 * u:2 * u + 2], t)


def tile_of(X, t):
    return one(X, t, 1)


def block_one_out(k, ps, io, mix, X, sb):
    V, A = k.V, k.A
    y = sb("h_tile", [P, D], F32)
    xin = sb("h_in", [P, D], F32)
    dump = sb("squares", [P, D], F32)
    g = sb("final_g", [P, D], F32)
    st = sb("out_stats", [P, 2], F32)
    row_in(k, "final_g_in", g, io["final_norm_g"])

    def finish(t, banks, m):
        x = k.dma("h_in", xin[:, :], io["x"][0, bass.ds(t * P, P), :], after=[V])
        for h in range(2):
            s = slice(512 * h, 512 * h + 512)
            V.tt(y[:, s], banks[h][:, :], xin[:, s], ALU.add, after=[m, x, A])
        rms_scale(k, st, y[:, :], P, 1e-6, dump[:, :], after=[V])
        V.stt(tile_of(X, t), y[:, :], st[:, 1:2], g[:, :], ALU.mult, ALU.mult)

    out_project(k, ps, sb, mix, 12, io["w_out"][0], finish)


def mixer_out(k, ps, io, mix, blocks, w, layer, X, sb):
    V, A, G = k.V, k.A, k.G
    y = sb("y_tile", [P, D], F32)
    dump = sb("squares", [P, D], F32)
    g, b = sb("ln_g", [P, D], F32), sb("ln_b", [P, D], F32)
    st = sb("ln_stats", [P, 6], F32)
    row_in(k, "ln_in", g, io["ln_mix_g_2"][layer])
    row_in(k, "ln_in", b, io["ln_mix_b_2"][layer])

    def finish(t, banks, m):
        for h in range(2):
            s = slice(512 * h, 512 * h + 512)
            V.start([m, A, G])
            V.done(V.eng.scalar_tensor_tensor(y[:, s], tile_of(X, t)[:, s], ALPHA, banks[h][:, :], ALU.mult, ALU.add,
                                              accum_out=st[:, 3 + h:4 + h]))
        V.tt(st[:, 5:6], st[:, 3:4], st[:, 4:5], ALU.add)
        both(layer_norm_tile(k, st, y[:, :], st[:, 5:6], g[:, :], b[:, :], tile_of(X, t), dump[:, :]))

    out_project(k, ps, sb, mix, blocks, w, finish)


def turned(k, c, ps, X, tile, take):
    with k.loop(NT) as t:
        m = k.A.copy(tile[:, :], tile_of(X, t))
        k.T.after(m)
        for b in range(KD):
            m = k.T.turn(ps[b // 4][:, (b % 4) * P:(b % 4) * P + P], tile[:, b * P:(b + 1) * P], c["ident"][:, :])
        take(t, m)


def transpose_x(k, c, ps, X, xT, sb):
    tile = sb("x_tile", [P, D], F32)

    def take(t, m):
        for h in range(2):
            (k.V if h else k.A).copy(xT[:, 4 * h:4 * h + 4, bass.ds(t * P, P)],
                                     ps[h][:, :].rearrange("p (b t) -> p b t", b=4), after=[m])
    turned(k, c, ps, X, tile, take)


def windowed_attention(k, c, ps, io, X, mix, sb):
    V, A, T, G = k.V, k.A, k.T, k.G
    HQ, HK, HD = 16, 4, 64
    BAND = 3 * P
    spans = [(0, 512), (512, 512)]
    xT = sb("xT", [P, KD, SEQ], F32)
    transpose_x(k, c, ps, X, xT, sb)
    pr = Projector(k, ps, io["attn_w_qkv_2"], xT, sb, 3)
    cos, sin = sb("cos", [P, SEQ], F32), sb("sin", [P, SEQ], F32)
    rot = sb("rotate", [P, P], F32)
    wv = sb("wv", [P, KD, HK * HD], F32)
    qT = sb("aq", [P, 2, SEQ], F32)
    kT = sb("ak", [P, SEQ + 2 * P], F32)
    vt = sb("av", [P, NT + 2, HK * HD], F32)
    raw, tmp = sb("a_raw", [P, SEQ], F32), sb("a_tmp", [P, SEQ], F32)
    oT = sb("ao", [P, 2, SEQ], F32)
    mask = sb("a_mask", [P, 3, BAND], F32)
    sink = sb("a_sink", [P, HQ], F32)
    lanes = [[sb(f"a_{n}{u}", shape, F32) for n, shape in (
        ("qw", [P, P]), ("kw", [P, BAND]), ("vw", [P, 3, HD]), ("s", [P, 2, BAND]), ("pT", [P, 2, BAND]), ("st", [P, 5, 2]))]
        for u in range(4)]
    for e in range(3):
        G.fill(mask[:, e, :], 0.0)
        rules = [(0, 1, -1), (2 * P, -1, 1)]
        if e != 1:
            rules.append((-P, 1, 0) if e == 0 else (2 * P - 1, -1, 0))
        for base, col, part in rules:
            G.start(())
            G.done(G.eng.affine_select(out=mask[:, e, :], in_=mask[:, e, :], compare_op=ALU.is_ge, fill=NEG, base=base,
                                       pattern=[[col, BAND]], channel_multiplier=part))
    for e in (0, SEQ + P):
        G.fill(kT[:, e:e + P], 0.0)
    for e in (0, NT + 1):
        G.fill(vt[:, e, :], 0.0)
    k.dma("a_small_in", cos[:, :], io["rope_cos"])
    k.dma("a_small_in", sin[:, :], io["rope_sin"])
    k.dma("a_small_in", rot[:, :], io["rope_turn"])
    row_in(k, "a_small_in", sink, io["attn_sink_2"][0])
    w3 = io["attn_w_qkv_2"][0].rearrange("(k p) c -> p k c", p=P)
    m = k.dma("a_wv_in", wv[:, :, :], w3[:, :, (HQ + HK) * HD:])
    T.after(m)
    for t in range(NT):
        bank = ps[6 + t % 2]
        T.after(A)
        for d in range(KD):
            m = T.mm(bank[:, 0:HK * HD], xT[:, d, t * P:(t + 1) * P], wv[:, d, :], start=d == 0, stop=d == KD - 1)
        A.copy(vt[:, t + 1, :], bank[:, 0:HK * HD], after=[m])

    def rotary(out):
        def take(j, col, n, z, m):
            s = slice(col, col + n)
            a = A.copy(raw[:, s], z, after=[m, V, T])
            t = T.mm(ps[6 + j][:, 0:n], rot[:, :], raw[:, s], after=[a, V])
            V.tt(tmp[:, s], ps[6 + j][:, 0:n], sin[:, s], ALU.mult, after=[t])
            g = G.tt(out[:, s], raw[:, s], cos[:, s], ALU.mult, after=[a, V])
            return [V.tt(out[:, s], out[:, s], tmp[:, s], ALU.add, after=[g])]
        pr.block(take, spans)

    def pair(lane, qb, g, x, e):
        qw, kw, vw, s_sb, pT, st = lanes[lane]
        K = ps[2 * lane:2 * lane + 2]
        scale = HD ** -0.5
        m1 = A.copy(qw[:, :], qT[:, x, bass.ds(qb * P, P)])
        m0 = G.copy(kw[:, :], kT[:, bass.ds(qb * P, BAND)])
        m2 = G.copy(vw[:, :, :], vt[:, bass.ds(qb, 3), bass.ds(g * HD, HD)])
        T.after(m1, m0)
        for h, half in enumerate(HALF):
            m = T.mm(K[h][:, 0:BAND], qw[half, :], kw[half, :])
        yield
        for h in range(2):
            V.stt(s_sb[:, h, :], K[h][:, 0:BAND], scale, mask[:, e, :], ALU.mult, ALU.add, after=[m])
        V.reduce(st[:, 0, :], s_sb[:, :, :], ALU.max)
        sk = sink[:, bass.ds(g * 4 + 2 * x, 2)]
        V.tt(st[:, 0, :], st[:, 0, :], sk, ALU.max)
        V.ts(st[:, 1, :], st[:, 0, :], -1.0, ALU.mult)
        v = V.tt(st[:, 2, :], sk, st[:, 0, :], ALU.subtract)
        for h in range(2):
            A.act(s_sb[:, h, :], s_sb[:, h, :], ACT.Exp, bias=st[:, 1, h:h + 1], accum=st[:, 3, h:h + 1], after=[v])
        a = A.act(st[:, 2, :], st[:, 2, :], ACT.Exp)
        yield
        V.tt(st[:, 3, :], st[:, 3, :], st[:, 2, :], ALU.add, after=[a])
        V.recip(st[:, 4, :], st[:, 3, :])
        for h in range(2):
            v = V.ts(s_sb[:, h, :], s_sb[:, h, :], st[:, 4, h:h + 1], ALU.mult)
            T.after(v)
            for j in range(3):
                m = T.turn(K[h][:, j * P:(j + 1) * P], s_sb[:, h, j * P:(j + 1) * P], c["ident"][:, :])
            a = A.copy(pT[:, h, :], K[h][:, 0:BAND], after=[m])
        yield
        T.after(a, m2)
        for h, half in enumerate(HALF):
            for j in range(3):
                m = T.mm(K[0][half, BAND:], vw[:, j, :], pT[:, h, j * P:(j + 1) * P], start=j == 0, stop=j == 2)
        a = A.copy(oT[:, x, bass.ds(qb * P, P)], K[0][:, BAND:], after=[m])
        T.after(a)
        yield

    with k.loop(HK) as g:
        pr.reset()
        for half in HALF:
            pr.part(half, bass.ds(g * HD + HQ * HD, HD))
        pr.whole()
        pr.load(bass.ds(g * 2 * P, P))
        pr.load(bass.ds(g * 2 * P + P, P))
        rotary(kT[:, P:P + SEQ])
        for x in range(2):
            rotary(qT[:, x, :])
        for line in (A, G, T):
            line.after(V, A)
        both(*[pair(2 * u + x, qb, g, x, e) for u, (qb, e) in enumerate(((0, 0), (NT - 1, 2))) for x in range(2)])
        with k.loop((NT - 2) // 2) as b:
            both(*[pair(2 * u + x, b * 2 + (u + 1), g, x, 1) for u in range(2) for x in range(2)])
        k.dma("mix_out", mix[bass.ds(2 * g, 2), :, :].rearrange("x p t -> p x t"), oT[:, :, :], after=[A])


def lru(k, c, ps, io, X, mix, sb):
    V, A, T, G = k.V, k.A, k.T, k.G
    BLK = 256
    spans = [(0, 512), (512, 512)]
    xT = sb("xT", [P, KD, SEQ], F32)
    transpose_x(k, c, ps, X, xT, sb)
    pr = Projector(k, ps, io["lru_w_in_2"], xT, sb, 4)
    gate = sb("l_gate", [P, 2, SEQ], F32)
    raw = sb("l_raw", [P, SEQ + 3], F32)
    xc = sb("l_xc", [P, 2, SEQ], F32)
    work = [[sb(f"l_{n}{z}", [P, SEQ], F32) for z in range(2)] for n in ("r", "i", "a", "u")]
    t1 = work[0][0]
    hs = [sb(f"l_h{z}", [P, SEQ], F32) for z in range(2)]
    wg = sb("l_wg", [P, 2, 2, 2, BLK], F32)
    cw, cb = sb("l_cw", [P, 4, 8], F32), sb("l_cb", [P, 8], F32)
    bg = sb("l_bg", [P, 2, 2, 8], F32)
    lam = sb("l_lam", [P, 2, 8], F32)
    sm = [sb(f"l_sm{i}", [P, 2, 8], F32) for i in range(4)]
    for t, n in ((cw[:, :, :].rearrange("p a b -> p (a b)"), "lru_conv_w_2"), (cb[:, :], "lru_conv_b_2"),
                 (bg[:, 0].rearrange("p a b -> p (a b)"), "lru_b_rgate_2"),
                 (bg[:, 1].rearrange("p a b -> p (a b)"), "lru_b_igate_2"),
                 (lam[:, :, :].rearrange("p a b -> p (a b)"), "lru_lambda_2")):
        m = k.dma("l_small_in", t, io[n + "_cols"])
    G.fill(raw[:, :], 0.0)
    e, s, s2, acc = (x[:, :, :] for x in sm)
    L = lam[:, :, :]
    V.stt(e, L, -1.0, L, ALU.mult, ALU.min, after=[m])
    a = A.act(e, e, ACT.Exp, after=[V])
    V.ts(s, e, 2.0, ALU.add, after=[a])
    V.recip(s, s)
    V.tt(s, s, e, ALU.mult)
    V.tt(s2, s, s, ALU.mult)
    V.ts(acc, s2, 1.0 / 19, ALU.mult)
    for n in (17, 15, 13, 11, 9, 7, 5, 3):
        V.stt(acc, acc, 1.0 / n, s2, ALU.add, ALU.mult)
    V.stt(acc, acc, 1.0, s, ALU.add, ALU.mult)
    V.ts(L, L, -1.0, ALU.mult, 0.0, ALU.max)
    V.stt(L, acc, 2.0, L, ALU.mult, ALU.add)
    V.ts(L, L, -8.0, ALU.mult)
    A.after(V)

    with k.loop(4) as n:
        pr.reset()
        for x in range(2):
            pr.load(bass.ds(n * BLK + D + x * P, P))
        for x in range(2):
            pr.load(bass.ds(n * BLK + x * P, P))
        for q, name in enumerate(("lru_w_rgate_2", "lru_w_igate_2")):
            for z in range(2):
                wm = k.dma("l_wg_in", wg[:, q, z], one(io[name][0, z], n).rearrange("(c p) f -> p c f", p=P))
        for x in range(2):
            def take(j, col, m_, z, m):
                return [A.copy(raw[:, 2 + col:2 + col + m_], z, after=[m, V, G])]
            pr.block(take, spans)
            col = lambda t: t[:, bass.ds(2 * n + x, 1)]
            V.ts(xc[:, x, :], raw[:, 0:SEQ], cw[:, 0, bass.ds(2 * n + x, 1)], ALU.mult, col(cb), ALU.add, after=[A, G])
            for j in range(1, 4):
                V.stt(xc[:, x, :], raw[:, j:j + SEQ], cw[:, j, bass.ds(2 * n + x, 1)], xc[:, x, :], ALU.mult, ALU.add)
        for x in range(2):
            def take(j, col, m_, z, m):
                s = slice(col, col + m_)
                a = A.act(t1[:, s], z, ACT.Square, after=[m, V])
                V.ts(t1[:, s], t1[:, s], 0.044715, ALU.mult, 1.0, ALU.add, after=[a])
                V.tt(t1[:, s], t1[:, s], z, ALU.mult)
                a = A.act(t1[:, s], t1[:, s], ACT.Sigmoid, scale=2 * (2 / np.pi) ** 0.5, after=[V])
                return [V.tt(gate[:, x, s], z, t1[:, s], ALU.mult, after=[a])]
            pr.block(take, spans)

        def direction(x, z):
            rr, ii, a_, u = (w[z] for w in work)
            for q, out in enumerate((rr, ii)):
                for j, (col, m_) in enumerate(spans):
                    bank = ps[4 * z + 2 * q + j]
                    T.after(wm, V, A)
                    for h in range(2):
                        m = T.mm(bank[:, :], wg[:, q, z, h, x * P:(x + 1) * P], xc[:, h, col:col + m_], start=h == 0,
                                 stop=h == 1)
                    A.act(out[:, col:col + m_], bank[:, :], ACT.Sigmoid, bias=bg[:, q, z, bass.ds(2 * n + x, 1)],
                          after=[m, V])
                yield
            V.ts(rr[:, :], rr[:, :], lam[:, z, bass.ds(2 * n + x, 1)], ALU.mult, after=[A])
            v = V.tt(ii[:, :], ii[:, :], xc[:, x, :], ALU.mult)
            yield
            a = A.act(a_[:, :], rr[:, :], ACT.Exp, after=[v])
            a2 = A.act(u[:, :], a_[:, :], ACT.Square)
            yield
            a = A.act(rr[:, :], rr[:, :], ACT.Tanh)
            V.stt(u[:, :], u[:, :], 1.0, rr[:, :], ALU.add, ALU.mult, after=[a])
            yield
            a = A.act(u[:, :], u[:, :], ACT.Sqrt, scale=-1.0, after=[V])
            start = 0 if z == 0 else SEQ - 1
            V.fill(u[:, start:start + 1], 1.0, after=[a])
            V.tt(u[:, :], u[:, :], ii[:, :], ALU.mult)
            back = slice(0, SEQ) if z == 0 else slice(SEQ - 1, None, -1)
            V.scan(hs[z][:, back], a_[:, back], u[:, back])
            yield

        for x in range(2):
            both(*[direction(x, z) for z in range(2)])
            V.tt(hs[0][:, :], hs[0][:, :], hs[1][:, :], ALU.add)
            V.tt(gate[:, x, :], gate[:, x, :], hs[0][:, :], ALU.mult)
        k.dma("mix_out", mix[bass.ds(2 * n, 2), :, :].rearrange("x p t -> p x t"), gate[:, :, :], after=[V])


NE, FF, CAP = 16, 1024, 128
HALF_FF = FF // 2
SLABS = 24
AHEAD = 3


def slab(io, layer, e, i):
    if i < 16:
        h, d = i // 8, i % 8
        w = one(io["moe_w_gate_up_2"][layer], e)[d * P:(d + 1) * P, :]
        return w.rearrange("p (x c) -> p x c", x=2)[:, :, h * HALF_FF:(h + 1) * HALF_FF]
    w = one(io["moe_w_down_2"][layer], e)[(i - 16) * P:(i - 15) * P, :]
    return w.rearrange("p (x c) -> p x c", x=2)


def moe(k, c, ps, io, layer, X, rows, out, sb):
    nc, V, A, T, G = k.nc, k.V, k.A, k.T, k.G
    x_rows, y_rows = rows
    ring = sb("ring", [P, SLABS, 2, HALF_FF], F32)
    ahead = 4
    tile = [sb(f"m_tile{i}", [P, D], F32) for i in range(ahead)]
    spare = [sb(f"m_spare{i}", [P, KD, P], F32) for i in range(ahead)]
    xg = sb("m_picked", [P, D], F32)
    xs, hs = sb("m_picked_T", [P, D], F32), sb("m_hidden_T", [P, FF], F32)
    hid, ys = sb("m_hidden", [P, FF], F32), sb("m_ys", [P, D], F32)
    wr = sb("m_router", [P, KD, NE], F32)
    affT = sb("m_aff", [NE, SEQ], F32)
    top, at = sb("m_top", [NE, CAP], F32), sb("m_top_at", [NE, CAP], U32)
    atf = sb("m_top_at_float", [NE, CAP], F32)
    gates, tokens = sb("m_gates", [P, NE], F32), sb("m_tokens", [P, NE], I32)
    pick = [sb(f"m_pick{i}", [P, 1], I32) for i in range(AHEAD)]
    st = [sb(f"m_st{i}", [P, 6], F32) for i in range(ahead)]
    aff = [sb(f"m_aff_tile{i}", [P, NE], F32) for i in range(ahead)]
    unused = sb("m_unused", [P, 1], F32)
    landed = k.landed

    def load(e, i, after=()):
        k.S.after(*after)
        nc.sync.dma_start(ring[:, i, :, :], slab(io, layer, e, i)).then_inc(landed[i], 16)

    def arrived(i):
        nc.tensor.wait_ge(landed[i], 16)
        nc.tensor.sem_clear(landed[i])

    m = k.dma("router_in", wr[:, :, :], io["moe_w_router_2"][layer].rearrange("(k p) e -> p k e", p=P))
    for i in range(SLABS):
        load(0, i)

    for dst in rows:
        x_stored = k.dma("x_rows_out", dst.rearrange("(t p) d -> p t d", p=P), X[:, :, :], line=A)

    def route(t, u):
        K = ps[2 * u:2 * u + 2]
        m = (G if u % 2 else A).copy(tile[u][:, :], tile_of(X, t))
        yield
        T.after(m)
        for b in range(KD):
            m = T.turn(K[b // 4][:, (b % 4) * P:(b % 4) * P + P], tile[u][:, b * P:(b + 1) * P], c["ident"][:, :])
        for h in range(2):
            m1 = (V if h else A).copy(spare[u][:, 4 * h:4 * h + 4, :], K[h][:, :].rearrange("p (b t) -> p b t", b=4),
                                      after=[m])
            T.after(m1)
        yield
        for d in range(KD):
            m = T.mm(K[0][:, 0:NE], spare[u][:, d, :], wr[:, d, :], start=d == 0, stop=d == KD - 1)
        V.reduce(st[u][:, 0:1], K[0][:, 0:NE], ALU.max, after=[m])
        v = V.ts(st[u][:, 1:2], st[u][:, 0:1], -1.0, ALU.mult)
        a = A.act(aff[u][:, :], K[0][:, 0:NE], ACT.Exp, bias=st[u][:, 1:2], accum=st[u][:, 2:3], after=[v])
        yield
        V.recip(st[u][:, 3:4], st[u][:, 2:3], after=[a])
        v = V.ts(aff[u][:, :], aff[u][:, :], st[u][:, 3:4], ALU.mult)
        m = T.turn(K[1][0:NE, 0:P], aff[u][:, :], c["ident"][:, :], after=[v])
        V.copy(affT[:, bass.ds(t * P, P)], K[1][0:NE, 0:P], after=[m])
        yield

    with k.loop(NT // ahead) as t:
        both(*[route(ahead * t + u, u) for u in range(ahead)])

    for i in range(0, CAP, 8):
        s = slice(i, i + 8)
        for ins in (lambda: V.eng.max(top[:, s], affT[:, :]),
                    lambda: V.eng.max_index(at[:, s], top[:, s], affT[:, :]),
                    lambda: V.eng.match_replace(affT[:, :], top[:, s], affT[:, :], -1.0)):
            V.start(())
            V.done(ins())
    v = V.copy(atf[:, :], at[:, :])
    T.after(v)
    T.turn(ps[4][:, 0:NE], atf[:, :], c["ident"][0:NE, 0:NE])
    m = T.turn(ps[4][:, NE:2 * NE], top[:, :], c["ident"][0:NE, 0:NE])
    V.copy(tokens[:, :], ps[4][:, 0:NE], after=[m])
    v = V.copy(gates[:, :], ps[4][:, NE:2 * NE])

    gathered, scattered = (Count(k, f"{name}{layer}", steady=True) for name in ("gathered", "scattered"))
    by = lambda count, e: (count, 16 * (e + 1), None)

    def gather(e, u, after=()):
        G.copy(pick[u][:, :], tokens[:, bass.ds(e, 1)], after=after)
        G.start(())
        G.eng.indirect_dma_start(xg[:, :], None, x_rows[:, :],
                                 bass.IndirectOffsetOnAxis(ap=pick[u][:, 0:1], axis=0)).then_inc(gathered.sem, 16)

    def scatter(e, u, after=()):
        G.start(after)
        G.eng.indirect_dma_start(y_rows[:, :], bass.IndirectOffsetOnAxis(ap=pick[u][:, 0:1], axis=0), ys[:, :], None,
                                 compute_op=ALU.add).then_inc(scattered.sem, 16)

    def turn_tokens(got):
        for b in range(KD):
            m = T.turn(ps[4 + b // 4][:, (b % 4) * P:(b % 4) * P + P], xg[:, b * P:(b + 1) * P], c["ident"][:, :],
                       after=[got])
        return [(V if h else A).copy(xs[:, 512 * h:512 * h + 512], ps[4 + h][:, :], after=[m]) for h in range(2)]

    def experts(first, n, more):
        ready = None
        for x in range(n):
            e = first + x
            if ready is None:
                ready = turn_tokens(by(gathered, e))
            T.after(*ready)
            nxt = more or x < n - 1
            before = [by(scattered, e - 1)] if x else []
            if nxt:
                gather(e + 1, (x + 1) % AHEAD, after=[T, *ready, *before])
            halves = []
            for h in range(2):
                for d in range(KD):
                    arrived(8 * h + d)
                    for j in range(2):
                        m = T.mm(ps[2 * h + j][:, :], xs[:, d * P:(d + 1) * P], ring[:, 8 * h + d, j, :], start=d == 0,
                                 stop=d == KD - 1)
                    if nxt:
                        load(e + 1, 8 * h + d, after=[m])
                s = slice(HALF_FF * h, HALF_FF * h + HALF_FF)
                a = A.act(hid[:, s], ps[2 * h][:, :], ACT.Sigmoid, after=[m])
                V.tt(hid[:, s], hid[:, s], ps[2 * h][:, :], ALU.mult, after=[a])
                halves.append(V.tt(hid[:, s], hid[:, s], ps[2 * h + 1][:, :], ALU.mult))
            for h in range(2):
                T.after(halves[h])
                for b in range(4 * h, 4 * h + 4):
                    m = T.turn(ps[4 + b // 2 % 2][:, (2 * h + b % 2) * P:(2 * h + b % 2) * P + P],
                               hid[:, b * P:(b + 1) * P], c["ident"][:, :])
                got_h = [line.copy(hs[:, 512 * h + 256 * i:512 * h + 256 * i + 256],
                                   ps[4 + i][:, 256 * h:256 * h + 256], after=[m]) for i, line in enumerate((A, V))]
                T.after(*got_h)
                for d in range(4 * h, 4 * h + 4):
                    arrived(16 + d)
                    for j in range(2):
                        m = T.mm(ps[6 + j][:, :], hs[:, d * P:(d + 1) * P], ring[:, 16 + d, j, :], start=d == 0,
                                 stop=d == KD - 1)
                    if nxt:
                        load(e + 1, 16 + d, after=[m])
            if x < n - 1:
                ready = turn_tokens(by(gathered, e + 1))
            a = A.act(ys[:, 0:512], ps[6][:, :], ACT.Copy, scale=gates[:, bass.ds(e, 1)], after=[m, *before])
            v = V.ts(ys[:, 512:], ps[7][:, :], gates[:, bass.ds(e, 1)], ALU.mult, after=[m, *before])
            scatter(e, x, after=[a, v, *before])
            T.after(a, v)
        G.after(by(scattered, first + n - 1))
        G.tt(unused[:, :], unused[:, :], unused[:, :], ALU.add)

    G.fill(unused[:, :], 0.0)
    gather(0, 0, after=[v])
    turns = (NE - 1) // AHEAD
    with k.loop(turns) as i:
        experts(i * AHEAD, AHEAD, True)
    experts(NE - 1, 1, False)
    k.barrier()

    g, b = xs, hs
    k.dma("ffn_ln_in", g[:, :], io["ln_ffn_g_2"][layer].partition_broadcast(P))
    k.dma("ffn_ln_in", b[:, :], io["ln_ffn_b_2"][layer].partition_broadcast(P))

    def norm(t, u):
        y = spare[u][:, :, :].rearrange("p a b -> p (a b)")
        m = k.dma(f"y_rows_in{u}", tile[u][:, :], y_rows[bass.ds(t * P, P), :])
        yield
        V.start([m])
        V.done(V.eng.scalar_tensor_tensor(y, tile_of(X, t), ALPHA - 1.0, tile[u][:, :], ALU.mult, ALU.add,
                                          accum_out=st[u][:, 3:4]))
        yield
        yield from layer_norm_tile(k, st[u], y, st[u][:, 3:4], g[:, :], b[:, :], tile_of(X, t), tile[u][:, :])
        if out is not None:
            k.dma("final_out", out[0, bass.ds(t * P, P), :], tile_of(X, t), after=[G])
        yield

    with k.loop(NT // ahead) as t:
        both(*[norm(ahead * t + u, u) for u in range(ahead)])


_INS = ["x", "meta", "norm_g", "w_in", "w_out", "gla_g_up", "gla_g_b", "gla_norm_g", "rw_conv", "rw_w0", "rw_w_up",
        "rw_a0", "rw_a_up", "rw_k_k", "rw_k_a", "rw_r_k", "rw_ln_g", "rw_ln_b", "final_norm_g", "attn_w_qkv_2",
        "attn_w_o_2", "attn_sink_2", "lru_w_in_2", "lru_conv_w_2", "lru_conv_b_2", "lru_w_rgate_2", "lru_b_rgate_2",
        "lru_w_igate_2", "lru_b_igate_2", "lru_lambda_2", "lru_w_out_2", "moe_w_router_2", "moe_w_gate_up_2",
        "moe_w_down_2", "ln_mix_g_2", "ln_mix_b_2", "ln_ffn_g_2", "ln_ffn_b_2"]
_COLS = ["norm_g", "gla_g_b", "gla_norm_g", "rw_conv", "rw_w0", "rw_a0", "rw_k_k", "rw_k_a", "rw_r_k", "rw_ln_g",
         "rw_ln_b", "lru_conv_w_2", "lru_conv_b_2", "lru_b_rgate_2", "lru_b_igate_2", "lru_lambda_2"]


def phase(nc, k):
    @contextmanager
    def held():
        with ExitStack() as ctx:
            k.phases += 1
            yield lambda name, shape, dt, n=k.phases: ctx.enter_context(nc.sbuf_tensor(f"{name}_{n}", shape, dt))
            k.barrier()
    return held()


def program(nc, io, out, mix, rows):
    with ExitStack() as ctx:
        k = Core(nc, ctx)
        ps = [ctx.enter_context(nc.psum_tensor(f"bank{i}", [P, 512], F32)) for i in range(8)]
        c = constants(k, lambda name, shape, dt: ctx.enter_context(nc.sbuf_tensor(name, shape, dt)))
        with phase(nc, k) as own:
            hnT = own("hnT", [P, KD, COLS], F32)
            for stage in (
                lambda sb: block_one_norm(k, c, ps, io, hnT, sb),
                lambda sb: attention_branch(k, c, ps, io, hnT, mix, sb),
                lambda sb: gla_branch(k, c, ps, io, hnT, mix, sb),
                lambda sb: rwkv_branch(k, c, ps, io, hnT, mix, sb),
            ):
                with phase(nc, k) as sb:
                    stage(sb)
        with phase(nc, k) as own:
            X = own("X", [P, NT, D], F32)
            for stage in (
                lambda sb: block_one_out(k, ps, io, mix, X, sb),
                lambda sb: windowed_attention(k, c, ps, io, X, mix, sb),
                lambda sb: mixer_out(k, ps, io, mix, 8, io["attn_w_o_2"][0], 0, X, sb),
                lambda sb: moe(k, c, ps, io, 0, X, rows, None, sb),
                lambda sb: lru(k, c, ps, io, X, mix, sb),
                lambda sb: mixer_out(k, ps, io, mix, 8, io["lru_w_out_2"][0], 1, X, sb),
                lambda sb: moe(k, c, ps, io, 1, X, rows, out, sb),
            ):
                with phase(nc, k) as sb:
                    stage(sb)


def rope_tables():
    rot = 16
    angle = np.arange(SEQ, dtype=np.float32) * (
        np.float32(500000.0) ** (-np.arange(0, rot, 2, dtype=np.float32) / rot))[:, None]
    cos, sin, turn = np.ones((P, SEQ), np.float32), np.zeros((P, SEQ), np.float32), np.zeros((P, P), np.float32)
    for h in (0, 64):
        for i in range(rot // 2):
            for at in (h + i, h + i + rot // 2):
                cos[at], sin[at] = np.cos(angle[i]), np.sin(angle[i])
            turn[h + i + rot // 2, h + i] = -1.0
            turn[h + i, h + i + rot // 2] = 1.0
    return {"rope_cos": cos, "rope_sin": sin, "rope_turn": turn}


def layouts(inputs):
    arrays = {name: np.ascontiguousarray(inputs[name]) for name in _INS}
    arrays.update(rope_tables())
    for name in _COLS:
        a = np.asarray(inputs[name])
        a = a.reshape(-1, a.shape[-1] // P, P)
        arrays[name + "_cols"] = np.ascontiguousarray(a.transpose(2, 0, 1).reshape(P, -1))
    arrays["rpb_padded"] = np.pad(np.ascontiguousarray(inputs["na_rpb"]).reshape(-1), RPB_PAD)
    return arrays


def kernel(**inputs):
    import concourse.bacc as _bacc
    from concourse.bass_utils import run_bass_kernel_spmd as _run

    nc = _bacc.Bacc("TRN2", target_bir_lowering=False, num_devices=1)
    arrays = layouts(inputs)
    io = {name: nc.dram_tensor(f"in_{name}", a.shape, mybir.dt.from_np(a.dtype), kind="ExternalInput").ap()
          for name, a in arrays.items()}
    out = nc.dram_tensor("out", (1, SEQ, D), F32, kind="ExternalOutput").ap()
    mix = nc.dram_tensor("mix", (12, P, SEQ), F32, kind="Internal").ap()
    rows = [nc.dram_tensor(name, (SEQ, D), F32, kind="Internal").ap() for name in ("x_rows", "y_rows")]
    program(nc, io, out, mix, rows)
    return _run(nc, [{f"in_{name}": a for name, a in arrays.items()}], core_ids=[0]).results[0]["out"]
```

```python
from contextlib import ExitStack, contextmanager

import numpy as np

import concourse.bass as bass
from concourse import mybir

F32 = mybir.dt.float32
I32 = mybir.dt.int32
U32 = mybir.dt.uint32
ALU = mybir.AluOpType
ACT = mybir.ActivationFunctionType
AX = mybir.AxisListType
P = 128


class Count:

    def __init__(self, core, name, steady=False):
        self.sem = core.ctx.enter_context(core.nc.semaphore(name))
        self.n, self.core, self.steady = 0, core, steady
        if not steady:
            core.counts.append(self)

    def mark(self):
        return self, self.n, self.core.epoch


class Line(Count):

    def __init__(self, core, name, eng, chained):
        super().__init__(core, name)
        self.eng, self.chained, self.seen = eng, chained, {}

    def after(self, *marks):
        for m in marks:
            if m is None:
                continue
            c, n, epoch = m.mark() if isinstance(m, Count) else m
            if c.steady:
                self.eng.wait_ge(c.sem, n)
            elif epoch == self.core.epoch and n > self.seen.get(c, 0):
                self.eng.wait_ge(c.sem, n)
                self.seen[c] = n

    def start(self, marks):
        self.after(*marks)
        if self.chained:
            self.after(self)

    def done(self, ins):
        ins.then_inc(self.sem, 1)
        self.n += 1
        return self.mark()


class Elementwise(Line):

    def tt(self, out, a, b, op, after=()):
        self.start(after)
        return self.done(self.eng.tensor_tensor(out, a, b, op))

    def ts(self, out, a, s1, op0, s2=None, op1=None, after=()):
        self.start(after)
        if op1 is None:
            return self.done(self.eng.tensor_scalar(out, a, s1, None, op0))
        return self.done(self.eng.tensor_scalar(out, a, s1, s2, op0, op1))

    def stt(self, out, a, s, b, op0, op1, after=()):
        self.start(after)
        return self.done(self.eng.scalar_tensor_tensor(out, a, s, b, op0, op1))

    def copy(self, out, a, after=()):
        self.start(after)
        return self.done(self.eng.tensor_copy(out, a))

    def fill(self, out, value, after=()):
        self.start(after)
        return self.done(self.eng.memset(out, value))

    def recip(self, out, a, after=()):
        self.start(after)
        return self.done(self.eng.reciprocal(out, a))

    def reduce(self, out, a, op, after=()):
        self.start(after)
        return self.done(self.eng.tensor_reduce(out, a, AX.X, op))

    def scan(self, out, keep, add, after=()):
        self.start(after)
        return self.done(self.eng.tensor_tensor_scan(out, keep, add, 0.0, ALU.mult, ALU.add))


class Activations(Line):
    def act(self, out, a, func, bias=0.0, scale=1.0, accum=None, after=()):
        self.start(after)
        return self.done(self.eng.activation(out, a, func, bias=bias, scale=scale, accum_out=accum))

    def copy(self, out, a, after=()):
        return self.act(out, a, ACT.Copy, after=after)


class Products(Line):
    def mm(self, out, lhsT, rhs, start=True, stop=True, after=()):
        self.start(after)
        return self.done(self.eng.matmul(out, lhsT, rhs, start=start, stop=stop))

    def turn(self, out, a, ident, after=()):
        self.start(after)
        return self.done(self.eng.transpose(out, a, ident))


class Core:

    def __init__(self, nc, ctx):
        self.nc, self.ctx, self.counts, self.epoch = nc, ctx, [], 0
        self.V = Elementwise(self, "vector_done", nc.vector, True)
        self.G = Elementwise(self, "gpsimd_done", nc.gpsimd, True)
        self.A = Activations(self, "scalar_done", nc.scalar, True)
        self.T = Products(self, "tensor_done", nc.tensor, False)
        self.S = Line(self, "sync_done", nc.sync, False)
        self.lines = [self.V, self.G, self.A, self.T, self.S]
        self.loads, self.phases = {}, 0
        self.landed = [ctx.enter_context(nc.semaphore(f"slab_landed{i}")) for i in range(SLABS)]

    def dma(self, name, out, in_, after=(), line=None):
        line = line or self.S
        if name not in self.loads:
            self.loads[name] = Count(self, name)
        c = self.loads[name]
        line.after(*after)
        line.eng.dma_start(out, in_).then_inc(c.sem, 16)
        c.n += 16
        return c.mark()

    def barrier(self):
        self.S.after(*self.loads.values())
        self.nc.all_engine_barrier()
        used = {c.sem.num for c in self.counts if c.n}
        own = {c.sem.num for c in self.counts}
        while used:
            first = last = min(used)
            while last + 1 in own and any(n > last for n in used):
                last += 1
            self.nc.sync.sem_clear(range(first, last + 1))
            used -= set(range(first, last + 1))
        self.nc.all_engine_barrier()
        self.epoch += 1
        for c in self.counts:
            c.n = 0
        for line in self.lines:
            line.seen = {}

    @contextmanager
    def loop(self, n):
        self.barrier()
        with self.nc.Fori(0, n) as i:
            yield i
            self.barrier()


def one(ap, i, dim=0):
    return ap[i] if dim == 0 else ap[:, i]


D = 1024
KD = D // P
SEQ = 1024
META = 16
CH = 64
X0 = CH
M0 = X0 - META
COLS = X0 + SEQ
NT = SEQ // P
NC = SEQ // CH
SPANS = [(M0, 5 * CH + META), (6 * CH, 6 * CH), (12 * CH, 5 * CH)]
SEQ_SPANS = [(X0, 512), (X0 + 512, 512)]
BW = 512
NA_COLS, GLA_COLS = 4 * BW, 3 * BW + 32
RW0 = NA_COLS + GLA_COLS
HALF = (slice(0, 64), slice(64, 128))
WIN_R, WIN_C = 8, 16
RPB_R, RPB_C = 2 * WIN_R - 1, 2 * WIN_C - 1
RPB_PAD = CH
NEG = -1e30
RB = 4


def constants(k, sb):
    G = k.G
    c = {}

    def mask(name, cols, conds):
        m = c[name] = sb(name, [P, cols], F32)
        G.fill(m[:, :], 1.0)
        for base, col, part in conds:
            G.start(())
            G.done(G.eng.affine_select(out=m[:, :], in_=m[:, :], compare_op=ALU.is_ge, fill=0.0, base=base,
                                       pattern=[[col, cols]], channel_multiplier=part))

    mask("ident", P, [(0, 1, -1), (0, -1, 1)])
    mask("ones", P, [])
    mask("before", P, [(-1, 1, -1)])
    mask("after", P, [(-1, -1, 1)])
    mask("upto", P, [(0, 1, -1)])
    mask("from", P, [(0, -1, 1)])
    for name, sign in (("upto64", 1), ("from64", -1)):
        m = c[name] = sb(name, [P, CH], F32)
        G.fill(m[:, :], 1.0)
        for h in HALF:
            G.start(())
            G.done(G.eng.affine_select(out=m[h, :], in_=m[h, :], compare_op=ALU.is_ge, fill=0.0, base=0,
                                       pattern=[[sign, CH]], channel_multiplier=-sign))
    m = c["halves"] = sb("halves", [P, P], F32)
    G.fill(m[:, :], 0.0)
    for h in HALF:
        G.fill(m[h, h], 1.0)
    return c


def rms_scale(k, st, x, rows, eps, dump, after=()):
    a = k.A.act(dump, x, ACT.Square, accum=st[0:rows, 0:1], after=after)
    k.V.ts(st[0:rows, 0:1], st[0:rows, 0:1], 1.0 / D, ALU.mult, eps, ALU.add, after=[a])
    a = k.A.act(st[0:rows, 0:1], st[0:rows, 0:1], ACT.Sqrt, after=[k.V])
    return k.V.recip(st[0:rows, 1:2], st[0:rows, 0:1], after=[a])


def block_one_norm(k, c, ps, io, hnT, sb):
    gcol = sb("norm_g_cols", [P, KD], F32)
    xt, dump, st = ([sb(f"{n}{u}", [P, w], F32) for u in range(4)]
                    for n, w in (("x_tile", D), ("squares", D), ("norm_stats", 2)))
    g_in = k.dma("norm_g_in", gcol[:, :], io["norm_g_cols"])
    zeros = k.G.fill(hnT[:, :, 0:M0], 0.0)
    k.V.after(g_in, zeros)

    def rows_of(src, rows, col, u):
        load = k.dma(f"x_in{u}", xt[u][0:rows, :], src, after=[k.T])
        v = rms_scale(k, st[u], xt[u][0:rows, :], rows, 1e-6, dump[u][0:rows, :], after=[load])
        yield
        v = k.V.ts(xt[u][0:rows, :], xt[u][0:rows, :], st[u][0:rows, 1:2], ALU.mult)
        yield
        k.T.after(v)
        K = ps[2 * u:2 * u + 2]
        for b in range(KD):
            t = k.T.turn(K[b // 4][:, (b % 4) * P:(b % 4) * P + rows], xt[u][0:rows, b * P:(b + 1) * P],
                         c["ident"][0:rows, 0:rows])
        for half in range(2):
            src_ps = K[half][:, 0:512].rearrange("p (b t) -> p b t", b=4)[:, :, 0:rows]
            g = gcol[:, 4 * half:4 * half + 4].unsqueeze(2).broadcast_to([P, 4, rows])
            v = k.V.tt(hnT[:, 4 * half:4 * half + 4, col], src_ps, g, ALU.mult, after=[t])
        k.T.after(v)
        yield

    def tile(t, u):
        yield from rows_of(io["x"][0, t * P:(t + 1) * P, :], P, slice(X0 + t * P, X0 + (t + 1) * P), u)
        if t == NT - 1:
            yield from rows_of(io["meta"], META, slice(M0, X0), u)

    in_lanes(tile)


class Projector:

    def __init__(self, k, ps, w_in, hnT, sb, ring):
        self.k, self.ps, self.hnT, self.ring, self.n = k, ps, hnT, ring, 0
        self.w = w_in[0].rearrange("(k p) c -> p k c", p=P)
        self.bufs = [sb(f"w_block{i}", [P, KD, P], F32) for i in range(ring)]
        self.used = [None] * ring
        self.evac = [None, None]
        self.side = 1
        self.loads = []

    def reset(self):
        self.used, self.evac, self.n, self.loads = [None] * self.ring, [None, None], 0, []

    def load(self, cols, width=P):
        b = self.n % self.ring
        self.n += 1
        mark = self.k.dma(f"w_in{b}", self.bufs[b][:, :, 0:width], self.w[:, :, cols], after=[self.used[b]])
        self.loads.append((b, mark, width))

    def part(self, half, cols):
        b = self.n % self.ring
        self.mark = self.k.dma(f"w_in{b}", self.bufs[b][:, :, half], self.w[:, :, cols], after=[self.used[b]])

    def whole(self):
        self.loads.append((self.n % self.ring, self.mark, P))
        self.n += 1

    def block(self, take, spans=SPANS):
        self.evacuate(self.multiply(spans), take)

    def multiply(self, spans=SPANS):
        k = self.k
        b, mark, width = self.loads.pop(0)
        s = self.side = 1 - self.side
        k.T.after(mark, *(self.evac[s] or ()))
        done = []
        for j, (col, n) in enumerate(spans):
            out = self.ps[3 * s + j][0:width, 0:n]
            for d in range(KD):
                m = k.T.mm(out, self.bufs[b][:, d, 0:width], self.hnT[:, d, col:col + n], start=d == 0, stop=d == KD - 1)
            done.append((j, col, n, out, m))
        self.used[b] = m
        return s, done

    def evacuate(self, products, take):
        s, done = products
        self.evac[s] = [m for span in done for m in take(*span)]


def silu_block(k, pr, out, tmp, off=X0, products=None):
    def take(j, col, n, z, m):
        s = slice(col - off, col - off + n)
        a = k.A.act(tmp[:, s], z, ACT.Sigmoid, after=[m, k.V])
        return [k.V.tt(out[:, s], z, tmp[:, s], ALU.mult, after=[a])]
    pr.evacuate(products or pr.multiply(SEQ_SPANS), take)


def copy_block(k, pr, out):
    def take(j, col, n, z, m):
        return [k.A.copy(out[0:z.shape[0], col:col + n], z, after=[m])]
    pr.block(take)


def attention_branch(k, c, ps, io, hnT, mix, sb):
    V, A, T, G = k.V, k.A, k.T, k.G
    NP = BW // P
    pr = Projector(k, ps, io["w_in"], hnT, sb, 4)
    qT = sb("na_q", [P, COLS], F32)
    kT = sb("na_k", [P, COLS], F32)
    vT = sb("na_v", [P, COLS], F32)
    gate = sb("na_gate", [P, SEQ], F32)
    vt = sb("na_v_tiles", [P, NC, P], F32)
    vm = sb("na_v_meta", [META, P], F32)
    bias = sb("na_bias", [P, BW // P * RPB_R, CH], F32)
    away = sb("na_outside", [P, CH], F32)
    lanes = [[sb(f"na_{n}{u}", shape, F32) for n, shape in (
        ("q_pair", [P, P]), ("scores", [P, 512 + META]), ("probs_T", [P, 5, P]), ("o", [P, P]), ("stats", [P, 4]))]
        for u in range(4)]
    oT = sb("na_oT", [P, SEQ], F32)
    for qbd, *_ in lanes:
        G.fill(qbd[:, :], 0.0)
    for h in HALF:
        G.fill(away[h, :], 0.0)
        for base, col, q in ((WIN_C // 2, 1, -1), (WIN_C // 2 - 1, -1, 1)):
            G.start(())
            G.done(G.eng.affine_select(out=away[h, :], in_=away[h, :], compare_op=ALU.is_ge, fill=NEG,
                                       base=base + (CH - 1) * q, pattern=[[col, CH]], channel_multiplier=-q))
    edge = sb("na_edge", [P, 2, CH], F32)
    for h in HALF:
        for e, (base, q) in enumerate(((WIN_C // 2 - 1, -1), (-(CH - WIN_C // 2), 1))):
            G.fill(edge[h, e, :], 1.0)
            G.start(())
            G.done(G.eng.affine_select(out=edge[h, e, :], in_=edge[h, e, :], compare_op=ALU.is_ge, fill=0.0,
                                       base=base + (CH - 1) * q, pattern=[[0, CH]], channel_multiplier=-q))
            G.start(())
            G.done(G.eng.affine_select(out=edge[h, e, :], in_=edge[h, e, :], compare_op=ALU.is_ge, fill=0.0,
                                       base=(WIN_C - 1) if e == 0 else -(CH - WIN_C),
                                       pattern=[[-1 if e == 0 else 1, CH]], channel_multiplier=0))
    G.tt(edge[:, 0, :], edge[:, 0, :], edge[:, 1, :], ALU.add)
    G.ts(edge[:, 0, :], edge[:, 0, :], -1.0, ALU.mult, 1.0, ALU.add)
    G.tt(away[:, :], away[:, :], edge[:, 0, :], ALU.mult)

    rpb = bass.AP(io["rpb_padded"].tensor, RPB_PAD + WIN_C - 1 - (CH - 1),
                  [[RPB_R * RPB_C, BW // 64], [1, CH], [RPB_C, RPB_R], [1, CH]])
    for h in range(2):
        for p in range(NP):
            m = k.dma("na_bias_in", bias[HALF[h], p * RPB_R:(p + 1) * RPB_R, :], rpb[2 * p + h])
    G.tt(bias[:, :, :], bias[:, :, :], away[:, :].unsqueeze(1).broadcast_to([P, NP * RPB_R, CH]), ALU.add, after=[m])
    with k.loop(NP) as p:
        pr.reset()
        for j in range(4):
            pr.load(bass.ds(p * P + j * BW, P))
        copy_block(k, pr, qT)
        copy_block(k, pr, kT)
        copy_block(k, pr, vT)
        silu_block(k, pr, gate, oT)
        T.after(A)
        for g in range(0, NC, 4):
            bank = ps[6 + (g // 4) % 2]
            T.after(A)
            for j in range(g, min(g + 4, NC - 1)):
                t = T.turn(bank[:, (j - g) * P:(j - g + 1) * P], vT[:, X0 + CH * j:X0 + CH * j + P], c["ident"][:, :])
            n = min(4, NC - 1 - g)
            A.copy(vt[:, g:g + n, :], bank[:, 0:n * P].rearrange("p (j f) -> p j f", f=P), after=[t])
        t = T.turn(ps[6][0:META, 0:P], vT[:, M0:X0], c["ident"][:, :], after=[A])
        A.copy(vm[:, :], ps[6][0:META, 0:P], after=[t])

        free = [None] * 4

        def grid_row(u, r, first, dr0):
            qbd, s_sb, pT, o_sb, st = lanes[u]
            K, R = ps[2 * u], ps[2 * u + 1]
            qs = slice(X0 + r * CH, X0 + r * CH + CH)
            for h in HALF:
                m = A.copy(qbd[h, h][:, ::-1], qT[h, qs])
            yield
            T.after(free[u])
            T.mm(K[:, :], qbd[:, :], kT[:, X0 + first * CH:X0 + first * CH + 512], after=[m])
            t = T.mm(R[:, 0:META], qbd[:, :], kT[:, M0:X0])
            yield
            scale = CH ** -0.5
            V.stt(s_sb[:, 0:512].rearrange("p (r c) -> p r c", c=CH), K[:, :].rearrange("p (r c) -> p r c", c=CH),
                  scale, bias[:, bass.ds(p * RPB_R + dr0, WIN_R), :], ALU.mult, ALU.add, after=[t, G])
            V.ts(s_sb[:, 512:], R[:, 0:META], scale, ALU.mult)
            V.reduce(st[:, 0:1], s_sb[:, :], ALU.max)
            v = V.ts(st[:, 1:2], st[:, 0:1], -1.0, ALU.mult)
            yield
            a = A.act(s_sb[:, :], s_sb[:, :], ACT.Exp, bias=st[:, 1:2], accum=st[:, 2:3], after=[v])
            yield
            for j in range(4):
                t = T.turn(K[:, j * P:(j + 1) * P], s_sb[:, j * P:(j + 1) * P], c["ident"][:, :], after=[a])
            tm = T.turn(R[0:META, 0:P], s_sb[:, 512:512 + META], c["ident"][:, :])
            yield
            m1 = A.copy(pT[:, 0:4, :], K[:, :].rearrange("p (j q) -> p j q", q=P), after=[t])
            m2 = V.copy(pT[0:META, 4, :], R[0:META, 0:P], after=[tm])
            V.recip(st[:, 3:4], st[:, 2:3])
            yield
            T.after(m1, m2)
            for j in range(4):
                T.mm(R[:, P:2 * P], pT[:, j, :], vt[:, first + 2 * j, :], start=j == 0, stop=False)
            t = T.mm(R[:, P:2 * P], pT[0:META, 4, :], vm[:, :], start=False)
            yield
            v = V.ts(o_sb[:, :], R[:, P:2 * P], st[:, 3:4], ALU.mult, after=[t])
            yield
            t = T.turn(R[:, 2 * P:3 * P], o_sb[:, :], c["ident"][:, :], after=[v])
            yield
            os = slice(r * CH, r * CH + CH)
            for h in HALF:
                free[u] = V.tt(oT[h, os], R[h, 2 * P + h.start:2 * P + h.stop][:, ::-1], gate[h, os], ALU.mult,
                               after=[t])
            yield

        def lane(u):
            for _ in range(u):
                yield
            for r in range(u, NC, 4):
                first = min(max(r - WIN_R // 2, 0), NC - WIN_R)
                yield from grid_row(u, r, first, first - r + WIN_R - 1)

        for line in (A, V, T):
            line.after(A, V)
        both(*[lane(u) for u in range(4)])
        k.dma("mix_out", one(mix, p), oT[:, :], after=[V])


def keep_masks(k, sb):
    keep = sb("keep", [P, 2, COLS], F32)
    k.G.fill(keep[:, :, :], 1.0)
    for d, at in ((0, 0), (1, CH - 1)):
        m = k.G.fill(keep[:, d, :].rearrange("p (c t) -> p c t", t=CH)[:, :, at:at + 1], 0.0)
    return keep, m


def chunk_sums(k, out, x, keep, d, after=()):
    V = k.V
    if d == 0:
        return V.scan(out[:, :], keep[:, 0, :], x[:, :], after=after)
    V.scan(out[:, 0:X0], keep[:, 0, 0:X0], x[:, 0:X0], after=after)
    back = slice(COLS - 1, X0 - 1, -1)
    return V.scan(out[:, back], keep[:, 1, back], x[:, back])


def chunk_ends(k, out, e, d, after=()):
    v = e[:, :].rearrange("p (c t) -> p c t", t=CH)
    if d == 0:
        return k.V.copy(out[:, :], v[:, :, CH - 1], after=after)
    k.V.copy(out[:, 0:1], v[:, 0:1, CH - 1], after=after)
    return k.V.copy(out[:, 1:], v[:, 1:, 0])


def both(*steps):
    steps = list(steps)
    while steps:
        for s in list(steps):
            if next(s, StopIteration) is StopIteration:
                steps.remove(s)


def in_lanes(step, n=4):
    def lane(u):
        for t in range(u, NT, n):
            yield from step(t, u)
    both(*[lane(u) for u in range(n)])


def spread(line, pair, src, n, after=()):
    for h in HALF:
        m = line.copy(pair[h, 0:n, h], src[h, :].rearrange("p (c t) -> p c t", t=CH), after=after)
    return m


def gla_branch(k, c, ps, io, hnT, mix, sb):
    V, A, T, G = k.V, k.A, k.T, k.G
    pr = Projector(k, ps, io["w_in"], hnT, sb, 4)
    keep, _ = keep_masks(k, sb)
    q = sb("gla_q", [P, COLS], F32)
    kk = sb("gla_k", [P, COLS], F32)
    vT = sb("gla_v", [P, NC + 1, 2, CH], F32)
    gd = [sb(f"gla_gd{d}", [META, COLS], F32) for d in range(2)]
    up = sb("gla_up", [16, 2, 2 * P], F32)
    upb = sb("gla_up_bias", [P, 2, 2], F32)
    upp = sb("gla_up_pair", [16, 2, P], F32)
    ng = sb("gla_norm", [P, 1], F32)
    gate = sb("gla_gate", [P, 2, SEQ], F32)
    o = sb("gla_out", [P, 2, SEQ], F32)
    lw, cum, tmp = ([sb(f"gla_{n}{d}", [P, COLS], F32) for d in range(2)] for n in ("log_decay", "sums", "tmp"))
    qe = [sb(f"gla_qe{d}", [P, COLS], F32) for d in range(2)]
    ke = [sb(f"gla_ke{d}", [P, COLS], F32) for d in range(2)]
    dec = [sb(f"gla_dec{d}", [P, NC + 1], F32) for d in range(2)]
    small = [{n: sb(f"gla_{n}{d}", [P, RB, P], F32) for n in ("q2", "k2", "vc", "kt", "vt", "at", "ds")}
             for d in range(2)]
    state = [sb(f"gla_state{d}", [P, RB + 1, P], F32) for d in range(2)]
    for d in range(2):
        for n in ("q2", "k2"):
            G.fill(small[d][n][:, :, :], 0.0)
    for t in (q, kk, *lw):
        G.fill(t[:, 0:M0], 0.0)
    G.fill(vT[:, 0, :, 0:M0], 0.0)
    k.dma("gla_small_in", up[:, :, :], io["gla_g_up"][0].rearrange("d r c -> r d c"))
    k.dma("gla_small_in", upb[:, :, :], io["gla_g_b_cols"].rearrange("p (d b) -> p d b", d=2))
    k.dma("gla_small_in", ng[:, :], io["gla_norm_g_cols"])
    base = NA_COLS
    for d in range(2):
        pr.load(slice(base + 3 * BW + 16 * d, base + 3 * BW + 16 * d + 16), 16)
    for d in range(2):
        copy_block(k, pr, gd[d])

    def chunks(d, n, first, seq, order):
        w, S = small[d], state[d]
        K = ps[4 * d:4 * d + 4]
        cols = bass.ds(first * CH, n * CH)
        a = A.copy(w["vc"][:, 0:n, :].rearrange("p c (h t) -> p c h t", t=CH), vT[:, bass.ds(first, n), :, :])
        g1 = spread(G, w["q2"], qe[d][:, cols], n)
        g2 = spread(G, w["k2"], ke[d][:, cols], n)
        yield
        T.after(a, g1, g2)
        for j in range(n):
            js = slice(j * P, j * P + P)
            T.mm(K[0][:, js], w["k2"][:, j, :], w["q2"][:, j, :])
            T.turn(K[1][:, js], w["k2"][:, j, :], c["ident"][:, :])
            t = T.turn(K[2][:, js], w["vc"][:, j, :], c["ident"][:, :])
        v3 = lambda b: K[b][:, 0:n * P].rearrange("p (c t) -> p c t", t=P)
        forwards = d == 0 or not seq
        mask = c["upto" if forwards else "from"][:, :].unsqueeze(1).broadcast_to([P, n, P])
        v1 = V.tt(w["at"][:, 0:n, :], v3(0), mask, ALU.mult, after=[t])
        a1 = A.copy(w["kt"][:, 0:n, :], v3(1), after=[t])
        a2 = A.copy(w["vt"][:, 0:n, :], v3(2))
        yield
        T.after(v1, a1, a2)
        for j in range(n):
            t = T.mm(K[1][:, j * P:j * P + P], w["kt"][:, j, :], w["vt"][:, j, :])
        V.tt(w["ds"][:, 0:n, :], v3(1), dec[d][:, bass.ds(first, n)].unsqueeze(2).broadcast_to([P, n, P]), ALU.mult,
             after=[t])
        for i, j in enumerate(order):
            m = V.stt(S[:, i + 1, :], S[:, i, :], dec[d][:, bass.ds(first + j, 1)], w["ds"][:, j, :], ALU.mult, ALU.add)
        yield
        if seq:
            T.after(m)
            for i, j in enumerate(order):
                js = slice(j * P, j * P + P)
                T.mm(K[0][:, js], w["vt"][:, j, :], w["at"][:, j, :], stop=False)
                t = T.mm(K[0][:, js], S[:, i, :], w["q2"][:, j, :], start=False)
            ov = o[:, :, bass.ds(first * CH - X0, n * CH)].rearrange("p h (c t) -> p c h t", t=CH)
            V.tt(ov, K[0][:, 0:n * P].rearrange("p (c h t) -> p c h t", h=2, t=CH), ov, ALU.add, after=[t])
        V.copy(S[:, 0, :], S[:, n, :])
        yield

    with k.loop(2) as p:
        pr.reset()
        for cols in (bass.ds(p * P + base, P), bass.ds(p * P + base + 256, P),
                     bass.ds(p * 256 + base + BW, P), bass.ds(p * 256 + base + BW + P, P)):
            pr.load(cols)
        u = A.copy(upp[:, :, :], up[:, :, bass.ds(p * P, P)])

        def decay(d):
            free = None
            for col, n in SPANS:
                s = slice(col, col + n)
                t = T.mm(ps[6 + d][:, 0:n], upp[:, d, :], gd[d][:, s], after=[u, free])
                free = V.ts(lw[d][:, s], ps[6 + d][:, 0:n], upb[:, d, bass.ds(p, 1)], ALU.add, after=[t])
            yield
            s = slice(M0, COLS)
            v = V.stt(tmp[d][:, s], lw[d][:, s], -1.0, lw[d][:, s], ALU.mult, ALU.min)
            A.act(tmp[d][:, s], tmp[d][:, s], ACT.Exp, after=[v])
            a = A.act(tmp[d][:, s], tmp[d][:, s], ACT.Ln, bias=1.0)
            yield
            V.stt(lw[d][:, s], lw[d][:, s], 0.0, tmp[d][:, s], ALU.min, ALU.subtract, after=[a])
            g = G.fill(lw[d][:, 0:M0], 0.0)
            v = chunk_sums(k, cum[d], lw[d], keep, d, after=[g])
            A.act(lw[d][:, :], cum[d][:, :], ACT.Exp, scale=-1.0 / 16, after=[v])
            a = A.act(cum[d][:, :], cum[d][:, :], ACT.Exp, scale=1.0 / 16)
            yield
            chunk_ends(k, dec[d], cum[d], d, after=[a])
            G.fill(state[d][:, 0, :], 0.0)
            yield

        both(*[decay(d) for d in range(2)])
        copy_block(k, pr, q)
        copy_block(k, pr, kk)
        for cols in (bass.ds(p * 256 + base + 2 * BW, P), bass.ds(p * 256 + base + 2 * BW + P, P)):
            pr.load(cols)
        for d in range(2):
            V.stt(qe[d][:, :], q[:, :], CH ** -0.5, cum[d][:, :], ALU.mult, ALU.mult, after=[A])
            V.tt(ke[d][:, :], kk[:, :], lw[d][:, :], ALU.mult)
        for h in range(2):
            def take(j, col, n, z, m, h=h):
                dst = vT[:, :, :, :].rearrange("p c h t -> p h c t")[:, h]
                if col == M0:
                    A.copy(dst[:, 0, M0:X0], z[:, 0:META], after=[m])
                    col, n, z = X0, n - META, z[:, META:]
                return [A.copy(dst[:, col // CH:(col + n) // CH, :], z.rearrange("p (c t) -> p c t", t=CH), after=[m])]
            pr.block(take)
        for h in range(2):
            silu_block(k, pr, gate[:, h, :], tmp[0])
        G.fill(o[:, :, :], 0.0)
        for line in (A, G, T):
            line.after(V)
        V.after(G)
        both(*[chunks(d, 1, 0, False, [0]) for d in range(2)])
        with k.loop(NC // RB) as i:
            both(chunks(0, RB, i * RB + 1, True, range(RB)),
                 chunks(1, RB, (NC - RB + 1) - i * RB, True, range(RB)[::-1]))
        def head_norm(h, i):
            s, w, bank = slice(512 * i, 512 * i + 512), tmp[h][:, 512 * i:512 * i + 512], ps[2 * h + i]
            a = A.act(w, o[:, h, s], ACT.Square)
            t = T.mm(bank[:, :], c["ones"][:, :], w, after=[a])
            v = V.ts(w, bank[:, :], 1.0 / P, ALU.mult, 1e-5, ALU.add, after=[t])
            yield
            a = A.act(w, w, ACT.Sqrt, after=[v])
            V.recip(w, w, after=[a])
            V.tt(w, w, gate[:, h, s], ALU.mult)
            v = V.stt(o[:, h, s], o[:, h, s], ng[:, 0:1], w, ALU.mult, ALU.mult)
            k.dma("mix_out", one(mix, 2 * p + 4 + h)[:, s], o[:, h, s], after=[v])
            yield

        both(*[head_norm(h, i) for h in range(2) for i in range(2)])


DECAY = float(np.exp(-0.5))


def rwkv_branch(k, c, ps, io, hnT, mix, sb):
    V, A, T, G = k.V, k.A, k.T, k.G
    pr = Projector(k, ps, io["w_in"], hnT, sb, 3)
    keep, _ = keep_masks(k, sb)
    full = lambda name, n=COLS: sb("rw_" + name, [P, n], F32)
    raws = [full(f"raw{i}", COLS + 2) for i in range(2)]
    r, kx, v, kk = full("r"), full("k"), full("v"), full("kk")
    twd, ad = full("decay_in"), full("alpha_in")
    kt, bt, at, rt = ([full(f"{n}{d}") for d in range(2)] for n in ("kt", "bt", "at", "rt"))
    gate = full("gate", SEQ)
    bonus = full("bonus", SEQ)
    y = kx
    conv = sb("rw_conv_cols", [P, 3, 14], F32)
    wup = sb("rw_w_up", [P, BW], F32)
    aup = sb("rw_a_up", [P, BW], F32)
    up2 = sb("rw_up_pair", [P, 2, P], F32)
    w0 = sb("rw_w0c", [P, 2, 4], F32)
    a0 = sb("rw_a0c", [P, 2, 4], F32)
    vec = {n: sb(f"rw_{n}c", [P, 4], F32) for n in ("k_k", "k_a", "one_k_a", "r_k", "ln_g", "ln_b")}
    dec = [sb(f"rw_dec{d}", [P, NC + 1], F32) for d in range(2)]
    names = ("a2", "b2", "k2", "v2", "P0", "PT0", "P1", "PT1", "TT", "AK", "RQ", "aT", "bT", "kT", "vT", "QY")
    small = [{n: sb(f"rw_{n}_{d}", [P, RB, P], F32) for n in names[:4]} for d in range(2)]
    temps = []
    for d in range(2):
        work = sb(f"rw_work{d}", [P, (len(names) - 4) * RB * P], F32)
        for i, n in enumerate(names[4:]):
            small[d][n] = work[:, i * RB * P:(i + 1) * RB * P].rearrange("p (c t) -> p c t", t=P)
        temps.append([work[:, i * COLS:(i + 1) * COLS] for i in range(5)])
    state = [sb(f"rw_state{d}", [P, P], F32) for d in range(2)]

    for d in range(2):
        for n in ("a2", "b2", "k2", "v2"):
            G.fill(small[d][n][:, :, :], 0.0)
    for t in (r, kk, v, *kt, *bt, *at, *rt):
        G.fill(t[:, 0:M0], 0.0)
    for raw in raws:
        G.fill(raw[:, :], 0.0)
    for name, t in (("rw_conv", conv), ("rw_w0", w0), ("rw_a0", a0)):
        k.dma("rw_small_in", t[:, :, :].rearrange("p a b -> p (a b)"), io[name + "_cols"])
    for n, t in vec.items():
        if n != "one_k_a":
            k.dma("rw_small_in", t[:, :], io[f"rw_{n}_cols"])
    k.dma("rw_small_in", wup[:, :], io["rw_w_up"][0].rearrange("d r c -> (d r) c"))
    small_in = k.dma("rw_small_in", aup[:, :], io["rw_a_up"][0].rearrange("d r c -> (d r) c"))
    V.ts(vec["one_k_a"][:, :], vec["k_a"][:, :], -1.0, ALU.mult, 1.0, ALU.add, after=[small_in, G])
    V.ts(vec["r_k"][:, :], vec["r_k"][:, :], 0.5, ALU.mult)
    A.after(V, G)
    T.after(V)

    def conv_block(out, blk, raw):
        def take(j, col, n, z, m):
            return [A.copy(raw[:, 1 + col:1 + col + n], z, after=[m, V])]
        pr.block(take)
        s = slice(M0, COLS)
        tap = lambda i: conv[:, i, blk]
        V.ts(out[:, s], raw[:, 1 + M0:1 + COLS], tap(1), ALU.mult, after=[A, G])
        V.stt(out[:, s], raw[:, M0:COLS], tap(0), out[:, s], ALU.mult, ALU.add)
        return V.stt(out[:, s], raw[:, 2 + M0:2 + COLS], tap(2), out[:, s], ALU.mult, ALU.add)

    for j in range(2):
        pr.load(slice(RW0 + 3 * BW + P * j, RW0 + 3 * BW + P * j + P))
    conv_block(twd, slice(12, 13), raws[0])
    conv_block(ad, slice(13, 14), raws[1])
    s0 = slice(M0, COLS)
    A.act(twd[:, s0], twd[:, s0], ACT.Tanh, after=[V])

    def chunks(d, n, first, seq, order):
        w, S = small[d], state[d]
        K = ps[4 * d:4 * d + 4]
        cols = bass.ds(first * CH, n * CH)
        v3 = lambda b: K[b][:, 0:n * P].rearrange("p (c t) -> p c t", t=P)
        v4 = lambda b: K[b][:, 0:n * P].rearrange("p (c x t) -> p c x t", x=2, t=CH)
        gk = spread(G, w["k2"], kt[d][:, cols], n)
        gv = spread(G, w["v2"], v[:, cols], n)
        a = spread(A, w["b2"], bt[d][:, cols], n)
        m = spread(V, w["a2"], at[d][:, cols], n)
        rs = A.copy(w["QY"][:, 0:n, 0:CH], rt[d][:, cols].rearrange("p (c t) -> p c t", t=CH))
        yield
        T.after(rs, m)
        for j in range(n):
            js = slice(j * P, j * P + P)
            T.mm(K[0][:, js], w["b2"][:, j, :], w["a2"][:, j, :])
            T.mm(K[1][:, js], w["a2"][:, j, :], w["b2"][:, j, :])
            T.mm(K[3][:, j * P:j * P + CH], w["b2"][:, j, :], w["QY"][:, j, 0:CH])
        T.after(gk)
        for j in range(n):
            js = slice(j * P, j * P + P)
            T.mm(K[2][:, js], w["k2"][:, j, :], w["a2"][:, j, :])
            t = T.mm(K[3][:, j * P + CH:j * P + P], w["k2"][:, j, :], w["QY"][:, j, 0:CH])
        forwards = d == 0 or not seq
        less, more, upto = ("before", "after", "upto64") if forwards else ("after", "before", "from64")
        wide = lambda name: c[name][:, :].unsqueeze(1).broadcast_to([P, n, P])
        f1 = V.tt(w["PT0"][:, 0:n, :], v3(0), wide(less), ALU.mult, after=[t])
        V.tt(w["P0"][:, 0:n, :], v3(1), wide(more), ALU.mult)
        gt = G.tt(w["TT"][:, 0:n, :], w["PT0"][:, 0:n, :], wide("ident"), ALU.add, after=[f1])
        V.tt(w["AK"][:, 0:n, :], v3(2), wide(less), ALU.mult)
        for x in range(2):
            f3 = V.tt(w["RQ"][:, 0:n, x * CH:x * CH + CH], v4(3)[:, :, x, :],
                      c[upto][:, :].unsqueeze(1).broadcast_to([P, n, CH]), ALU.mult)
        yield
        T.after(f3, gv)
        for b, (src, dst) in enumerate((("a2", "aT"), ("b2", "bT"), ("k2", "kT"), ("v2", "vT"))):
            for j in range(n):
                t = T.turn(K[b][:, j * P:j * P + P], w[src][:, j, :], c["ident"][:, :])
        for b, dst in enumerate(("aT", "bT", "kT", "vT")):
            a = A.copy(w[dst][:, 0:n, :], v3(b), after=[t])
        yield
        T.after(a, gt)
        x, xt = "P0", "PT0"
        for i in range(5):
            nx, nxt = ("P1", "PT1") if i % 2 == 0 else ("P0", "PT0")
            for j in range(n):
                js = slice(j * P, j * P + P)
                t = T.mm(K[0][:, js], w[xt][:, j, :], w[x][:, j, :])
            f = V.copy(w[nx][:, 0:n, :], v3(0), after=[t])
            if i < 4:
                for j in range(n):
                    t = T.mm(K[1][:, j * P:j * P + P], w[x][:, j, :], w[xt][:, j, :])
                a = A.copy(w[nxt][:, 0:n, :], v3(1), after=[t])
            yield
            T.after(f)
            for j in range(n):
                t = T.mm(K[2][:, j * P:j * P + P], w[nx][:, j, :], w["TT"][:, j, :])
            f = V.tt(w["TT"][:, 0:n, :], v3(2), w["TT"][:, 0:n, :], ALU.add, after=[t])
            T.after(a)
            x, xt = nx, nxt
            yield
        for j in range(n):
            t = T.mm(K[3][:, j * P:j * P + P], w["AK"][:, j, :], w["vT"][:, j, :])
        a = A.copy(w["P0"][:, 0:n, :], v3(3), after=[t])
        yield
        T.after(f, a)
        for j in range(n):
            js = slice(j * P, j * P + P)
            T.mm(K[0][:, js], w["TT"][:, j, :], w["aT"][:, j, :])
            t = T.mm(K[1][:, js], w["TT"][:, j, :], w["P0"][:, j, :])
        a = A.copy(w["PT0"][:, 0:n, :], v3(0), after=[t])
        f = V.copy(w["PT1"][:, 0:n, :], v3(1), after=[t])
        yield
        T.after(a, f)
        for j in range(n):
            js = slice(j * P, j * P + P)
            T.mm(K[0][:, js], w["PT0"][:, j, :], w["bT"][:, j, :])
            T.mm(K[1][:, js], w["kT"][:, j, :], w["vT"][:, j, :], stop=False)
            T.mm(K[1][:, js], w["bT"][:, j, :], w["PT1"][:, j, :], start=False)
            q, yy = slice(j * P, j * P + CH), slice(j * P + CH, j * P + P)
            T.mm(K[2][:, q], w["PT0"][:, j, :], w["RQ"][:, j, 0:CH])
            T.mm(K[2][:, yy], w["vT"][:, j, :], w["RQ"][:, j, CH:], stop=False)
            t = T.mm(K[2][:, yy], w["PT1"][:, j, :], w["RQ"][:, j, 0:CH], start=False)
        V.tt(w["P1"][:, 0:n, :], v3(0), wide("ident"), ALU.add, after=[t])
        V.tt(w["a2"][:, 0:n, :], v3(1), dec[d][:, bass.ds(first, n)].unsqueeze(2).broadcast_to([P, n, P]), ALU.mult)
        f = V.tt(w["QY"][:, 0:n, 0:CH], v4(2)[:, :, 0, :], w["QY"][:, 0:n, 0:CH], ALU.add)
        yv = None
        if seq:
            yv = y[:, bass.ds(first * CH - X0, n * CH)].rearrange("p (c t) -> p c t", t=CH)
            f = V.tt(w["QY"][:, 0:n, CH:], v4(2)[:, :, 1, :], yv, ALU.add)
        yield
        for j in order:
            T.after(f)
            if seq:
                T.mm(K[3][:, 0:CH], S[:, :], w["QY"][:, j, 0:CH])
            t = T.mm(K[3][:, P:2 * P], w["P1"][:, j, :], S[:, :])
            f = V.stt(S[:, :], K[3][:, P:2 * P], dec[d][:, bass.ds(first + j, 1)], w["a2"][:, j, :], ALU.mult, ALU.add,
                      after=[t])
            if seq:
                f = V.tt(y[:, bass.ds((first + j) * CH - X0, CH)], K[3][:, 0:CH], w["QY"][:, j, CH:], ALU.add)
            yield

    blocks = SEQ // 512
    with k.loop(4) as p:
        pr.reset()
        one_col = lambda t: t[:, bass.ds(p, 1)]
        for j in (1, 0, 2):
            pr.load(bass.ds(p * P + RW0 + j * BW, P))

        def group_sum(bank, x, s, after):
            return T.mm(bank[:, 0:s.stop - s.start], c["halves"][:, :], x[:, s], after=after)

        A.copy(up2[:, 0, :], wup[:, bass.ds(p * P, P)])
        free = [A.copy(up2[:, 1, :], aup[:, bass.ds(p * P, P)])] * 2
        got, i = {}, 0
        for x, which, b in ((twd, 0, w0), (ad, 1, a0)):
            for d in range(2):
                out = temps[d][0 if which else 2]
                for col, n in SPANS:
                    bank, s = ps[6 + i % 2], slice(col, col + n)
                    t = T.mm(bank[:, 0:n], up2[HALF[d], which, :], x[HALF[d], s], after=[free[i % 2]])
                    free[i % 2] = A.act(out[:, s], bank[:, 0:n], ACT.Sigmoid, bias=b[:, d, bass.ds(p, 1)], after=[t])
                    i += 1
                got[which, d] = A.mark()
        for d in range(2):
            alpha, alpha_k, e1, e2, e3 = temps[d]
            G.fill(state[d][:, :], 0.0)
            g = G.fill(e1[:, 0:M0], 0.0)
            chunk_sums(k, e2, e1, keep, d, after=[got[0, d], g])
            v1 = V.tt(e1, e2, e1, ALU.subtract)
            A.act(e1, e1, ACT.Exp, scale=-DECAY, after=[v1])
            A.act(e3, e2, ACT.Exp, scale=DECAY)
            a = A.act(e2, e2, ACT.Exp, scale=-DECAY)
            chunk_ends(k, dec[d], e2, d, after=[a])
            A.act(alpha_k[:, s0], alpha[:, s0], ACT.Identity, bias=one_col(vec["one_k_a"]), scale=one_col(vec["k_a"]))
        m = conv_block(kx, bass.ds(p + 4, 1), raws[0])
        pr.load(bass.ds(p * P + RW0 + 3 * BW + 2 * P, P))
        squares, norm = at[1], at[0]
        sq = A.act(squares[:, s0], kx[:, s0], ACT.Square, scale=one_col(vec["k_k"]), after=[m])
        conv_block(r, bass.ds(p, 1), raws[1])
        for i, (col, n) in enumerate(SPANS):
            s, bank = slice(col, col + n), ps[6 + i % 2]
            t = group_sum(bank, squares, s, [sq, free[i % 2]])
            free[i % 2] = a = A.act(norm[:, s], bank[:, 0:n], ACT.Sqrt, after=[t])
        V.ts(norm[:, s0], norm[:, s0], 1e-12, ALU.max, after=[a])
        V.recip(norm[:, s0], norm[:, s0])
        V.stt(kk[:, s0], kx[:, s0], one_col(vec["k_k"]), norm[:, s0], ALU.mult, ALU.mult)
        for d in range(2):
            alpha, alpha_k, e1, e2, e3 = temps[d]
            V.tt(kt[d][:, s0], kx[:, s0], alpha_k[:, s0], ALU.mult)
            if d:
                V.tt(bonus[:, :], kt[0][:, X0:], kt[1][:, X0:], ALU.add)
        V.stt(bonus[:, :], bonus[:, :], one_col(vec["r_k"]), r[:, X0:], ALU.mult, ALU.mult)
        for d in range(2):
            alpha, alpha_k, e1, e2, e3 = temps[d]
            V.tt(kt[d][:, s0], kt[d][:, s0], e3[:, s0], ALU.mult)
            V.tt(alpha[:, s0], alpha[:, s0], e3[:, s0], ALU.mult)
            V.tt(bt[d][:, s0], kk[:, s0], alpha[:, s0], ALU.mult)
            V.tt(rt[d][:, s0], r[:, s0], e2[:, s0], ALU.mult)
            v1 = V.stt(at[d][:, s0], kk[:, s0], -1.0, e1[:, s0], ALU.mult, ALU.mult)
        conv_block(v, bass.ds(p + 8, 1), raws[0])
        gate_z = pr.multiply(SEQ_SPANS)
        sums = [group_sum(ps[6 + i], bonus, slice(512 * i, 512 * i + 512), [v1, *free]) for i in range(blocks)]
        for i, t in enumerate(sums):
            s = slice(512 * i, 512 * i + 512)
            V.tt(bonus[:, s], ps[6 + i][:, :], v[:, X0 + 512 * i:X0 + 512 * i + 512], ALU.mult, after=[t])
        G.fill(y[:, 0:SEQ], 0.0, after=[V])
        silu_block(k, pr, gate, temps[0][0], products=gate_z)
        A.after(V)
        V.after(G)
        T.after(V)
        both(*[chunks(d, 1, 0, False, [0]) for d in range(2)])
        with k.loop(NC // RB) as i:
            both(chunks(0, RB, i * RB + 1, True, range(RB)),
                 chunks(1, RB, (NC - RB + 1) - i * RB, True, range(RB)[::-1]))
        def group_norm(i):
            s, bank, tmp = slice(512 * i, 512 * i + 512), ps[i], temps[i][0][:, 0:512]
            t = group_sum(bank, y, s, [])
            v = V.stt(y[:, s], bank[:, :], -1.0 / CH, y[:, s], ALU.mult, ALU.add, after=[t])
            a = A.act(tmp, y[:, s], ACT.Square, after=[v])
            yield
            t = T.mm(bank[:, :], c["halves"][:, :], tmp, after=[a])
            v = V.ts(tmp, bank[:, :], 1.0 / CH, ALU.mult, 64e-5, ALU.add, after=[t])
            a = A.act(tmp, tmp, ACT.Sqrt, after=[v])
            yield
            V.recip(tmp, tmp, after=[a])
            V.stt(y[:, s], y[:, s], one_col(vec["ln_g"]), tmp, ALU.mult, ALU.mult)
            V.stt(y[:, s], y[:, s], one_col(vec["ln_b"]), bonus[:, s], ALU.add, ALU.add)
            v = V.tt(y[:, s], y[:, s], gate[:, s], ALU.mult)
            k.dma("mix_out", one(mix, p + 8)[:, s], y[:, s], after=[v])
            yield

        both(*[group_norm(i) for i in range(blocks)])


ALPHA = 4 ** 0.25
LN_EPS = 1e-5


def row_in(k, name, t, src):
    return k.dma(name, t[:, :], src.partition_broadcast(P))


def layer_norm_tile(k, st, y, total, g, b, out, dump):
    V, A, G = k.V, k.A, k.G
    v = V.ts(st[:, 0:1], total, -1.0 / D, ALU.mult)
    a = A.act(dump, y, ACT.Square, bias=st[:, 0:1], accum=st[:, 1:2], after=[v])
    yield
    V.ts(st[:, 1:2], st[:, 1:2], 1.0 / D, ALU.mult, LN_EPS, ALU.add, after=[a])
    a = A.act(st[:, 1:2], st[:, 1:2], ACT.Sqrt, after=[V])
    yield
    V.recip(st[:, 2:3], st[:, 1:2], after=[a])
    v = V.tt(st[:, 0:1], st[:, 0:1], st[:, 2:3], ALU.mult)
    a = A.act(y, y, ACT.Identity, bias=st[:, 0:1], scale=st[:, 2:3], after=[v])
    yield
    v = V.tt(y, y, g, ALU.mult, after=[a])
    G.tt(out, y, b, ALU.add, after=[v])


def out_project(k, ps, sb, src, blocks, w, finish):
    T = k.T
    lanes = 4
    wt = sb("out_w", [P, blocks, D], F32)
    xt = [sb(f"out_in{i}", [P, blocks, P], F32) for i in range(lanes)]
    wv = w.rearrange("(b p) n -> p b n", p=P)
    used, free, arrived = [None] * lanes, [None] * lanes, {}

    def load(t):
        arrived[t] = k.dma(f"out_in{t % lanes}", xt[t % lanes][:, :, :],
                           src[0:blocks, :, t * P:(t + 1) * P].rearrange("b p t -> p b t"), after=[used[t % lanes]])

    load(0)
    w_in = [k.dma(f"out_w_in{b}", wt[:, b:b + 2, :], wv[:, b:b + 2, :]) for b in range(0, blocks, 2)]
    for t in range(1, lanes):
        load(t)
    for t in range(NT):
        u = t % lanes
        T.after(arrived[t], free[u])
        for b in range(blocks):
            T.after(w_in[b // 2])
            for h in range(2):
                m = T.mm(ps[2 * u + h][:, :], xt[u][:, b, :], wt[:, b, 512 * h:512 * h + 512], start=b == 0,
                         stop=b == blocks - 1)
        used[u] = m
        if t + lanes < NT:
            load(t + lanes)
        free[u] = finish(t, ps[2 * u:2 * u + 2], m)


def block_one_out(k, ps, io, mix, X, sb):
    V, A = k.V, k.A
    y = sb("h_tile", [P, D], F32)
    xin = sb("h_in", [P, D], F32)
    dump = sb("squares", [P, D], F32)
    g = sb("final_g", [P, D], F32)
    st = sb("out_stats", [P, 2], F32)
    V.after(row_in(k, "final_g_in", g, io["final_norm_g"]))

    def finish(t, banks, m):
        x = k.dma("h_in", xin[:, :], io["x"][0, bass.ds(t * P, P), :], after=[V])
        for h in range(2):
            s = slice(512 * h, 512 * h + 512)
            v = V.tt(y[:, s], banks[h][:, :], xin[:, s], ALU.add, after=[m, x, A])
        rms_scale(k, st, y[:, :], P, 1e-6, dump[:, :], after=[V])
        V.stt(X[:, t, :], y[:, :], st[:, 1:2], g[:, :], ALU.mult, ALU.mult)
        return v

    out_project(k, ps, sb, mix, 12, io["w_out"][0], finish)


def mixer_out(k, ps, io, mix, blocks, w, layer, X, sb):
    V, A, G = k.V, k.A, k.G
    y = sb("y_tile", [P, D], F32)
    dump = sb("squares", [P, D], F32)
    g, b = sb("ln_g", [P, D], F32), sb("ln_b", [P, D], F32)
    st = sb("ln_stats", [P, 6], F32)
    row_in(k, "ln_in", g, io["ln_mix_g_2"][layer])
    m = row_in(k, "ln_in", b, io["ln_mix_b_2"][layer])
    V.after(m)
    G.after(m)

    def finish(t, banks, m):
        for h in range(2):
            s = slice(512 * h, 512 * h + 512)
            V.start([m, A, G])
            V.done(V.eng.scalar_tensor_tensor(y[:, s], X[:, t, :][:, s], ALPHA, banks[h][:, :], ALU.mult, ALU.add,
                                              accum_out=st[:, 3 + h:4 + h]))
        v = V.tt(st[:, 5:6], st[:, 3:4], st[:, 4:5], ALU.add)
        both(layer_norm_tile(k, st, y[:, :], st[:, 5:6], g[:, :], b[:, :], X[:, t, :], dump[:, :]))
        return v

    out_project(k, ps, sb, mix, blocks, w, finish)


def transpose_x(k, c, ps, X, xT):
    V, A, T = k.V, k.A, k.T
    free = [None] * 8
    for i in range(2 * NT):
        t, h, bank = i // 2, i % 2, ps[i % 8]
        T.after(free[i % 8])
        for b in range(4):
            m = T.turn(bank[:, b * P:b * P + P], X[:, t, (4 * h + b) * P:(4 * h + b + 1) * P], c["ident"][:, :])
        free[i % 8] = (V if h else A).copy(xT[:, 4 * h:4 * h + 4, t * P:(t + 1) * P],
                                           bank[:, :].rearrange("p (b t) -> p b t", b=4), after=[m])
    T.after(V, A)


def windowed_attention(k, c, ps, io, X, mix, sb):
    V, A, T, G = k.V, k.A, k.T, k.G
    HQ, HK, HD = 16, 4, 64
    BAND = 3 * P
    spans = [(0, 512), (512, 512)]
    xT = sb("xT", [P, KD, SEQ], F32)
    transpose_x(k, c, ps, X, xT)
    pr = Projector(k, ps, io["attn_w_qkv_2"], xT, sb, 3)
    cos, sin = sb("cos", [P, SEQ], F32), sb("sin", [P, SEQ], F32)
    rot = sb("rotate", [P, P], F32)
    wv = sb("wv", [P, KD, HK * HD], F32)
    qT = sb("aq", [P, 2, SEQ], F32)
    kT = sb("ak", [P, SEQ + 2 * P], F32)
    vt = sb("av", [P, NT + 2, HK * HD], F32)
    raw, tmp = sb("a_raw", [P, SEQ], F32), sb("a_tmp", [P, SEQ], F32)
    oT = sb("ao", [P, 2, SEQ], F32)
    mask = sb("a_mask", [P, 3, BAND], F32)
    sink = sb("a_sink", [P, HQ], F32)
    vg = sb("a_vg", [P, NT + 2, HD], F32)
    lanes = [[sb(f"a_{n}{u}", shape, F32) for n, shape in (
        ("s", [P, 2, BAND]), ("pT", [P, 2, BAND]), ("st", [P, 5, 2]))]
        for u in range(4)]
    for e in range(3):
        G.fill(mask[:, e, :], 0.0)
        rules = [(0, 1, -1), (2 * P, -1, 1)]
        if e != 1:
            rules.append((-P, 1, 0) if e == 0 else (2 * P - 1, -1, 0))
        for base, col, part in rules:
            G.start(())
            G.done(G.eng.affine_select(out=mask[:, e, :], in_=mask[:, e, :], compare_op=ALU.is_ge, fill=NEG, base=base,
                                       pattern=[[col, BAND]], channel_multiplier=part))
    for e in (0, SEQ + P):
        G.fill(kT[:, e:e + P], 0.0)
    for e in (0, NT + 1):
        G.fill(vt[:, e, :], 0.0)
    k.dma("a_small_in", cos[:, :], io["rope_cos"])
    k.dma("a_small_in", sin[:, :], io["rope_sin"])
    k.dma("a_small_in", rot[:, :], io["rope_turn"])
    row_in(k, "a_small_in", sink, io["attn_sink_2"][0])
    w3 = io["attn_w_qkv_2"][0].rearrange("(k p) c -> p k c", p=P)
    m = k.dma("a_wv_in", wv[:, :, :], w3[:, :, (HQ + HK) * HD:])
    T.after(m)
    for t in range(NT):
        bank = ps[6 + t % 2]
        T.after(A)
        for d in range(KD):
            m = T.mm(bank[:, 0:HK * HD], xT[:, d, t * P:(t + 1) * P], wv[:, d, :], start=d == 0, stop=d == KD - 1)
        A.copy(vt[:, t + 1, :], bank[:, 0:HK * HD], after=[m])

    def rotary(out):
        def take(j, col, n, z, m):
            s = slice(col, col + n)
            a = A.copy(raw[:, s], z, after=[m, V, T])
            t = T.mm(ps[6 + j][:, 0:n], rot[:, :], raw[:, s], after=[a, V])
            V.tt(tmp[:, s], ps[6 + j][:, 0:n], sin[:, s], ALU.mult, after=[t])
            g = G.tt(out[:, s], raw[:, s], cos[:, s], ALU.mult, after=[a, V])
            return [V.tt(out[:, s], out[:, s], tmp[:, s], ALU.add, after=[g])]
        pr.block(take, spans)

    free = [None] * 4

    def pair(lane, qb, g, x):
        s_sb, pT, st = lanes[lane]
        K = ps[2 * lane:2 * lane + 2]
        scale = HD ** -0.5
        e = {0: 0, NT - 1: 2}.get(qb, 1)
        T.after(free[lane])
        for h, half in enumerate(HALF):
            m = T.mm(K[h][:, 0:BAND], qT[half, x, qb * P:(qb + 1) * P], kT[half, qb * P:qb * P + BAND])
        yield
        for h in range(2):
            V.stt(s_sb[:, h, :], K[h][:, 0:BAND], scale, mask[:, e, :], ALU.mult, ALU.add, after=[m])
        V.reduce(st[:, 0, :], s_sb[:, :, :], ALU.max)
        sk = sink[:, bass.ds(g * 4 + 2 * x, 2)]
        V.tt(st[:, 0, :], st[:, 0, :], sk, ALU.max)
        V.ts(st[:, 1, :], st[:, 0, :], -1.0, ALU.mult)
        v = V.tt(st[:, 2, :], sk, st[:, 0, :], ALU.subtract)
        yield
        for h in range(2):
            A.act(s_sb[:, h, :], s_sb[:, h, :], ACT.Exp, bias=st[:, 1, h:h + 1], accum=st[:, 3, h:h + 1], after=[v])
        a = A.act(st[:, 2, :], st[:, 2, :], ACT.Exp)
        yield
        V.tt(st[:, 3, :], st[:, 3, :], st[:, 2, :], ALU.add, after=[a])
        V.recip(st[:, 4, :], st[:, 3, :])
        for h in range(2):
            v = V.ts(s_sb[:, h, :], s_sb[:, h, :], st[:, 4, h:h + 1], ALU.mult)
        yield
        T.after(v)
        turned = [[T.turn(K[h][:, j * P:(j + 1) * P], s_sb[:, h, j * P:(j + 1) * P], c["ident"][:, :])
                   for j in range(3)][-1] for h in range(2)]
        yield
        for h in range(2):
            a = A.copy(pT[:, h, :], K[h][:, 0:BAND], after=[turned[h]])
        yield
        T.after(a)
        for h, half in enumerate(HALF):
            for j in range(3):
                m = T.mm(K[0][half, BAND:], vg[:, qb + j, :], pT[:, h, j * P:(j + 1) * P], start=j == 0, stop=j == 2)
        yield
        free[lane] = A.copy(oT[:, x, qb * P:(qb + 1) * P], K[0][:, BAND:], after=[m])
        yield

    with k.loop(HK) as g:
        pr.reset()
        for half in HALF:
            pr.part(half, bass.ds(g * HD + HQ * HD, HD))
        pr.whole()
        pr.load(bass.ds(g * 2 * P, P))
        pr.load(bass.ds(g * 2 * P + P, P))
        rotary(kT[:, P:P + SEQ])
        for x in range(2):
            rotary(qT[:, x, :])
        G.copy(vg[:, :, :], vt[:, :, bass.ds(g * HD, HD)])
        T.after(V, G)

        def lane(u, x):
            for _ in range(2 * u + x):
                yield
            for qb in range(u * NT // 2, (u + 1) * NT // 2):
                yield from pair(2 * u + x, qb, g, x)

        T.after(A)
        both(*[lane(u, x) for u in range(2) for x in range(2)])
        k.dma("mix_out", mix[bass.ds(2 * g, 2), :, :].rearrange("x p t -> p x t"), oT[:, :, :], after=[A])


def lru(k, c, ps, io, X, mix, sb):
    V, A, T, G = k.V, k.A, k.T, k.G
    BLK = 256
    spans = [(0, 512), (512, 512)]
    xT = sb("xT", [P, KD, SEQ], F32)
    transpose_x(k, c, ps, X, xT)
    pr = Projector(k, ps, io["lru_w_in_2"], xT, sb, 4)
    gate = sb("l_gate", [P, 2, SEQ], F32)
    raw = sb("l_raw", [P, SEQ + 3], F32)
    xc = sb("l_xc", [P, 2, SEQ], F32)
    work = [[sb(f"l_{n}{lane}", [P, SEQ], F32) for n in ("r", "i", "a", "u", "h")] for lane in range(4)]
    wg = sb("l_wg", [P, 2, 2, 2, BLK], F32)
    cw, cb = sb("l_cw", [P, 4, 8], F32), sb("l_cb", [P, 8], F32)
    bg = sb("l_bg", [P, 2, 2, 8], F32)
    lam = sb("l_lam", [P, 2, 8], F32)
    sm = [sb(f"l_sm{i}", [P, 2, 8], F32) for i in range(4)]
    for t, n in ((cw[:, :, :].rearrange("p a b -> p (a b)"), "lru_conv_w_2"), (cb[:, :], "lru_conv_b_2"),
                 (bg[:, 0].rearrange("p a b -> p (a b)"), "lru_b_rgate_2"),
                 (bg[:, 1].rearrange("p a b -> p (a b)"), "lru_b_igate_2"),
                 (lam[:, :, :].rearrange("p a b -> p (a b)"), "lru_lambda_2")):
        m = k.dma("l_small_in", t, io[n + "_cols"])
    G.fill(raw[:, :], 0.0)
    e, s, s2, acc = (x[:, :, :] for x in sm)
    L = lam[:, :, :]
    V.stt(e, L, -1.0, L, ALU.mult, ALU.min, after=[m])
    a = A.act(e, e, ACT.Exp, after=[V])
    V.ts(s, e, 2.0, ALU.add, after=[a])
    V.recip(s, s)
    V.tt(s, s, e, ALU.mult)
    V.tt(s2, s, s, ALU.mult)
    V.ts(acc, s2, 1.0 / 19, ALU.mult)
    for n in (17, 15, 13, 11, 9, 7, 5, 3):
        V.stt(acc, acc, 1.0 / n, s2, ALU.add, ALU.mult)
    V.stt(acc, acc, 1.0, s, ALU.add, ALU.mult)
    V.ts(L, L, -1.0, ALU.mult, 0.0, ALU.max)
    V.stt(L, acc, 2.0, L, ALU.mult, ALU.add)
    V.ts(L, L, -8.0, ALU.mult)
    A.after(V)

    with k.loop(4) as n:
        pr.reset()
        for x in range(2):
            pr.load(bass.ds(n * BLK + D + x * P, P))
        for x in range(2):
            pr.load(bass.ds(n * BLK + x * P, P))
        for q, name in enumerate(("lru_w_rgate_2", "lru_w_igate_2")):
            for z in range(2):
                wm = k.dma("l_wg_in", wg[:, q, z], one(io[name][0, z], n).rearrange("(c p) f -> p c f", p=P))
        for x in range(2):
            def take(j, col, m_, z, m):
                return [A.copy(raw[:, 2 + col:2 + col + m_], z, after=[m, V, G])]
            pr.block(take, spans)
            col = lambda t: t[:, bass.ds(2 * n + x, 1)]
            V.ts(xc[:, x, :], raw[:, 0:SEQ], cw[:, 0, bass.ds(2 * n + x, 1)], ALU.mult, col(cb), ALU.add, after=[A, G])
            for j in range(1, 4):
                V.stt(xc[:, x, :], raw[:, j:j + SEQ], cw[:, j, bass.ds(2 * n + x, 1)], xc[:, x, :], ALU.mult, ALU.add)
        def gates(x, z):
            free = [None] * 2
            for q in range(2):
                for j, (col, m_) in enumerate(spans):
                    bank = ps[2 * (2 * x + z) + j]
                    T.after(wm, V, free[j])
                    for h in range(2):
                        m = T.mm(bank[:, :], wg[:, q, z, h, x * P:(x + 1) * P], xc[:, h, col:col + m_], start=h == 0,
                                 stop=h == 1)
                    free[j] = A.act(work[2 * x + z][q][:, col:col + m_], bank[:, :], ACT.Sigmoid,
                                    bias=bg[:, q, z, bass.ds(2 * n + x, 1)], after=[m])
                yield
            T.after(*free)

        def recurrence(x, z):
            rr, ii, a_, u, h = work[2 * x + z]
            V.ts(rr[:, :], rr[:, :], lam[:, z, bass.ds(2 * n + x, 1)], ALU.mult, after=[gated])
            v = V.tt(ii[:, :], ii[:, :], xc[:, x, :], ALU.mult)
            a = A.act(a_[:, :], rr[:, :], ACT.Exp, after=[v])
            yield
            A.act(u[:, :], a_[:, :], ACT.Square)
            a = A.act(rr[:, :], rr[:, :], ACT.Tanh)
            v = V.stt(u[:, :], u[:, :], 1.0, rr[:, :], ALU.add, ALU.mult, after=[a])
            yield
            a = A.act(u[:, :], u[:, :], ACT.Sqrt, scale=-1.0, after=[v])
            start = 0 if z == 0 else SEQ - 1
            V.fill(u[:, start:start + 1], 1.0, after=[a])
            V.tt(u[:, :], u[:, :], ii[:, :], ALU.mult)
            back = slice(0, SEQ) if z == 0 else slice(SEQ - 1, None, -1)
            V.scan(h[:, back], a_[:, back], u[:, back])
            yield

        lanes = [(x, z) for x in range(2) for z in range(2)]
        both(*[gates(x, z) for x, z in lanes])
        gated = A.mark()
        products = [pr.multiply(spans) for x in range(2)]
        both(*[recurrence(x, z) for x, z in lanes])
        for x in range(2):
            def take(j, col, m_, z, m):
                s, tmp = slice(col, col + m_), work[2 * x][3]
                a = A.act(tmp[:, s], z, ACT.Square, after=[m, V])
                V.ts(tmp[:, s], tmp[:, s], 0.044715, ALU.mult, 1.0, ALU.add, after=[a])
                v = V.tt(tmp[:, s], tmp[:, s], z, ALU.mult)
                a = A.act(tmp[:, s], tmp[:, s], ACT.Sigmoid, scale=2 * (2 / np.pi) ** 0.5, after=[v])
                return [V.tt(gate[:, x, s], z, tmp[:, s], ALU.mult, after=[a])]
            pr.evacuate(products[x], take)
            g = G.tt(work[2 * x][4][:, :], work[2 * x][4][:, :], work[2 * x + 1][4][:, :], ALU.add, after=[V])
            V.tt(gate[:, x, :], gate[:, x, :], work[2 * x][4][:, :], ALU.mult, after=[g])
        k.dma("mix_out", mix[bass.ds(2 * n, 2), :, :].rearrange("x p t -> p x t"), gate[:, :, :], after=[V])


NE, FF, CAP = 16, 1024, 128
HALF_FF = FF // 2
SLABS = 24
AHEAD = 5


def slab(io, layer, e, i):
    if i < 16:
        h, d = i // 8, i % 8
        w = one(io["moe_w_gate_up_2"][layer], e)[d * P:(d + 1) * P, :]
        return w.rearrange("p (x c) -> p x c", x=2)[:, :, h * HALF_FF:(h + 1) * HALF_FF]
    w = one(io["moe_w_down_2"][layer], e)[(i - 16) * P:(i - 15) * P, :]
    return w.rearrange("p (x c) -> p x c", x=2)


def moe(k, c, ps, io, layer, X, rows, out, sb):
    nc, V, A, T, G = k.nc, k.V, k.A, k.T, k.G
    x_rows, y_rows = rows
    ring = sb("ring", [P, SLABS, 2, HALF_FF], F32)
    spare = [sb(f"m_spare{i}", [P, KD, P], F32) for i in range(4)]
    xg = sb("m_picked", [P, D], F32)
    xs, hs = sb("m_picked_T", [P, D], F32), sb("m_hidden_T", [P, FF], F32)
    hid, ys = sb("m_hidden", [P, FF], F32), sb("m_ys", [P, D], F32)
    wr = sb("m_router", [P, KD, NE], F32)
    affT = sb("m_aff", [NE, SEQ], F32)
    top, at = sb("m_top", [NE, CAP], F32), sb("m_top_at", [NE, CAP], U32)
    atf = sb("m_top_at_float", [NE, CAP], F32)
    gates, tokens = sb("m_gates", [P, NE], F32), sb("m_tokens", [P, NE], I32)
    pick = [sb(f"m_pick{i}", [P, 1], I32) for i in range(AHEAD)]
    st = [sb(f"m_st{i}", [P, 6], F32) for i in range(4)]
    aff = [sb(f"m_aff_tile{i}", [P, NE], F32) for i in range(4)]
    unused = sb("m_unused", [P, 1], F32)
    landed = k.landed

    def load(e, i, after=()):
        k.S.after(*after)
        nc.sync.dma_start(ring[:, i, :, :], slab(io, layer, e, i)).then_inc(landed[i], 16)

    def arrived(i):
        nc.tensor.wait_ge(landed[i], 16)
        nc.tensor.sem_clear(landed[i])

    router_in = k.dma("router_in", wr[:, :, :], io["moe_w_router_2"][layer].rearrange("(k p) e -> p k e", p=P))
    for i in range(SLABS):
        load(0, i)

    for dst in rows:
        x_stored = k.dma("x_rows_out", dst.rearrange("(t p) d -> p t d", p=P), X[:, :, :], line=A)

    def route(t, u):
        K = ps[2 * u:2 * u + 2]
        for b in range(KD):
            m = T.turn(K[b // 4][:, (b % 4) * P:(b % 4) * P + P], X[:, t, b * P:(b + 1) * P], c["ident"][:, :])
        for h in range(2):
            m1 = (V if h else A).copy(spare[u][:, 4 * h:4 * h + 4, :], K[h][:, :].rearrange("p (b t) -> p b t", b=4),
                                      after=[m])
            T.after(m1)
        yield
        T.after(router_in)
        for d in range(KD):
            m = T.mm(K[0][:, 0:NE], spare[u][:, d, :], wr[:, d, :], start=d == 0, stop=d == KD - 1)
        V.reduce(st[u][:, 0:1], K[0][:, 0:NE], ALU.max, after=[m])
        v = V.ts(st[u][:, 1:2], st[u][:, 0:1], -1.0, ALU.mult)
        a = A.act(aff[u][:, :], K[0][:, 0:NE], ACT.Exp, bias=st[u][:, 1:2], accum=st[u][:, 2:3], after=[v])
        yield
        V.recip(st[u][:, 3:4], st[u][:, 2:3], after=[a])
        v = V.ts(aff[u][:, :], aff[u][:, :], st[u][:, 3:4], ALU.mult)
        m = T.turn(K[1][0:NE, 0:P], aff[u][:, :], c["ident"][:, :], after=[v])
        v = V.copy(affT[:, t * P:(t + 1) * P], K[1][0:NE, 0:P], after=[m])
        T.after(v)
        yield

    in_lanes(route)

    for i in range(0, CAP, 8):
        s = slice(i, i + 8)
        for ins in (lambda: V.eng.max(top[:, s], affT[:, :]),
                    lambda: V.eng.max_index(at[:, s], top[:, s], affT[:, :]),
                    lambda: V.eng.match_replace(affT[:, :], top[:, s], affT[:, :], -1.0)):
            V.start(())
            V.done(ins())
    v = V.copy(atf[:, :], at[:, :])
    T.after(v)
    T.turn(ps[4][:, 0:NE], atf[:, :], c["ident"][0:NE, 0:NE])
    m = T.turn(ps[4][:, NE:2 * NE], top[:, :], c["ident"][0:NE, 0:NE])
    V.copy(tokens[:, :], ps[4][:, 0:NE], after=[m])
    v = V.copy(gates[:, :], ps[4][:, NE:2 * NE])

    gathered, scattered = (Count(k, f"{name}{layer}", steady=True) for name in ("gathered", "scattered"))
    by = lambda count, e: (count, 16 * (e + 1), None)

    def gather(e, u, after=()):
        G.copy(pick[u][:, :], tokens[:, bass.ds(e, 1)], after=after)
        G.start(())
        G.eng.indirect_dma_start(xg[:, :], None, x_rows[:, :],
                                 bass.IndirectOffsetOnAxis(ap=pick[u][:, 0:1], axis=0)).then_inc(gathered.sem, 16)

    def scatter(e, u, after=()):
        G.start(after)
        G.eng.indirect_dma_start(y_rows[:, :], bass.IndirectOffsetOnAxis(ap=pick[u][:, 0:1], axis=0), ys[:, :], None,
                                 compute_op=ALU.add).then_inc(scattered.sem, 16)

    def turn_tokens(got):
        for b in range(KD):
            m = T.turn(ps[4 + b // 4][:, (b % 4) * P:(b % 4) * P + P], xg[:, b * P:(b + 1) * P], c["ident"][:, :],
                       after=[got])
        return [(V if h else A).copy(xs[:, 512 * h:512 * h + 512], ps[4 + h][:, :], after=[m]) for h in range(2)]

    def experts(first, n, more):
        ready = None
        for x in range(n):
            e = first + x
            if ready is None:
                ready = turn_tokens(by(gathered, e))
            T.after(*ready)
            nxt = more or x < n - 1
            before = [by(scattered, e - 1)] if x else []
            if nxt:
                gather(e + 1, (x + 1) % AHEAD, after=[T, *ready, *before])
            def rows(i, lhsT, banks):
                arrived(i)
                for j in range(2):
                    m = T.mm(banks[j][:, :], lhsT[:, (i % 8) * P:(i % 8 + 1) * P], ring[:, i, j, :], start=i % 8 == 0,
                             stop=i % 8 == KD - 1)
                if nxt:
                    load(e + 1, i, after=[m])
                return m

            def act(h, m):
                s = slice(HALF_FF * h, HALF_FF * h + HALF_FF)
                a = A.act(hid[:, s], ps[2 * h][:, :], ACT.Sigmoid, after=[m])
                V.tt(hid[:, s], hid[:, s], ps[2 * h][:, :], ALU.mult, after=[a])
                return V.tt(hid[:, s], hid[:, s], ps[2 * h + 1][:, :], ALU.mult)

            def turn_hidden(h, acted):
                T.after(acted)
                for b in range(4 * h, 4 * h + 4):
                    m = T.turn(ps[4 + b // 2 % 2][:, (2 * h + b % 2) * P:(2 * h + b % 2) * P + P],
                               hid[:, b * P:(b + 1) * P], c["ident"][:, :])
                return [line.copy(hs[:, 512 * h + 256 * i:512 * h + 256 * i + 256],
                                  ps[4 + i][:, 256 * h:256 * h + 256], after=[m]) for i, line in enumerate((A, V))]

            for d in range(KD):
                m = rows(d, xs, ps[0:2])
            acted = act(0, m)
            for d in range(KD):
                if d == 5:
                    got_h = turn_hidden(0, acted)
                m = rows(8 + d, xs, ps[2:4])
            acted = act(1, m)
            T.after(*got_h)
            for d in range(KD):
                if d == 3:
                    got_h = turn_hidden(1, acted)
                if d == 4:
                    T.after(*got_h)
                if d == 6 and x < n - 1:
                    ready = turn_tokens(by(gathered, e + 1))
                m = rows(16 + d, hs, ps[6:8])
            a = A.act(ys[:, 0:512], ps[6][:, :], ACT.Copy, scale=gates[:, bass.ds(e, 1)], after=[m, *before])
            v = V.ts(ys[:, 512:], ps[7][:, :], gates[:, bass.ds(e, 1)], ALU.mult, after=[m, *before])
            scatter(e, x, after=[a, v, *before])
            T.after(a, v)
        G.after(by(scattered, first + n - 1))
        G.tt(unused[:, :], unused[:, :], unused[:, :], ALU.add)

    G.fill(unused[:, :], 0.0)
    gather(0, 0, after=[v, x_stored])
    turns = (NE - 1) // AHEAD
    with k.loop(turns) as i:
        experts(i * AHEAD, AHEAD, True)
    experts(NE - 1, 1, False)
    k.barrier()

    g, b = xs, hs
    k.dma("ffn_ln_in", g[:, :], io["ln_ffn_g_2"][layer].partition_broadcast(P))
    ln_in = k.dma("ffn_ln_in", b[:, :], io["ln_ffn_b_2"][layer].partition_broadcast(P))

    slabs = lambda i: ring[:, i, :, :].rearrange("p x c -> p (x c)")
    loads = [k.dma(f"y_rows_in{t}", slabs(t), y_rows[t * P:(t + 1) * P, :]) for t in range(NT)]
    for line in (V, G):
        line.after(ln_in)

    def norm(t, u):
        y = slabs(NT + t)
        V.start([loads[t]])
        V.done(V.eng.scalar_tensor_tensor(y, X[:, t, :], ALPHA - 1.0, slabs(t), ALU.mult, ALU.add,
                                          accum_out=st[u][:, 3:4]))
        yield
        yield from layer_norm_tile(k, st[u], y, st[u][:, 3:4], g[:, :], b[:, :], X[:, t, :], slabs(2 * NT + t))
        if out is not None:
            k.dma("final_out", out[0, t * P:(t + 1) * P, :], X[:, t, :], after=[G])
        yield

    in_lanes(norm)


_INS = ["x", "meta", "norm_g", "w_in", "w_out", "gla_g_up", "gla_g_b", "gla_norm_g", "rw_conv", "rw_w0", "rw_w_up",
        "rw_a0", "rw_a_up", "rw_k_k", "rw_k_a", "rw_r_k", "rw_ln_g", "rw_ln_b", "final_norm_g", "attn_w_qkv_2",
        "attn_w_o_2", "attn_sink_2", "lru_w_in_2", "lru_conv_w_2", "lru_conv_b_2", "lru_w_rgate_2", "lru_b_rgate_2",
        "lru_w_igate_2", "lru_b_igate_2", "lru_lambda_2", "lru_w_out_2", "moe_w_router_2", "moe_w_gate_up_2",
        "moe_w_down_2", "ln_mix_g_2", "ln_mix_b_2", "ln_ffn_g_2", "ln_ffn_b_2"]
_COLS = ["norm_g", "gla_g_b", "gla_norm_g", "rw_conv", "rw_w0", "rw_a0", "rw_k_k", "rw_k_a", "rw_r_k", "rw_ln_g",
         "rw_ln_b", "lru_conv_w_2", "lru_conv_b_2", "lru_b_rgate_2", "lru_b_igate_2", "lru_lambda_2"]


def phase(nc, k):
    @contextmanager
    def held():
        with ExitStack() as ctx:
            k.phases += 1
            yield lambda name, shape, dt, n=k.phases: ctx.enter_context(nc.sbuf_tensor(f"{name}_{n}", shape, dt))
            k.barrier()
    return held()


def program(nc, io, out, mix, rows):
    with ExitStack() as ctx:
        k = Core(nc, ctx)
        ps = [ctx.enter_context(nc.psum_tensor(f"bank{i}", [P, 512], F32)) for i in range(8)]
        c = constants(k, lambda name, shape, dt: ctx.enter_context(nc.sbuf_tensor(name, shape, dt)))
        with phase(nc, k) as own:
            hnT = own("hnT", [P, KD, COLS], F32)
            for stage in (
                lambda sb: block_one_norm(k, c, ps, io, hnT, sb),
                lambda sb: attention_branch(k, c, ps, io, hnT, mix, sb),
                lambda sb: gla_branch(k, c, ps, io, hnT, mix, sb),
                lambda sb: rwkv_branch(k, c, ps, io, hnT, mix, sb),
            ):
                with phase(nc, k) as sb:
                    stage(sb)
        with phase(nc, k) as own:
            X = own("X", [P, NT, D], F32)
            for stage in (
                lambda sb: block_one_out(k, ps, io, mix, X, sb),
                lambda sb: windowed_attention(k, c, ps, io, X, mix, sb),
                lambda sb: mixer_out(k, ps, io, mix, 8, io["attn_w_o_2"][0], 0, X, sb),
                lambda sb: moe(k, c, ps, io, 0, X, rows, None, sb),
                lambda sb: lru(k, c, ps, io, X, mix, sb),
                lambda sb: mixer_out(k, ps, io, mix, 8, io["lru_w_out_2"][0], 1, X, sb),
                lambda sb: moe(k, c, ps, io, 1, X, rows, out, sb),
            ):
                with phase(nc, k) as sb:
                    stage(sb)


def rope_tables():
    rot = 16
    angle = np.arange(SEQ, dtype=np.float32) * (
        np.float32(500000.0) ** (-np.arange(0, rot, 2, dtype=np.float32) / rot))[:, None]
    cos, sin, turn = np.ones((P, SEQ), np.float32), np.zeros((P, SEQ), np.float32), np.zeros((P, P), np.float32)
    for h in (0, 64):
        for i in range(rot // 2):
            for at in (h + i, h + i + rot // 2):
                cos[at], sin[at] = np.cos(angle[i]), np.sin(angle[i])
            turn[h + i + rot // 2, h + i] = -1.0
            turn[h + i, h + i + rot // 2] = 1.0
    return {"rope_cos": cos, "rope_sin": sin, "rope_turn": turn}


def layouts(inputs):
    arrays = {name: np.ascontiguousarray(inputs[name]) for name in _INS}
    arrays.update(rope_tables())
    for name in _COLS:
        a = np.asarray(inputs[name])
        a = a.reshape(-1, a.shape[-1] // P, P)
        arrays[name + "_cols"] = np.ascontiguousarray(a.transpose(2, 0, 1).reshape(P, -1))
    arrays["rpb_padded"] = np.pad(np.ascontiguousarray(inputs["na_rpb"]).reshape(-1), RPB_PAD)
    return arrays


def kernel(**inputs):
    import concourse.bacc as _bacc
    from concourse.bass_utils import run_bass_kernel_spmd as _run

    nc = _bacc.Bacc("TRN2", target_bir_lowering=False, num_devices=1)
    arrays = layouts(inputs)
    io = {name: nc.dram_tensor(f"in_{name}", a.shape, mybir.dt.from_np(a.dtype), kind="ExternalInput").ap()
          for name, a in arrays.items()}
    out = nc.dram_tensor("out", (1, SEQ, D), F32, kind="ExternalOutput").ap()
    mix = nc.dram_tensor("mix", (12, P, SEQ), F32, kind="Internal").ap()
    rows = [nc.dram_tensor(name, (SEQ, D), F32, kind="Internal").ap() for name in ("x_rows", "y_rows")]
    program(nc, io, out, mix, rows)
    return _run(nc, [{f"in_{name}": a for name, a in arrays.items()}], core_ids=[0]).results[0]["out"]
```
